# Optimizing a Trainium2 kernel written in Bass

```python
import jax, jax.numpy as jnp
from jax import lax
import numpy as np

D_MODEL = 1024
BATCH = 1
SEQ = 256
DEPTH = 2

GRID_W = 64
CTX_LEN = 256
N_Q_HEADS = 8
N_KV_HEADS = 2
HEAD_DIM = 64
ATTN_WIDTH = N_Q_HEADS * HEAD_DIM
KV_WIDTH = N_KV_HEADS * HEAD_DIM
Q_BLOCK = 128
ROPE_THETA = 10000.0
POOL_WINDOWS = (2, 4, 8, 16)
N_POOL_GROUPS = 4
POOL_GROUP_DIM = 128
POOL_WIDTH = N_POOL_GROUPS * POOL_GROUP_DIM
MIX_IN_WIDTH = ATTN_WIDTH + 2 * KV_WIDTH + POOL_WIDTH
MIX_OUT_WIDTH = ATTN_WIDTH + POOL_WIDTH
CONV_WIDTH = D_MODEL
CONV_K = 3
N_EXPERTS = 16
EXPERT_FF = 1024
CAPACITY_FACTOR = 2
NORM_EPS = 1e-6
DEEPNORM_ALPHA = (2 * DEPTH) ** 0.25
DEEPNORM_BETA = (8 * DEPTH) ** -0.25


def _layer_norm(x, g, b):
    xf = x.astype(jnp.float32)
    mu = jnp.mean(xf, axis=-1, keepdims=True)
    xc = xf - mu
    var = jnp.mean(xc * xc, axis=-1, keepdims=True)
    y = xc * lax.rsqrt(var + NORM_EPS) * g.astype(jnp.float32) + b.astype(jnp.float32)
    return y.astype(x.dtype)

def _rms_norm(x, g):
    xf = x.astype(jnp.float32)
    y = xf * lax.rsqrt(jnp.mean(xf * xf, axis=-1, keepdims=True) + NORM_EPS)
    return (y * g.astype(jnp.float32)).astype(x.dtype)

def _modulation(cond, w, b):
    m = (cond @ w + b)[:, None, :]
    return jnp.split(m, 6, axis=-1)

def _modulate(h, shift, scale):
    return h * (1.0 + scale) + shift

def _post_norm(h, branch, g, b):
    return _layer_norm(DEEPNORM_ALPHA * h + branch, g, b)

def _axial_rope_tables(rows):
    row = jnp.broadcast_to(jnp.arange(rows, dtype=jnp.float32)[:, None], (rows, GRID_W)).reshape(-1)
    col = jnp.broadcast_to(jnp.arange(GRID_W, dtype=jnp.float32)[None, :], (rows, GRID_W)).reshape(-1)
    axis_dim = HEAD_DIM // 2
    inv_freq = ROPE_THETA ** (-jnp.arange(0, axis_dim, 2, dtype=jnp.float32) / axis_dim)
    ang = jnp.concatenate([row[:, None] * inv_freq, col[:, None] * inv_freq], axis=-1)
    return jnp.cos(ang), jnp.sin(ang)

def _apply_rope(x, cos, sin):
    xf = x.astype(jnp.float32).reshape(x.shape[:-1] + (HEAD_DIM // 2, 2))
    x0, x1 = xf[..., 0], xf[..., 1]
    c = cos[None, :, None, :]
    s = sin[None, :, None, :]
    out = jnp.stack([x0 * c - x1 * s, x0 * s + x1 * c], axis=-1).reshape(x.shape)
    return out.astype(x.dtype)

def _blocked_attention(q, k, v):
    b, lq = q.shape[:2]
    grp = N_Q_HEADS // N_KV_HEADS
    nb = lq // Q_BLOCK
    qb = q.reshape(b, nb, Q_BLOCK, N_KV_HEADS, grp, HEAD_DIM).transpose(1, 0, 2, 3, 4, 5)
    scale = HEAD_DIM ** -0.5

    def one_block(qi):
        s = jnp.einsum('bqhgd,bkhd->bhgqk', qi, k, preferred_element_type=jnp.float32) * scale
        p = jax.nn.softmax(s, axis=-1)
        return jnp.einsum('bhgqk,bkhd->bqhgd', p.astype(v.dtype), v)

    o = lax.map(one_block, qb)
    return o.transpose(1, 0, 2, 3, 4, 5).reshape(b, lq, ATTN_WIDTH)

def _pool_branch(p, w_grp, p_scale):
    b, l, _ = p.shape
    pf = p.astype(jnp.float32)
    cs = jnp.concatenate([jnp.zeros((b, 1, POOL_WIDTH), jnp.float32), jnp.cumsum(pf, axis=1)], axis=1)
    t = jnp.arange(l)
    means = []
    for g, w in enumerate(POOL_WINDOWS):
        lo = jnp.maximum(t - w // 2, 0)
        hi = jnp.minimum(t + w // 2, l)
        seg = cs[:, :, g * POOL_GROUP_DIM:(g + 1) * POOL_GROUP_DIM]
        cnt = (hi - lo).astype(jnp.float32)[None, :, None]
        means.append((seg[:, hi] - seg[:, lo]) / cnt)
    pooled = (jnp.concatenate(means, axis=-1) - pf).astype(p.dtype)
    pooled = pooled.reshape(b, l, N_POOL_GROUPS, POOL_GROUP_DIM)
    out = jnp.einsum('blgc,gcd->blgd', pooled, w_grp).reshape(b, l, POOL_WIDTH)
    return out * p_scale

def _split_mix_in(h):
    return jnp.split(h, [ATTN_WIDTH, ATTN_WIDTH + KV_WIDTH, ATTN_WIDTH + 2 * KV_WIDTH], axis=-1)

def _attn_pool_mixer(u_lat, u_ctx, cos, sin, w_in, q_g, k_g, w_grp, p_scale, w_out, ctx_out):
    b, s, _ = u_lat.shape
    lc = u_ctx.shape[1]
    q, k, v, p = _split_mix_in(u_lat @ w_in)
    q = _apply_rope(_rms_norm(q.reshape(b, s, N_Q_HEADS, HEAD_DIM), q_g), cos, sin)
    k = _apply_rope(_rms_norm(k.reshape(b, s, N_KV_HEADS, HEAD_DIM), k_g), cos, sin)
    v = v.reshape(b, s, N_KV_HEADS, HEAD_DIM)
    if ctx_out:
        qc, kc, vc, pc = _split_mix_in(u_ctx @ w_in)
    else:
        kc, vc = jnp.split(u_ctx @ w_in[:, ATTN_WIDTH:ATTN_WIDTH + 2 * KV_WIDTH], 2, axis=-1)
    kc = _rms_norm(kc.reshape(b, lc, N_KV_HEADS, HEAD_DIM), k_g)
    vc = vc.reshape(b, lc, N_KV_HEADS, HEAD_DIM)
    k_all = jnp.concatenate([kc, k], axis=1)
    v_all = jnp.concatenate([vc, v], axis=1)
    a_lat = _blocked_attention(q, k_all, v_all)
    y_lat = jnp.concatenate([a_lat, _pool_branch(p, w_grp, p_scale)], axis=-1) @ w_out
    y_ctx = None
    if ctx_out:
        qc = _rms_norm(qc.reshape(b, lc, N_Q_HEADS, HEAD_DIM), q_g)
        a_ctx = _blocked_attention(qc, kc, vc)
        y_ctx = jnp.concatenate([a_ctx, _pool_branch(pc, w_grp, p_scale)], axis=-1) @ w_out
    return y_lat, y_ctx

def _short_conv_mixer(u, w_in, conv_w, w_out):
    b_gate, c_gate, x_in = jnp.split(u @ w_in, 3, axis=-1)
    z = lax.conv_general_dilated(c_gate * x_in, conv_w[:, None, :], window_strides=(1,),
                                 padding=((CONV_K // 2, CONV_K // 2),),
                                 dimension_numbers=('NWC', 'WIO', 'NWC'),
                                 feature_group_count=CONV_WIDTH)
    return (b_gate * z) @ w_out

def _expert_choice_ffn(u, w_router, w_g, w_u, w_d):
    b, n, _ = u.shape
    cap = CAPACITY_FACTOR * n // N_EXPERTS
    logits = jnp.einsum('bnd,de->ben', u, w_router, preferred_element_type=jnp.float32)
    aff = jax.nn.softmax(logits, axis=1)
    gate, idx = lax.top_k(aff, cap)
    bidx = jnp.arange(b)[:, None, None]
    xe = u[bidx, idx]
    hg = jnp.einsum('becd,edf->becf', xe, w_g)
    hu = jnp.einsum('becd,edf->becf', xe, w_u)
    ye = jnp.einsum('becf,efd->becd', jax.nn.silu(hg) * hu, w_d) * gate[..., None].astype(u.dtype)
    return jnp.zeros_like(u).at[bidx, idx].add(ye)

def first_inputs(seed: int = 0) -> dict:
    key = jax.random.key(seed)
    ks = jax.random.split(key, 24)
    f32 = jnp.float32
    n_even = (DEPTH + 1) // 2
    n_odd = DEPTH // 2

    def dense(k, shape, fan_in, mult=1.0):
        return jax.random.normal(k, shape, f32) * (mult * fan_in ** -0.5)

    def gain(k, shape):
        return 1.0 + 0.02 * jax.random.normal(k, shape, f32)

    def small(k, shape):
        return 0.02 * jax.random.normal(k, shape, f32)

    return {
        'x': jax.random.normal(ks[0], (BATCH, SEQ, D_MODEL), f32),
        'c': jax.random.normal(ks[1], (BATCH, D_MODEL), f32),
        'ctx': jax.random.normal(ks[2], (BATCH, CTX_LEN, D_MODEL), f32),
        'c_ctx': jax.random.normal(ks[3], (D_MODEL,), f32),
        'w_mod': dense(ks[4], (DEPTH, D_MODEL, 6 * D_MODEL), D_MODEL, 0.5),
        'b_mod': 0.01 * jax.random.normal(ks[5], (DEPTH, 6 * D_MODEL), f32),
        'ln_mix_g': gain(ks[6], (DEPTH, D_MODEL)),
        'ln_mix_b': small(ks[7], (DEPTH, D_MODEL)),
        'ln_ffn_g': gain(ks[8], (DEPTH, D_MODEL)),
        'ln_ffn_b': small(ks[9], (DEPTH, D_MODEL)),
        'w_mix_in': dense(ks[10], (n_even, D_MODEL, MIX_IN_WIDTH), D_MODEL),
        'q_norm_g': gain(ks[11], (n_even, HEAD_DIM)),
        'k_norm_g': gain(ks[12], (n_even, HEAD_DIM)),
        'w_pool_grp': dense(ks[13], (n_even, N_POOL_GROUPS, POOL_GROUP_DIM, POOL_GROUP_DIM), POOL_GROUP_DIM),
        'pool_scale': gain(ks[14], (n_even, POOL_WIDTH)),
        'w_mix_out': dense(ks[15], (n_even, MIX_OUT_WIDTH, D_MODEL), MIX_OUT_WIDTH, DEEPNORM_BETA),
        'w_conv_in': dense(ks[16], (n_odd, D_MODEL, 3 * CONV_WIDTH), D_MODEL),
        'conv_w': dense(ks[17], (n_odd, CONV_K, CONV_WIDTH), CONV_K),
        'w_conv_out': dense(ks[18], (n_odd, CONV_WIDTH, D_MODEL), CONV_WIDTH, DEEPNORM_BETA),
        'w_router': dense(ks[19], (DEPTH, D_MODEL, N_EXPERTS), D_MODEL),
        'w_exp_gate': dense(ks[20], (DEPTH, N_EXPERTS, D_MODEL, EXPERT_FF), D_MODEL),
        'w_exp_up': dense(ks[21], (DEPTH, N_EXPERTS, D_MODEL, EXPERT_FF), D_MODEL),
        'w_exp_down': dense(ks[22], (DEPTH, N_EXPERTS, EXPERT_FF, D_MODEL), EXPERT_FF, DEEPNORM_BETA),
    }

def first_block(x, c, ctx, c_ctx, w_mod, b_mod, ln_mix_g, ln_mix_b, ln_ffn_g, ln_ffn_b,
              w_mix_in, q_norm_g, k_norm_g, w_pool_grp, pool_scale, w_mix_out,
              w_conv_in, conv_w, w_conv_out,
              w_router, w_exp_gate, w_exp_up, w_exp_down):
    rows = x.shape[1] // GRID_W
    cos, sin = _axial_rope_tables(rows)
    cond_lat = jax.nn.silu(c)
    cond_ctx = jax.nn.silu(c_ctx)[None, :]
    h_lat, h_ctx = x, ctx
    for layer in range(DEPTH):
        is_even = layer % 2 == 0
        ctx_out = any(j % 2 == 0 for j in range(layer + 1, DEPTH))
        ctx_in = is_even or ctx_out
        m_lat = _modulation(cond_lat, w_mod[layer], b_mod[layer])
        u_lat = _modulate(h_lat, m_lat[0], m_lat[1])
        u_ctx = None
        if ctx_in:
            m_ctx = _modulation(cond_ctx, w_mod[layer], b_mod[layer])
            u_ctx = _modulate(h_ctx, m_ctx[0], m_ctx[1])
        if is_even:
            e = layer // 2
            y_lat, y_ctx = _attn_pool_mixer(u_lat, u_ctx, cos, sin, w_mix_in[e], q_norm_g[e], k_norm_g[e],
                                            w_pool_grp[e], pool_scale[e], w_mix_out[e], ctx_out)
        else:
            o = layer // 2
            y_lat = _short_conv_mixer(u_lat, w_conv_in[o], conv_w[o], w_conv_out[o])
            y_ctx = _short_conv_mixer(u_ctx, w_conv_in[o], conv_w[o], w_conv_out[o]) if ctx_out else None
        h_lat = _post_norm(h_lat, m_lat[2] * y_lat, ln_mix_g[layer], ln_mix_b[layer])
        f_lat = _expert_choice_ffn(_modulate(h_lat, m_lat[3], m_lat[4]), w_router[layer],
                                   w_exp_gate[layer], w_exp_up[layer], w_exp_down[layer])
        h_lat = _post_norm(h_lat, m_lat[5] * f_lat, ln_ffn_g[layer], ln_ffn_b[layer])
        if ctx_out:
            h_ctx = _post_norm(h_ctx, m_ctx[2] * y_ctx, ln_mix_g[layer], ln_mix_b[layer])
            f_ctx = _expert_choice_ffn(_modulate(h_ctx, m_ctx[3], m_ctx[4]), w_router[layer],
                                       w_exp_gate[layer], w_exp_up[layer], w_exp_down[layer])
            h_ctx = _post_norm(h_ctx, m_ctx[5] * f_ctx, ln_ffn_g[layer], ln_ffn_b[layer])
    return h_lat


H_A = 8
NOPE = 64
ROPE_D = 32
V_A = 64
Q_LORA = 256
KV_LORA = 128
W_A = H_A * V_A
H_B = 8
HD_B = 64
W_B = H_B * HD_B
H_C = 8
HD_C = 64
W_C = H_C * HD_C
DECAY_LORA = 64
AAA_LORA = 64
MV_LORA = 32
SHIFT_COLS = 3 * W_C + DECAY_LORA + AAA_LORA
RWKV_DECAY_SCALE = 0.606531
GN_EPS = 64e-5
EPS = 1e-6
NEG_INF = -1e30

IN_SIZES = (Q_LORA, KV_LORA, ROPE_D, W_A,
            W_B, W_B, W_B, H_B, W_B,
            SHIFT_COLS, W_C,
            3 * D_MODEL)
IN_COLS = sum(IN_SIZES)
RWKV_SIZES = (W_C, W_C, W_C, DECAY_LORA, AAA_LORA)


def rmsnorm(x, g, eps=EPS):
    xf = x.astype(jnp.float32)
    y = xf * lax.rsqrt(jnp.mean(xf * xf, axis=-1, keepdims=True) + eps)
    return (y * g.astype(jnp.float32)).astype(x.dtype)

def split_cols(p, sizes):
    idx = np.cumsum(np.array(sizes))[:-1].tolist()
    return jnp.split(p, idx, axis=-1)

def rope_tables(seq):
    inv = ROPE_THETA ** (-jnp.arange(0, ROPE_D, 2, dtype=jnp.float32) / ROPE_D)
    ang = jnp.arange(seq, dtype=jnp.float32)[:, None] * inv[None, :]
    return jnp.cos(ang)[:, None, :], jnp.sin(ang)[:, None, :]

def apply_rope(x, cos, sin):
    half = ROPE_D // 2
    x1 = x[..., :half].astype(jnp.float32)
    x2 = x[..., half:].astype(jnp.float32)
    out = jnp.concatenate([x1 * cos - x2 * sin, x2 * cos + x1 * sin], axis=-1)
    return out.astype(x.dtype)

def causal_block_attention(q, k, v, cum=None):
    B, H, S, Dk = q.shape
    Dv = v.shape[-1]
    nb = S // Q_BLOCK
    scale = Dk ** -0.5
    kpos = jnp.arange(S)
    q_blocks = q.reshape(B, H, nb, Q_BLOCK, Dk).transpose(2, 0, 1, 3, 4)
    use_decay = cum is not None
    xs = (jnp.arange(nb), q_blocks)
    if use_decay:
        xs = xs + (cum.reshape(B, H, nb, Q_BLOCK).transpose(2, 0, 1, 3),)

    def block(args):
        i, qb = args[0], args[1]
        s = jnp.einsum('bhqd,bhkd->bhqk', qb, k).astype(jnp.float32) * scale
        if use_decay:
            s = s + args[2][..., :, None] - cum[:, :, None, :]
        qpos = i * Q_BLOCK + jnp.arange(Q_BLOCK)
        s = jnp.where(kpos[None, :] <= qpos[:, None], s, NEG_INF)
        p = jax.nn.softmax(s, axis=-1)
        return jnp.einsum('bhqk,bhkd->bhqd', p.astype(v.dtype), v)

    o = lax.map(block, xs)
    return o.transpose(1, 0, 3, 2, 4).reshape(B, S, H * Dv)

def mla_branch(c_q, c_kv, k_r, gate, qa_g, w_uq, kva_g, w_ukv, q_g, knope_g, krope_g, cos, sin):
    B, S, _ = c_q.shape
    q = (rmsnorm(c_q, qa_g) @ w_uq).reshape(B, S, H_A, NOPE + ROPE_D)
    q = rmsnorm(q, q_g)
    q = jnp.concatenate([q[..., :NOPE], apply_rope(q[..., NOPE:], cos, sin)], axis=-1)
    kv = (rmsnorm(c_kv, kva_g) @ w_ukv).reshape(B, S, H_A, NOPE + V_A)
    k_nope = rmsnorm(kv[..., :NOPE], knope_g)
    v = kv[..., NOPE:]
    k_rope = apply_rope(rmsnorm(k_r, krope_g)[:, :, None, :], cos, sin)
    k = jnp.concatenate([k_nope, jnp.broadcast_to(k_rope, (B, S, H_A, ROPE_D))], axis=-1)
    o = causal_block_attention(q.transpose(0, 2, 1, 3), k.transpose(0, 2, 1, 3), v.transpose(0, 2, 1, 3))
    return o * jax.nn.silu(gate)

def fox_branch(fq, fk, fv, ff, gate, b_f, q_g, k_g):
    B, S, _ = fq.shape
    q = rmsnorm(fq.reshape(B, S, H_B, HD_B), q_g)
    k = rmsnorm(fk.reshape(B, S, H_B, HD_B), k_g)
    v = fv.reshape(B, S, H_B, HD_B)
    log_f = jax.nn.log_sigmoid((ff + b_f).astype(jnp.float32))
    cum = jnp.cumsum(log_f, axis=1).transpose(0, 2, 1)
    o = causal_block_attention(q.transpose(0, 2, 1, 3), k.transpose(0, 2, 1, 3), v.transpose(0, 2, 1, 3), cum)
    return o * jax.nn.silu(gate)

def rwkv7_scan(r, w, k, v, kk, a):
    B, S, H, N = r.shape

    def step(state, inp):
        r_t, w_t, k_t, v_t, kk_t, a_t = inp
        sa = jnp.einsum('bhvk,bhk->bhv', state, -kk_t)
        state = (state * w_t[:, :, None, :] + sa[..., None] * (kk_t * a_t)[:, :, None, :]
                 + v_t[..., None] * k_t[:, :, None, :])
        return state, jnp.einsum('bhvk,bhk->bhv', state, r_t)

    xs = tuple(t.transpose(1, 0, 2, 3) for t in (r, w, k, v, kk, a))
    _, y = lax.scan(step, jnp.zeros((B, H, N, N), jnp.float32), xs)
    return y.transpose(1, 0, 2, 3)

def rwkv_branch(r, k, v, wl, al, gate, w0, w_up, a0, a_up, k_k, k_a, r_k, lnx_g, lnx_b):
    B, S, _ = r.shape
    f32 = jnp.float32
    heads = lambda t: t.astype(f32).reshape(B, S, H_C, HD_C)
    w = jnp.exp(-RWKV_DECAY_SCALE * jax.nn.sigmoid((w0 + jnp.tanh(wl) @ w_up).astype(f32)))
    a = jax.nn.sigmoid((a0 + al @ a_up).astype(f32))
    kk = heads(k * k_k)
    kk = kk / jnp.maximum(jnp.sqrt(jnp.sum(kk * kk, axis=-1, keepdims=True)), 1e-12)
    k_mod = k.astype(f32) * (1.0 + (a - 1.0) * k_a.astype(f32))
    r_h, w_h, k_h, v_h, a_h = heads(r), heads(w), heads(k_mod), heads(v), heads(a)
    y = rwkv7_scan(r_h, w_h, k_h, v_h, kk, a_h)
    mu = jnp.mean(y, axis=-1, keepdims=True)
    var = jnp.mean(jnp.square(y - mu), axis=-1, keepdims=True)
    y = ((y - mu) * lax.rsqrt(var + GN_EPS)).reshape(B, S, W_C) * lnx_g.astype(f32) + lnx_b.astype(f32)
    bonus = jnp.sum(r_h * k_h * r_k.astype(f32), axis=-1, keepdims=True) * v_h
    out = (y + bonus.reshape(B, S, W_C)) * jax.nn.silu(gate.astype(f32))
    return out.astype(gate.dtype)

def second_inputs(seed: int = 0) -> dict:
    key = jax.random.key(seed)
    ks = iter(jax.random.split(key, 48))
    f32 = jnp.float32
    L, Lv = DEPTH, DEPTH - 1

    def nrm(shape, scale):
        return scale * jax.random.normal(next(ks), shape, f32)

    def gain(shape):
        return 1.0 + nrm(shape, 0.02)

    x = jax.random.normal(next(ks), (BATCH, SEQ, D_MODEL), f32)
    return {
        "x": x,
        "norm_g": gain((L, D_MODEL)),
        "w_in": nrm((L, D_MODEL, IN_COLS), D_MODEL ** -0.5),
        "mla_qa_g": gain((L, Q_LORA)),
        "mla_w_uq": nrm((L, Q_LORA, H_A * (NOPE + ROPE_D)), Q_LORA ** -0.5),
        "mla_kva_g": gain((L, KV_LORA)),
        "mla_w_ukv": nrm((L, KV_LORA, H_A * (NOPE + V_A)), KV_LORA ** -0.5),
        "mla_q_g": gain((L, NOPE + ROPE_D)),
        "mla_knope_g": gain((L, NOPE)),
        "mla_krope_g": gain((L, ROPE_D)),
        "fox_b_f": jnp.broadcast_to(jnp.linspace(1.0, 6.0, H_B, dtype=f32), (L, H_B)) + nrm((L, H_B), 0.1),
        "fox_q_g": gain((L, HD_B)),
        "fox_k_g": gain((L, HD_B)),
        "rwkv_mu": jax.random.uniform(next(ks), (L, SHIFT_COLS), f32),
        "rwkv_w0": nrm((L, W_C), 1.0),
        "rwkv_w_up": nrm((L, DECAY_LORA, W_C), 0.5 * DECAY_LORA ** -0.5),
        "rwkv_a0": nrm((L, W_C), 0.5),
        "rwkv_a_up": nrm((L, AAA_LORA, W_C), 0.5 * AAA_LORA ** -0.5),
        "rwkv_k_k": 0.85 + nrm((L, W_C), 0.1),
        "rwkv_k_a": 1.0 + nrm((L, W_C), 0.1),
        "rwkv_r_k": nrm((L, H_C, HD_C), 0.1),
        "rwkv_lnx_g": gain((L, W_C)),
        "rwkv_lnx_b": nrm((L, W_C), 0.02),
        "rwkv_v0": nrm((Lv, W_C), 0.5),
        "rwkv_v_down": nrm((Lv, W_C, MV_LORA), W_C ** -0.5),
        "rwkv_v_up": nrm((Lv, MV_LORA, W_C), 0.5 * MV_LORA ** -0.5),
        "w_pa": nrm((L, W_A, D_MODEL), W_A ** -0.5),
        "w_pb": nrm((L, W_B, D_MODEL), W_B ** -0.5),
        "w_pc": nrm((L, W_C, D_MODEL), W_C ** -0.5),
        "w_out": nrm((L, D_MODEL, D_MODEL), D_MODEL ** -0.5),
    }

def second_block(x, norm_g, w_in, mla_qa_g, mla_w_uq, mla_kva_g, mla_w_ukv, mla_q_g, mla_knope_g,
              mla_krope_g, fox_b_f, fox_q_g, fox_k_g, rwkv_mu, rwkv_w0, rwkv_w_up, rwkv_a0, rwkv_a_up,
              rwkv_k_k, rwkv_k_a, rwkv_r_k, rwkv_lnx_g, rwkv_lnx_b, rwkv_v0, rwkv_v_down, rwkv_v_up,
              w_pa, w_pb, w_pc, w_out):
    S = x.shape[1]
    cos, sin = rope_tables(S)
    v_first = None
    for l in range(DEPTH):
        h = rmsnorm(x, norm_g[l])
        p = h @ w_in[l]
        (c_q, c_kv, k_r, gate_a, fq, fk, fv, ff, gate_b,
         shift_cols, gate_c, merge_cols) = split_cols(p, IN_SIZES)

        o_a = mla_branch(c_q, c_kv, k_r, gate_a, mla_qa_g[l], mla_w_uq[l], mla_kva_g[l], mla_w_ukv[l],
                         mla_q_g[l], mla_knope_g[l], mla_krope_g[l], cos, sin)
        o_b = fox_branch(fq, fk, fv, ff, gate_b, fox_b_f[l], fox_q_g[l], fox_k_g[l])
        prev = jnp.pad(shift_cols, ((0, 0), (1, 0), (0, 0)))[:, :-1]
        shifted = shift_cols + rwkv_mu[l] * (prev - shift_cols)
        r, k, v, wl, al = split_cols(shifted, RWKV_SIZES)
        if l == 0:
            v_first = v
        else:
            nu = jax.nn.sigmoid(rwkv_v0[l - 1] + (v @ rwkv_v_down[l - 1]) @ rwkv_v_up[l - 1])
            v = v + (v_first - v) * nu
        o_c = rwkv_branch(r, k, v, wl, al, gate_c, rwkv_w0[l], rwkv_w_up[l], rwkv_a0[l], rwkv_a_up[l],
                          rwkv_k_k[l], rwkv_k_a[l], rwkv_r_k[l], rwkv_lnx_g[l], rwkv_lnx_b[l])

        g_a, g_b, g_c = jnp.split(merge_cols, 3, axis=-1)
        merged = (jax.nn.sigmoid(g_a) * (o_a @ w_pa[l])
                  + jax.nn.sigmoid(g_b) * (o_b @ w_pb[l])
                  + jax.nn.sigmoid(g_c) * (o_c @ w_pc[l]))
        x = x + (merged @ w_out[l]).astype(x.dtype)
    return x


def setup_inputs(seed=0):
    out = dict(first_inputs(seed))
    for name, value in second_inputs(seed + 1).items():
        if name != "x":
            out[name + "_2"] = value
    return out


def reference(
    x, c, ctx, c_ctx, w_mod, b_mod, ln_mix_g, ln_mix_b, ln_ffn_g, ln_ffn_b, w_mix_in, q_norm_g,
    k_norm_g, w_pool_grp, pool_scale, w_mix_out, w_conv_in, conv_w, w_conv_out, w_router,
    w_exp_gate, w_exp_up, w_exp_down, norm_g_2, w_in_2, mla_qa_g_2, mla_w_uq_2, mla_kva_g_2,
    mla_w_ukv_2, mla_q_g_2, mla_knope_g_2, mla_krope_g_2, fox_b_f_2, fox_q_g_2, fox_k_g_2,
    rwkv_mu_2, rwkv_w0_2, rwkv_w_up_2, rwkv_a0_2, rwkv_a_up_2, rwkv_k_k_2, rwkv_k_a_2,
    rwkv_r_k_2, rwkv_lnx_g_2, rwkv_lnx_b_2, rwkv_v0_2, rwkv_v_down_2, rwkv_v_up_2, w_pa_2,
    w_pb_2, w_pc_2, w_out_2,
):
    x = first_block(
        x, c, ctx, c_ctx, w_mod, b_mod, ln_mix_g, ln_mix_b, ln_ffn_g, ln_ffn_b, w_mix_in,
        q_norm_g, k_norm_g, w_pool_grp, pool_scale, w_mix_out, w_conv_in, conv_w, w_conv_out,
        w_router, w_exp_gate, w_exp_up, w_exp_down,
    )
    return second_block(
        x, norm_g_2, w_in_2, mla_qa_g_2, mla_w_uq_2, mla_kva_g_2, mla_w_ukv_2, mla_q_g_2,
        mla_knope_g_2, mla_krope_g_2, fox_b_f_2, fox_q_g_2, fox_k_g_2, rwkv_mu_2, rwkv_w0_2,
        rwkv_w_up_2, rwkv_a0_2, rwkv_a_up_2, rwkv_k_k_2, rwkv_k_a_2, rwkv_r_k_2, rwkv_lnx_g_2,
        rwkv_lnx_b_2, rwkv_v0_2, rwkv_v_down_2, rwkv_v_up_2, w_pa_2, w_pb_2, w_pc_2, w_out_2,
    )


_drawn_inputs = setup_inputs


def setup_inputs(seed=0):
    import zlib

    import numpy as np

    out = dict(_drawn_inputs(seed))
    spreads = {}
    factors = {'ctx': 8.0,
     'c_ctx': 3.175,
     'b_mod': 5.926,
     'q_norm_g': 8.0,
     'k_norm_g': 8.0,
     'pool_scale': 8.0,
     'mla_qa_g_2': 8.0,
     'mla_kva_g_2': 8.0,
     'mla_q_g_2': 8.0,
     'mla_knope_g_2': 8.0,
     'mla_krope_g_2': 8.0,
     'fox_q_g_2': 8.0,
     'fox_k_g_2': 8.0,
     'rwkv_k_k_2': 4.613,
     'rwkv_lnx_g_2': 6.202,
     'rwkv_lnx_b_2': 6.457}
    for name, (base, spread) in spreads.items():
        noise = np.random.default_rng([zlib.crc32(name.encode()), seed]).standard_normal(out[name].shape)
        drawn = base * np.exp(spread * noise) if base else spread * noise
        out[name] = __import__('jax').numpy.asarray(drawn.astype(out[name].dtype))
    for name, factor in factors.items():
        out[name] = (out[name] * factor).astype(out[name].dtype)
    return out
```

```python
from contextlib import ExitStack

import numpy as np

import concourse.bass as bass
from concourse import mybir

F32 = mybir.dt.float32
U32 = mybir.dt.uint32
ALU = mybir.AluOpType
ACT = mybir.ActivationFunctionType
AX_X = mybir.AxisListType.X

P = 128
T = 256
TT = T // P
D = 1024
KD = D // P
E = 16
CAP = 2 * T // E
EG = 4
NG = E // EG
HALF = 512
ALPHA = 4.0 ** 0.25
EPS = 1e-6
GN_EPS = 64e-5
RING = 4
SLOT = 8 * 520
CH = 64
DECAY = 0.606531
NEG = -1e30
LEVELS = 6
H2 = 8

C_Q, C_KV, K_R, G_A, F_Q, F_K, F_V, F_F, G_B = 0, 256, 384, 416, 928, 1440, 1952, 2464, 2472
SH, G_C, MG = 2984, 4648, 5160


def _put(parts, offsets, name, a):
    a = np.asarray(a, np.float32)
    a = a.reshape(a.shape[0], -1)
    full = np.zeros((P, a.shape[1]), np.float32)
    full[:a.shape[0]] = a
    offsets[name] = (sum(x.shape[1] for x in parts), a.shape[1])
    parts.append(full)


def common_tables():
    parts, at = [], {}
    _put(parts, at, "ident", np.eye(P))
    _put(parts, at, "head_ones", np.kron(np.eye(2), np.ones((64, 64))))
    _put(parts, at, "ones", np.ones((P, P)))
    strip = np.arange(P) % 32
    _put(parts, at, "sum_row0", np.repeat((strip == 0)[:, None], P, 1))
    _put(parts, at, "sum_cols", np.stack([strip == 0, strip == 1], 1))
    _put(parts, at, "eps", np.full((P, 1), EPS))
    _put(parts, at, "gn_eps", np.full((P, 1), GN_EPS))
    return np.concatenate(parts, 1), at


def first_tables():
    parts, at = [], {}
    swap = np.zeros((P, P))
    for i in range(0, P, 2):
        swap[i + 1, i] = -1
        swap[i, i + 1] = 1
    _put(parts, at, "swap", swap)
    inv = np.float32(10000.0) ** (-np.arange(0, 32, 2, dtype=np.float32) / np.float32(32))
    row, col = np.arange(T) // 64, np.arange(T) % 64
    ang = np.concatenate([row[:, None].astype(np.float32) * inv, col[:, None].astype(np.float32) * inv], 1)
    ang = np.tile(np.repeat(ang, 2, 1).T, (2, 1))
    _put(parts, at, "cos", np.cos(ang))
    _put(parts, at, "sin", np.sin(ang))
    band = np.zeros((TT, P, 4, T))
    for g, w in enumerate((2, 4, 8, 16)):
        for t in range(T):
            lo, hi = max(t - w // 2, 0), min(t + w // 2, T)
            for s in range(lo, hi):
                band[s // P, s % P, g, t] += 1.0 / (hi - lo)
            band[t // P, t % P, g, t] -= 1.0
    _put(parts, at, "band", band.transpose(1, 0, 2, 3))
    _put(parts, at, "iota", np.repeat(np.arange(T)[None], P, 0))
    _put(parts, at, "token", np.stack([np.arange(P), np.arange(P) + P], 1))
    _put(parts, at, "own_expert", np.kron(np.eye(E), np.ones((1, CAP))))
    return np.concatenate(parts, 1), at


def second_tables():
    parts, at = [], {}
    swap = np.zeros((96, 96))
    for i in range(16):
        swap[64 + 16 + i, 64 + i] = -1
        swap[64 + i, 64 + 16 + i] = 1
    _put(parts, at, "swap", swap)
    inv = np.float32(10000.0) ** (-np.arange(0, 32, 2, dtype=np.float32) / np.float32(32))
    ang = (np.arange(T, dtype=np.float32)[:, None] * inv).T
    c, s = np.ones((96, T)), np.zeros((96, T))
    c[64:80] = c[80:96] = np.cos(ang)
    s[64:80] = s[80:96] = np.sin(ang)
    _put(parts, at, "cos", c)
    _put(parts, at, "sin", s)
    causal = np.where(np.arange(P)[None] <= np.arange(P)[:, None], 0.0, NEG)
    _put(parts, at, "causal", np.concatenate([causal, np.zeros((P, P)), causal], 1))
    i, t = np.arange(P)[:, None], np.arange(P)[None]
    same = i // CH == t // CH
    _put(parts, at, "upper", np.concatenate([same & (i < t), same & (i <= t)], 1))
    _put(parts, at, "neg_pair", -1.0 * (same & (i // 2 == t // 2) & (i > t)))
    _put(parts, at, "neg_pair_t", -1.0 * (same & (i // 2 == t // 2) & (i < t)))
    for n in range(1, LEVELS):
        b = 2 ** n
        _put(parts, at, f"level{n}", (i // (2 * b) == t // (2 * b)) & (i // b + 1 == t // b))
    _put(parts, at, "carry", np.repeat((np.arange(2 * T)[None] % CH != 0), P, 0))
    return np.concatenate(parts, 1), at


def param_columns(inp=None):
    f = (lambda n: inp[n]) if inp is not None else (lambda n: None)
    parts, at = [], {}

    def col(name, a, tiles, rows=P):
        a = np.zeros((tiles, rows), np.float32) if a is None else np.asarray(a).reshape(tiles, rows)
        _put(parts, at, name, a.T)

    def sub(a, *i):
        return None if a is None else np.asarray(a)[i]

    col("cond", None if inp is None else np.stack([f("c")[0], f("c_ctx")]), 2 * KD)
    for layer in range(2):
        b = sub(f("b_mod"), layer)
        for m in (0, 1, 3, 4):
            col(f"b_mod{layer}{m}", None if b is None else b[m * D:(m + 1) * D], KD)
    two = lambda a: None if a is None else np.tile(a, 2)
    col("q_g", two(sub(f("q_norm_g"), 0)), 1)
    col("k_g", two(sub(f("k_norm_g"), 0)), 1)
    col("pool_scale", sub(f("pool_scale"), 0), 4)
    col("conv_w", sub(f("conv_w"), 0), 3 * KD)
    for layer in range(2):
        g = lambda n: sub(f(n + "_2"), layer)
        col(f"norm_g{layer}", g("norm_g"), KD)
        col(f"qa_g{layer}", g("mla_qa_g"), 2)
        col(f"kva_g{layer}", g("mla_kva_g"), 1)
        col(f"mq_g{layer}", g("mla_q_g"), 1, 96)
        kn, kr = g("mla_knope_g"), g("mla_krope_g")
        col(f"mk_g{layer}", None if kn is None else np.concatenate([kn, kr]), 1, 96)
        col(f"fb{layer}", g("fox_b_f"), 1, 8)
        col(f"fq_g{layer}", two(g("fox_q_g")), 1)
        col(f"fk_g{layer}", two(g("fox_k_g")), 1)
        col(f"mu{layer}", g("rwkv_mu"), 13)
        for n in ("w0", "a0", "k_k", "k_a", "r_k", "lnx_g", "lnx_b"):
            col(f"{n}{layer}", g("rwkv_" + n), 4)
    col("v0", sub(f("rwkv_v0_2"), 0), 4)
    return np.concatenate(parts, 1), at


class Signal:

    def __init__(self, handle, marks):
        self.handle, self.marks, self.value, self.period = handle, marks, 0, 0

    def up(self, *key):
        self.value += 1
        self.marks[key] = self.value
        return self.handle, 1

    def at(self, *key):
        return self.handle, self.marks.get(key, 1)

    def turn(self, g, *key):
        return self.handle, g * self.marks.get("period", 1) + self.marks.get(key, 1)

    def open_loop(self):
        self.start = self.value

    def close_loop(self, turns):
        self.marks["period"] = self.value - self.start
        self.value += (turns - 1) * (self.value - self.start)


INPUTS = ["x", "ctx", "b_mod", "ln_mix_g", "ln_mix_b", "ln_ffn_g", "ln_ffn_b", "w_mod", "w_mix_in", "w_pool_grp",
          "w_mix_out", "w_conv_in", "w_conv_out", "w_router", "w_exp_gate", "w_exp_up", "w_exp_down", "w_in_2",
          "mla_w_uq_2", "mla_w_ukv_2", "rwkv_lora", "rwkv_v_down_2", "rwkv_v_up_2", "w_pa_2", "w_pb_2", "w_pc_2",
          "w_out_2", "tables", "tables_first", "tables_second", "params"]


def weight_stream(w):
    order = []

    def rows(a):
        return a.rearrange("(k p) n -> p k n", p=P)

    def add(key, src):
        order.append((key, src))

    for layer in range(2):
        for j in range(12):
            add(("mod", layer, j), rows(w["w_mod"][layer, :, j * HALF:(j + 1) * HALF]))
        if layer == 0:
            for j, (a, b) in enumerate(((0, 512), (512, 768), (768, 1280))):
                add(("mix_in", j), rows(w["w_mix_in"][0, :, a:b]))
            for j in range(2):
                add(("mix_out", 0, j), rows(w["w_mix_out"][0, :, j * HALF:(j + 1) * HALF]))
        else:
            for j in (2, 4, 3, 5, 0, 1):
                add(("conv_in", j), rows(w["w_conv_in"][0, :, j * HALF:(j + 1) * HALF]))
            for j in range(2):
                add(("mix_out", 1, j), rows(w["w_conv_out"][0, :, j * HALF:(j + 1) * HALF]))
        for s in range(3 * KD * NG):
            add(("expert", layer, s), None)
    for layer in range(2):
        wi = w["w_in_2"][layer]
        for j in range(3):
            add(("in", layer, "rkv", j), rows(wi[:, SH + j * HALF:SH + (j + 1) * HALF]))
        add(("in", layer, "lora"), rows(wi[:, SH + 3 * HALF:SH + 3 * HALF + P]))
        add(("in", layer, "gate_c"), rows(wi[:, G_C:G_C + HALF]))
        add(("in", layer, "latent"), rows(wi[:, C_Q:G_A]))
        add(("uq", layer), rows(w["mla_w_uq_2"][layer]))
        add(("ukv", layer), rows(w["mla_w_ukv_2"][layer]))
        add(("in", layer, "gate_a"), rows(wi[:, G_A:G_A + HALF]))
        add(("in", layer, "fq"), rows(wi[:, F_Q:F_Q + HALF]))
        add(("in", layer, "fk"), rows(wi[:, F_K:F_K + HALF]))
        add(("in", layer, "fv"), rows(wi[:, F_V:F_V + HALF]))
        add(("in", layer, "ff_gate_b"), rows(wi[:, F_F:SH]))
        for b, n in enumerate(("w_pa_2", "w_pb_2", "w_pc_2")):
            add(("proj", layer, b), rows(w[n][layer]))
            for j in range(2):
                a = MG + b * D + j * HALF
                add(("in", layer, "merge", b, j), rows(wi[:, a:a + HALF]))
        for j in range(2):
            add(("out", layer, j), rows(w["w_out_2"][layer][:, j * HALF:(j + 1) * HALF]))
    return order


def two_block_program(nc, w, out, marks, upto=99):
    order = weight_stream(w)
    number = {key: n for n, (key, _) in enumerate(order)}
    view = {key: src for key, src in order}
    tab_at, first_at, second_at, par_at = (f()[1] for f in (common_tables, first_tables, second_tables, param_columns))
    n_tab, n_first, n_second, n_par = (w[n].shape[1] for n in ("tables", "tables_first", "tables_second", "params"))

    with ExitStack() as ctx:
        def sb(name, cols, dt=F32):
            return ctx.enter_context(nc.sbuf_tensor(name, [P, cols], dt))

        ring = sb("ring", RING * SLOT)
        h_t = sb("h", TT * D)
        h = h_t[:, :].rearrange("p (a d) -> p a d", a=TT)
        ln_t = sb("ln", 2 * D)
        ln = ln_t[:, :].rearrange("p (a d) -> p a d", a=2)
        gate_t = sb("gate", 2 * D)
        gate = gate_t[:, :].rearrange("p (a d) -> p a d", a=2)
        tab = sb("tab", n_tab)
        tab2 = sb("tab2", max(n_first, n_second))
        par = sb("par", n_par)
        small_t = sb("small", 1152)
        arena = sb("arena", 22600)
        ps_t = ctx.enter_context(nc.psum_tensor("ps", [P, 8 * HALF], F32))

        def bank(b, n=HALF):
            return ps_t[:, b * HALF:b * HALF + n]

        def T1(name):
            o, n = tab_at[name]
            return tab[:, o:o + n]

        def T2(name, which=first_at):
            o, n = which[name]
            return tab2[:, o:o + n]

        def PC(name, i=0, rows=P):
            o, _ = par_at[name]
            return par[0:rows, o + i:o + i + 1]

        class Scratch:
            def __init__(self, at=0):
                self.top = at

            def take(self, cols, *dims):
                v = arena[:, self.top:self.top + cols]
                self.top += cols
                assert self.top <= 22600, self.top
                if len(dims) == 1:
                    v = v.rearrange("p (a n) -> p a n", a=dims[0])
                if len(dims) == 2:
                    v = v.rearrange("p (a b n) -> p a b n", a=dims[0], b=dims[1])
                if len(dims) == 3:
                    v = v.rearrange("p (a b c n) -> p a b c n", a=dims[0], b=dims[1], c=dims[2])
                return v

        signals = {}

        def S(name):
            if name not in signals:
                handle = ctx.enter_context(nc.semaphore(name))
                signals[name] = Signal(handle, marks.setdefault(name, {}))
            return signals[name]

        landed = [ctx.enter_context(nc.semaphore(f"weights_landed{s}")) for s in range(RING)]
        used = ctx.enter_context(nc.semaphore("weights_used"))

        def slot(key, *dims):
            s = number[key] % RING
            src = view[key]
            k, n = (src.shape[1], src.shape[2]) if src is not None else (EG, D)
            return ring[:, s * SLOT:s * SLOT + k * n].rearrange("p (k n) -> p k n", k=k)

        def has_landed(key):
            n = number[key]
            return landed[n % RING], 16 * (n // RING + 1)

        def consumed(key):
            return used, number[key] + 1

        loads = {}

        def loaded(name, n=1):
            if name not in loads:
                loads[name] = ctx.enter_context(nc.semaphore("loaded_" + name))
            return loads[name], 16 * n

        sc = Scratch()
        m0 = dict(xc=sc.take(2048, TT), ut=sc.take(2048, KD), uc=sc.take(2048, KD), q=sc.take(1024, 4),
                  k=sc.take(1024, 2), v=sc.take(512, 4), pt=sc.take(1024, TT), mix=sc.take(2048, KD),
                  sq=sc.take(512), sd=sc.take(512), xn=sc.take(512), t1=sc.take(512), t2=sc.take(512),
                  prob=sc.take(1024, 2), prob_t=sc.take(1024, 2), stat=sc.take(64), pooled=sc.take(1024, 4))
        sc = Scratch()
        m1 = dict(ut=sc.take(2048, KD), c=sc.take(2048, KD), z=sc.take(KD * 258, KD), conv=sc.take(2048, KD),
                  mix=sc.take(2048, KD))
        sc = Scratch()
        ff = dict(ut=sc.take(2048, KD), wk=sc.take(256), vals=sc.take(32), ex=sc.take(32, TT), st=sc.take(16), idf=sc.take(32), di=sc.take(512, E), dg=sc.take(512, E),
                  cols=sc.take(8), pick=sc.take(1024, TT), put=sc.take(1024, NG), xe=sc.take(4096, KD),
                  xg=sc.take(1024, KD), hg=sc.take(1024), ht=sc.take(1024, KD), ye=sc.take(4096, NG))
        idx_u = ctx.enter_context(nc.sbuf_tensor("idx", [P, CAP], U32))
        sc = Scratch(21300)
        md = dict(part=sc.take(1024, 2), condT=sc.take(256, KD), sig=sc.take(16))
        modcol_t = sb("modcol", 64)
        modcol = modcol_t[:, :].rearrange("p (m k c) -> p m k c", m=4, k=KD)
        sc = Scratch(19200)
        pn = dict(t=sc.take(2048, TT), st=sc.take(24, TT), mv=sc.take(4, TT), rs=sc.take(4, TT))

        sc = Scratch()
        s2 = dict(ht=sc.take(2048, KD), oc=sc.take(1024, 4))
        low = sc.top
        s2.update(rkv=sc.take(3072, 3, 4), wal=sc.take(256))
        raw0 = sc.top
        s2.update(raw=sc.take(2 * 4 * 257, 2, 4), diff=sc.take(1024, 4), vd=sc.take(256), nu=sc.take(1024, 4))
        v_first = gate_t[:, 0:1024].rearrange("p (j t) -> p j t", j=4)
        merged = ln_t[:, :].rearrange("p (k t) -> p k t", k=KD)
        xn_tok = ln
        sc = Scratch(raw0)
        rw = {}
        x0 = sc.top
        for n in ("lw", "L", "a", "kk", "kmod", "eLm", "eN", "eH", "tmp"):
            rw[n] = sc.take(512)
        sg = Scratch(x0)
        rw.update(gb=sg.take(2048, 8), gk=sg.take(2048, 8))
        rw.update(eL=sc.take(512), kr=sc.take(1024, 2, 2, 2))
        b0 = sc.top
        rw.update(bt=sc.take(512, 2), kt=sc.take(512, 2), bh=sc.take(512, 2), kh=sc.take(512, 2), bonus=sc.take(512))
        rw.update(inv=sc.take(1024, 8), inv_t=sc.take(1024, 8), prod=sc.take(1024, 8), lev0=sc.take(1024, 8),
                  wk=sc.take(1024, 8), v_tok=sc.take(512, 8), bh_tok=sc.take(512, 8), kh_tok=sc.take(512, 8))
        sg = Scratch(b0)
        rw["lev1"] = sg.take(1024, 8)
        sg = Scratch(b0)
        rw.update(y=sg.take(512, 2), z=sg.take(512, 2), pm=sg.take(512, 4, 2), state=sg.take(512, 4, 2))
        rw["carried"] = rw["wk"].rearrange("p a n -> p (a n)")[:, 0:512].rearrange("p (c j n) -> p c j n", c=4, j=2)
        rw["tmp2"] = rw["inv"].rearrange("p a n -> p (a n)")[:, 0:512]
        sc = Scratch(low)
        at2 = dict(oa=sc.take(1024, 4), ob=sc.take(1024, 4), cq=sc.take(512, 2), ckv=sc.take(256), q=sc.take(2048, 8),
                   k=sc.take(2048, 8), v=sc.take(1024, TT), sq=sc.take(512), sd=sc.take(512), xn=sc.take(512),
                   t1=sc.take(512), t2=sc.take(512), score=sc.take(768, 2), prob=sc.take(768, 2), prob_t=sc.take(768, 2),
                   stat=sc.take(64), ff=sc.take(1024, 4), cum=sc.take(256), ncum=sc.take(256),
                   sg=sc.take(1024, 2), mt=sc.take(512))
        UNITS = 15

        def before(u):
            _, l, i = u
            return ("sec", l, i - 1) if i else (("sec", l - 1, UNITS - 1) if l else None)

        def unit(l, i):
            if i == 0:
                return 0, 128, 512, 256, 0, "ones"
            if i == 1:
                return 0, 128, 256, 128, 1, "ones"
            if i == 2:
                return 64, 96, 256, 32, 3, "ones"
            if i < 7:
                return 0, 96, 512, 96, (4, 5, 6, 0)[i - 3], "ones"
            if i < 11:
                return 0, 64, 512, 64, (1, 3, 4, 5)[i - 7], "ones"
            return 0, 128, 512, 64, (0, 1, 3, 4)[i - 11], "head_ones"

        def unit_ready(l, i):
            return consumed((("in", l, "latent") if i < 3 else ("uq", l) if i < 7 else ("ukv", l) if i < 11 else
                             ("in", l, "fq") if i < 13 else ("in", l, "fk")))

        block = ctx.enter_context(nc.Block())

        @block.sync
        def _(sp):
            n = 0
            while n < len(order):
                key, src = order[n]
                if key[0] == "expert":
                    layer = key[1]
                    if (layer == 0 and upto < 3) or (layer == 1 and upto < 6):
                        break
                    with sp.Fori(0, NG) as g:
                        for m, name in enumerate(("w_exp_gate", "w_exp_up", "w_exp_down")):
                            wv = w[name][layer].rearrange("(g e) (k p) f -> g p k e f", e=EG, p=P)
                            for k in range(KD):
                                i = n + m * KD + k
                                s = i % RING
                                sp.wait_ge(used, g * (3 * KD) + (i - RING + 1))
                                sp.dma_start(ring[:, s * SLOT:s * SLOT + EG * D].rearrange("p (e f) -> p e f", e=EG),
                                             wv[bass.ds(g, 1), :, k].rearrange("a p e f -> p (a e) f")
                                             ).then_inc(landed[s], 16)
                    n += 3 * KD * NG
                    continue
                if upto < 7 and key[0] in ("in", "uq", "ukv", "proj", "out") or (upto < 4 and key[1] == 1 and key[0] == "mod"):
                    break
                if n >= RING:
                    sp.wait_ge(used, n - RING + 1)
                sp.dma_start(slot(key), src).then_inc(landed[n % RING], 16)
                n += 1
            if upto >= 99:
                sp.wait_ge(*S("second_dve").at("residual", 1, 1))
                sp.dma_start(out[0].rearrange("(a p) d -> p a d", p=P), h).then_inc(loaded("result")[0], 16)
                sp.wait_ge(*loaded("result"))

        @block.scalar
        def _(act):
            A = nc.scalar.activation
            act.dma_start(par[:, :], w["params"]).then_inc(loaded("params")[0], 16)
            act.dma_start(tab[:, :], w["tables"]).then_inc(loaded("tables")[0], 16)
            act.dma_start(h, w["x"][0].rearrange("(a p) d -> p a d", p=P)).then_inc(loaded("x")[0], 16)
            act.dma_start(m0["xc"], w["ctx"][0].rearrange("(a p) d -> p a d", p=P)).then_inc(loaded("ctx")[0], 16)
            act.dma_start(tab2[:, 0:n_first], w["tables_first"]).then_inc(loaded("tables_first")[0], 16)
            act.dma_start(small_t[:, 0:512].rearrange("p (g d) -> p g d", g=4),
                          w["w_pool_grp"][0].rearrange("g c d -> c g d")).then_inc(loaded("small")[0], 16)

            def modulation(l):
                Sa, Sp, Sv = S("mod_act"), S("mod_pe"), S("mod_dve")
                if l == 0:
                    act.wait_ge(*loaded("params"))
                    o = par_at["cond"][0]
                    A(md["sig"], par[:, o:o + 16], ACT.Sigmoid).then_inc(*Sa.up("sigmoid"))
                for j in range(12):
                    act.wait_ge(*consumed(("mod", l, j)))
                    if j >= 2:
                        act.wait_ge(*Sp.at("fold", l, j - 2))
                    A(md["part"][:, j % 2], bank(j % 2), ACT.Copy).then_inc(*Sa.up("part", l, j))

            def turned(name, dst, scale, bias):
                for pair in (0, 2):
                    act.wait_ge(*S("turn_pe").at(name, pair))
                    for i in range(2):
                        k = 2 * pair + i
                        src = bank(4 + pair)[:, i * T:(i + 1) * T]
                        if bias is None:
                            A(dst[:, k], src, ACT.Copy, scale=scale(k)).then_inc(*S("turn_act").up(name, k))
                        else:
                            A(dst[:, k], src, ACT.Identity, scale=scale(k), bias=bias(k)).then_inc(*S("turn_act").up(name, k))

            def norm(u, ready, x, rows, n, width, bufs, eps="eps"):
                Sn, Sp, Sv = S("norm_act"), S("norm_pe"), S("norm_dve")
                act.wait_ge(*ready)
                if u[-1] > 0:
                    act.wait_ge(*Sp.at("sum", u[:-1] + (u[-1] - 1,)))
                A(bufs["sq"][0:rows, 0:n], x, ACT.Square).then_inc(*Sn.up("sq", u))
                act.wait_ge(*Sp.at("sum", u))
                if u[-1] > 0:
                    act.wait_ge(*Sv.at("rs", u[:-1] + (u[-1] - 1,)))
                A(bufs["sd"][0:rows, 0:n], bank(2)[0:rows, 0:n], ACT.Sqrt, scale=1.0 / width,
                  bias=T1(eps)[0:rows]).then_inc(*Sn.up("sd", u))

            def attention0():
                Sa, Sp, Sv = S("att_act"), S("att_pe"), S("att_dve")
                st = m0["stat"]
                for u in range(17):
                    if u < 16:
                        act.wait_ge(*Sv.at("max", 0, u))
                        if u >= 2:
                            act.wait_ge(*Sp.at("turned", 0, u - 2))
                        A(m0["prob"][:, u % 2], bank(4 + u % 2), ACT.Exp, scale=0.125, bias=st[:, u:u + 1],
                          accum_out=st[:, 32 + u:33 + u]).then_inc(*Sa.up("exp", 0, u))
                    if u >= 1:
                        act.wait_ge(*Sp.at("turned", 0, u - 1))
                        if u >= 3:
                            act.wait_ge(*Sp.at("value", 0, u - 3))
                        A(m0["prob_t"][:, (u - 1) % 2], bank(6), ACT.Copy).then_inc(*Sa.up("prob_t", 0, u - 1))

            def post_norm(l, part):
                for a in range(TT):
                    act.wait_ge(*S("post_dve").at("var", l, part, a))
                    A(pn["rs"][:, a, 0:1], pn["mv"][:, a, 1:2], ACT.Sqrt, bias=T1("eps")
                      ).then_inc(*S("post_act").up("sd", l, part, a))

            def ffn(l):
                Sa, Sp, Sv = S("ffn_act"), S("ffn_pe"), S("ffn_dve")
                act.wait_ge(*Sv.at("neg_max", l))
                for a in range(TT):
                    A(ff["ex"][:, a], bank(0)[:, a * E:(a + 1) * E], ACT.Exp, bias=ff["st"][:, 2 + a:3 + a],
                      accum_out=ff["st"][:, 4 + a:5 + a]).then_inc(*Sa.up("ex", l, a))
                for k in range(0, KD, 2):
                    act.wait_ge(*Sp.at("gather", l, k))
                    A(ff["xe"][:, k], bank(4 + k % 4), ACT.Identity, scale=modcol[:, 3, k, 0:1],
                      bias=modcol[:, 2, k, 0:1]).then_inc(*Sa.up("xe", l, k))
                Sx, Spx = S(f"expert{l}_act"), S(f"expert{l}_pe")
                base = number[("expert", l, 0)]
                Sx.open_loop()
                with act.Fori(0, NG) as g:
                    act.wait_ge(used, g * (3 * KD) + (base + KD))
                    A(ff["hg"], ps_t[:, 0:2 * HALF], ACT.Silu).then_inc(*Sx.up("silu"))
                    for b in range(2):
                        act.wait_ge(*Spx.turn(g, "turned", b))
                        A(ff["ht"][:, 4 * b:4 * b + 4], bank(6 + b).rearrange("p (k n) -> p k n", k=4), ACT.Copy
                          ).then_inc(*Sx.up("ht", b))
                Sx.close_loop(NG)

            def second(l):
                Sa, Sp, Sv, So = S("second_act"), S("second_pe"), S("second_dve"), S("second_pool")
                for a in range(TT):
                    act.wait_ge(*(Sv.at("residual", l - 1, a) if l else S("post_dve").at("h", 1, 1, 1)))
                    if l and a == 0:
                        act.wait_ge(*consumed(("out", l - 1, 1)))
                    A(xn_tok[:, a], h[:, a], ACT.Square, accum_out=at2["stat"][:, 40 + a:41 + a]).then_inc(*Sa.up("square", l, a))
                act.wait_ge(*Sa.at("square", l, 1))
                A(at2["stat"][:, 42:44], at2["stat"][:, 40:42], ACT.Sqrt, scale=1.0 / D, bias=T1("eps")).then_inc(*Sa.up("root", l))
                turned(f"sec{l}", s2["ht"], lambda k: PC(f"norm_g{l}", k), None)
                for n in range(4):
                    act.wait_ge(*consumed(("in", l, "rkv", n) if n < 3 else ("in", l, "lora")))
                    act.wait_ge(*Sv.at("edge", l, n % 2))
                    if n >= 2:
                        act.wait_ge(*Sv.at("mixed", l, n - 2))
                    if n < 3:
                        src = ps_t[:, 2 * n * HALF:(2 * n + 2) * HALF].rearrange("p (j t) -> p j t", j=4)
                        A(s2["raw"][:, n % 2, :, 1:257], src, ACT.Copy).then_inc(*Sa.up("raw", l, n))
                    else:
                        A(s2["raw"][:, 1, 0, 1:257], bank(6, T), ACT.Copy).then_inc(*Sa.up("raw", l, n))
                act.wait_ge(*Sv.at("mixed", l, 3))
                A(s2["wal"][0:64], s2["wal"][0:64], ACT.Tanh).then_inc(*Sa.up("tanh", l))
                act.wait_ge(*consumed(("in", l, "gate_c")))
                for i in range(2):
                    A(s2["oc"][:, 2 * i:2 * i + 2], bank(i).rearrange("p (j t) -> p j t", j=2), ACT.Silu
                      ).then_inc(*Sa.up("gate_c", l, i))
                if l:
                    act.wait_ge(*Sp.at("v_down"))
                    A(s2["vd"][0:32], bank(2, T)[0:32], ACT.Copy).then_inc(*Sa.up("v_down"))
                    for j in range(4):
                        act.wait_ge(*Sp.at("v_up"))
                        A(s2["nu"][:, j], bank(4 + j // 2)[:, j % 2 * T:j % 2 * T + T], ACT.Sigmoid, bias=PC("v0", j)
                          ).then_inc(*Sa.up("nu", j))
                for p in range(2):
                    recurrence(l, p)
                attention_parts(l)

            def recurrence(l, p):
                Sa, Sp, Sv, So = S("rwkv_act"), S("rwkv_pe"), S("rwkv_dve"), S("rwkv_pool")
                K = (l, p)
                act.wait_ge(*Sp.at("lora", *K))
                if p or l:
                    act.wait_ge(*Sv.at("o", *((l, p - 1) if p else (l - 1, 1))))
                if p == 0:
                    act.wait_ge(*(S("second_dve").at("blend", 1) if l else S("second_dve").at("mixed", 0, 3)))
                for jj in range(2):
                    A(rw["lw"][:, jj * T:jj * T + T], bank(0)[:, jj * T:jj * T + T], ACT.Sigmoid, bias=PC(f"w0{l}", 2 * p + jj)
                      ).then_inc(*Sa.up("w", *K, jj))
                    A(rw["a"][:, jj * T:jj * T + T], bank(1)[:, jj * T:jj * T + T], ACT.Sigmoid, bias=PC(f"a0{l}", 2 * p + jj)
                      ).then_inc(*Sa.up("a", *K, jj))
                act.wait_ge(*Sv.at("kk0", *K, 1))
                A(rw["tmp"], rw["kk"], ACT.Square).then_inc(*Sa.up("kk_sq", *K))
                act.wait_ge(*Sp.at("kk_sum", *K))
                A(rw["tmp"], bank(2), ACT.Sqrt).then_inc(*Sa.up("kk_root", *K))
                act.wait_ge(*Sv.at("exponents", *K))
                A(rw["eLm"], rw["eLm"], ACT.Exp).then_inc(*Sa.up("eLm", *K))
                A(rw["eN"], rw["L"], ACT.Exp, scale=-1.0).then_inc(*Sa.up("eN", *K))
                A(rw["eL"], rw["L"], ACT.Exp).then_inc(*Sa.up("eL", *K))
                A(rw["eH"], rw["eH"], ACT.Exp).then_inc(*Sa.up("eH", *K))
                for i, (n, c) in enumerate((("v_tok", 0), ("bh_tok", 0), ("kh_tok", 0), ("wk", 64))):
                    act.wait_ge(*Sp.at("tok", *K, i))
                    for hh in range(2):
                        A(rw[n][:, 4 * hh:4 * hh + 4, c:c + 64],
                          bank(4 + i).rearrange("p (r h c) -> p r h c", r=4, h=2)[:, :, hh], ACT.Copy
                          ).then_inc(*Sa.up("tok", *K, i, hh))
                for n in range(1, LEVELS):
                    for hh in range(2):
                        act.wait_ge(*Sp.at("step", *K, n, hh))
                        A(rw["prod"][:, 4 * hh:4 * hh + 4], bank(2 + hh).rearrange("p (q n) -> p q n", q=4), ACT.Copy
                          ).then_inc(*Sa.up("step", *K, n, hh))
                act.wait_ge(*Sp.at("w1", *K))
                A(rw["wk"][:, :, 0:64], bank(0).rearrange("p (q n) -> p q n", q=8), ACT.Copy).then_inc(*Sa.up("w1", *K))
                act.wait_ge(*Sp.at("y0", *K))
                A(rw["y"], bank(4).rearrange("p (j t) -> p j t", j=2), ACT.Copy).then_inc(*Sa.up("y0", *K))
                act.wait_ge(*Sp.at("pm", *K))
                A(rw["pm"][:, 1:4:2], bank(6, 256).rearrange("p (c j n) -> p c j n", c=2, j=2), ACT.Copy
                  ).then_inc(*Sa.up("pm", *K, 0))
                A(rw["pm"][:, 2], bank(7, 128).rearrange("p (j n) -> p j n", j=2), ACT.Copy).then_inc(*Sa.up("pm", *K, 1))
                act.wait_ge(*Sp.at("carried", *K))
                A(rw["carried"][:, 0:3:2],
                  bank(0, 256).rearrange("p (c j n) -> p c j n", c=2, j=2), ACT.Copy).then_inc(*Sa.up("carried", *K, 0))
                A(rw["carried"][:, 1], bank(1, 128).rearrange("p (j n) -> p j n", j=2), ACT.Copy).then_inc(*Sa.up("carried", *K, 1))
                act.wait_ge(*Sv.at("centred", *K))
                A(rw["tmp2"], rw["y"].rearrange("p j t -> p (j t)"), ACT.Square).then_inc(*Sa.up("gn_sq", *K))
                act.wait_ge(*Sp.at("gn_sum", *K))
                A(rw["tmp2"], bank(5), ACT.Sqrt, scale=1.0 / 64, bias=T1("gn_eps")).then_inc(*Sa.up("gn_root", *K))

            def attention_parts(l):
                Sa, Sp, Sv = S("second_act"), S("second_pe"), S("second_dve")

                def norm2(i):
                    u = ("sec", l, i)
                    r0, r1, n, width, b, _ = unit(l, i)
                    act.wait_ge(*unit_ready(l, i))
                    if before(u):
                        act.wait_ge(*S("norm_pe").at("sum", before(u)))
                    if i == 0:
                        act.wait_ge(*S("rwkv_dve").at("o", l, 1))
                    A(at2["sq"][r0:r1, 0:n], bank(b, n)[r0:r1], ACT.Square).then_inc(*S("norm_act").up("sq", u))
                    act.wait_ge(*S("norm_pe").at("sum", u))
                    if before(u):
                        act.wait_ge(*S("norm_dve").at("rs", before(u)))
                    m = T if i == 0 else n
                    A(at2["sd"][r0:r1, 0:m], bank(2, m)[r0:r1], ACT.Sqrt, scale=1.0 / width, bias=T1("eps")[r0:r1]
                      ).then_inc(*S("norm_act").up("sd", u))

                for i in range(11):
                    norm2(i)
                act.wait_ge(*consumed(("in", l, "gate_a")))
                for i in range(2):
                    A(at2["oa"][:, 2 * i:2 * i + 2], bank((3, 4)[i]).rearrange("p (j t) -> p j t", j=2), ACT.Silu
                      ).then_inc(*Sa.up("gate_a", l, i))
                attention2(l, 0)
                for i in range(11, 15):
                    norm2(i)
                act.wait_ge(*consumed(("in", l, "ff_gate_b")))
                A(at2["ff"][0:8, 0], bank(7, T)[0:8], ACT.Abs, bias=PC(f"fb{l}", 0, 8)).then_inc(*Sa.up("abs", l))
                act.wait_ge(*Sa.at("abs", l))
                A(at2["ff"][0:8, 0], at2["ff"][0:8, 0], ACT.Exp, scale=-1.0).then_inc(*Sa.up("exp", l))
                act.wait_ge(*Sa.at("exp", l))
                A(at2["ff"][0:8, 0], at2["ff"][0:8, 0], ACT.Ln, bias=1.0).then_inc(*Sa.up("log", l))
                for i in range(2):
                    A(at2["ob"][:, 2 * i:2 * i + 2], bank((0, 1)[i]).rearrange("p (j t) -> p j t", j=2), ACT.Silu
                      ).then_inc(*Sa.up("gate_b", l, i))
                attention2(l, 1)
                for b in range(3):
                    for i in range(4):
                        act.wait_ge(*consumed(("in", l, "merge", b, i // 2)))
                        if b or i >= 2:
                            x = 4 * b + i - 2
                            act.wait_ge(*Sv.at("weighed", l, x // 4, x % 4))
                        A(at2["sg"][:, i % 2], bank(4 + i), ACT.Sigmoid).then_inc(*Sa.up("merge", l, b, i))

            def attention2(l, br):
                Sa, Sp, Sv = S("att_act"), S("att_pe"), S("att_dve")
                st = at2["stat"]
                for u in range(9):
                    if u < 8:
                        act.wait_ge(*Sv.at("max", 1, l, br, u))
                        if u >= 2:
                            act.wait_ge(*Sp.at("turned", 1, l, br, u - 2))
                        for a in range(TT):
                            o, n = (0, P) if a == 0 else (P, 2 * P)
                            A(at2["prob"][:, u % 2, o:o + n], at2["score"][:, u % 2, o:o + n], ACT.Exp,
                              bias=st[:, 4 * (u % 2) + a:4 * (u % 2) + a + 1],
                              accum_out=st[:, 8 + 4 * (u % 2) + a:9 + 4 * (u % 2) + a]).then_inc(*Sa.up("exp", 1, l, br, u, a))
                    if u >= 1:
                        v = u - 1
                        act.wait_ge(*Sp.at("turned", 1, l, br, v))
                        if v >= 2:
                            act.wait_ge(*Sp.at("value", 1, l, br, v - 2))
                        A(at2["prob_t"][:, v % 2], bank(5 + v % 2, 384), ACT.Copy).then_inc(*Sa.up("prob_t", 1, l, br, v))

            modulation(0)
            if upto >= 1:
                turned("ctx", m0["uc"], lambda k: modcol[:, 1, k, 1:2], lambda k: modcol[:, 0, k, 1:2])
                turned("mix0", m0["ut"], lambda k: modcol[:, 1, k, 0:1], lambda k: modcol[:, 0, k, 0:1])
                for u in range(4):
                    norm(("first", u), consumed(("mix_in", u // 2)), bank((0, 1, 3, 4)[u]), P, 512, 64, m0)
            if upto >= 2:
                attention0()
                for g in range(4):
                    act.wait_ge(*S("pool_pe").at("mean", g))
                    if g >= 0:
                        A(m0["pooled"][:, g], bank(4 + g % 2, T), ACT.Copy).then_inc(*S("pool_act").up("mean", g))
                post_norm(0, 0)
            if upto >= 3:
                turned("ffn0", ff["ut"], lambda k: modcol[:, 3, k, 0:1], lambda k: modcol[:, 2, k, 0:1])
                ffn(0)
                post_norm(0, 1)
            if upto >= 4:
                modulation(1)
            if upto >= 5:
                turned("mix1", m1["ut"], lambda k: modcol[:, 1, k, 0:1], lambda k: modcol[:, 0, k, 0:1])
                for j in range(8):
                    act.wait_ge(*consumed(("conv_in", 2 + j // 4)))
                    A(m1["c"][:, j], bank(j % 4 // 2)[:, j % 2 * T:j % 2 * T + T], ACT.Copy
                      ).then_inc(*S("conv_act").up("c", j))
                post_norm(1, 0)
            if upto >= 6:
                turned("ffn1", ff["ut"], lambda k: modcol[:, 3, k, 0:1], lambda k: modcol[:, 2, k, 0:1])
                ffn(1)
                post_norm(1, 1)
            if upto >= 7:
                second(0)
            if upto >= 8:
                second(1)

        @block.tensor
        def _(pe):
            M = nc.tensor.matmul

            def modulation(l):
                Sp, Sa, Sv = S("mod_pe"), S("mod_act"), S("mod_dve")
                if l == 0:
                    pe.wait_ge(*Sv.at("cond"))
                    pe.wait_ge(*loaded("tables"))
                else:
                    pe.wait_ge(*S("post_dve").at("t", 0, 1, 1))
                condT = md["condT"]

                def fold(j):
                    m, half = j // 2, j % 2
                    pe.wait_ge(*Sa.at("part", l, j))
                    if m in (2, 5):
                        if m == 5:
                            pe.wait_ge(*Sv.at("gate", l, j - 6))
                        mm = M(bank(2 + half), T1("sum_row0"), md["part"][:, half], start=True, stop=True)
                    else:
                        c = (m if m < 2 else m - 1)
                        for i in range(4):
                            o = (c * KD + half * 4 + i) * 2
                            mm = M(ps_t[:, 4 * HALF + o:4 * HALF + o + 2], md["part"][:, half, i * P:(i + 1) * P],
                                   T1("sum_cols"), start=True, stop=True)
                    mm.then_inc(*Sp.up("fold", l, j))

                for j in range(12):
                    key = ("mod", l, j)
                    pe.wait_ge(*has_landed(key))
                    if j >= 2:
                        pe.wait_ge(*Sa.at("part", l, j - 2))
                    for k in range(KD):
                        o = k % 4 * 32
                        mm = M(bank(j % 2)[o:o + 32], condT[:, k], slot(key)[:, k], start=k < 4, stop=k >= 4,
                               tile_position=(0, o))
                    mm.then_inc(used, 1)
                    if j >= 1:
                        fold(j - 1)
                fold(11)

            def turn(name, src, ready):
                pe.wait_ge(*ready)
                for pair in range(4):
                    for i in range(2):
                        for a in range(TT):
                            k = 2 * pair + i
                            mm = nc.tensor.transpose(bank(4 + pair)[:, i * T + a * P:i * T + a * P + P],
                                                     src[:, a, k * P:(k + 1) * P], T1("ident"))
                    mm.then_inc(*S("turn_pe").up(name, pair))

            def turned(name):
                pe.wait_ge(*S("turn_act").at(name, 5))
                pe.wait_ge(*S("turn_dve").at(name, 7))

            def project(dst, lhs, rhs, n=KD):
                for k in range(n):
                    mm = M(dst, lhs(k), rhs(k), start=k == 0, stop=k == n - 1)
                return mm

            def norm_sum(u, rows, n, bufs, weights="head_ones"):
                pe.wait_ge(*S("norm_act").at("sq", u))
                if u[-1] > 0:
                    pe.wait_ge(*S("norm_act").at("sd", u[:-1] + (u[-1] - 1,)))
                M(bank(2)[0:rows, 0:n], T1(weights)[0:rows, 0:rows], bufs["sq"][0:rows, 0:n], start=True, stop=True
                  ).then_inc(*S("norm_pe").up("sum", u))

            def norm_swap(u, last, rows, n, swap, bufs):
                pe.wait_ge(*S("norm_dve").at("xn", u))
                if last is not None:
                    pe.wait_ge(*S("norm_dve").at("t2", last))
                M(bank(7)[0:rows, 0:n], swap, bufs["xn"][0:rows, 0:n], start=True, stop=True
                  ).then_inc(*S("norm_pe").up("swap", u))

            def mixer0():
                ut, uc = m0["ut"], m0["uc"]
                pe.wait_ge(*S("mod_dve").at("columns", 0))
                pe.wait_ge(*loaded("ctx"))
                turn("ctx", m0["xc"], loaded("x"))
                turned("ctx")
                turn("mix0", h, loaded("x"))
                turned("mix0")
                key = ("mix_in", 0)
                pe.wait_ge(*has_landed(key))
                for j in range(4):
                    mm = project(bank(j // 2)[:, j % 2 * T:j % 2 * T + T], lambda k: slot(key)[:, k, j * P:(j + 1) * P],
                                 lambda k: ut[:, k])
                mm.then_inc(used, 1)
                key = ("mix_in", 1)
                pe.wait_ge(*has_landed(key))
                wkv = slot(key)
                for kv in range(2):
                    for o in (0, 64):
                        for i, u in enumerate((uc, ut)):
                            project(bank(3 + kv)[o:o + 64, i * T:(i + 1) * T], lambda k: wkv[:, k, 64 * kv:64 * kv + 64],
                                    lambda k: u[:, k])
                for a in range(4):
                    u = uc if a < 2 else ut
                    mm = project(bank(5)[:, a * P:(a + 1) * P], lambda k: u[:, k, a % 2 * P:a % 2 * P + P],
                                 lambda k: wkv[:, k, P:2 * P])
                mm.then_inc(used, 1)
                key = ("mix_in", 2)
                pe.wait_ge(*has_landed(key))
                for a in range(TT):
                    if a == 1:
                        pe.wait_ge(*S("turn_dve").at("values"))
                    mm = project(bank(6 - a), lambda k: ut[:, k, a * P:(a + 1) * P], lambda k: slot(key)[:, k])
                mm.then_inc(used, 1)
                pe.wait_ge(*loaded("tables_first"))
                for u in range(5):
                    if u < 4:
                        norm_sum(("first", u), P, 512, m0)
                    if u >= 1:
                        v = ("first", u - 1)
                        n = T if u >= 3 else 512
                        norm_swap(v, ("first", u - 2) if u > 1 else None, P, n, T2("swap"), m0)

            def attention0():
                Sa, Sp, Sv = S("att_act"), S("att_pe"), S("att_dve")
                pe.wait_ge(*S("norm_dve").at("out", ("first", 3)))
                pe.wait_ge(*S("turn_dve").at("pool_in", 1))
                for u in range(18):
                    if u < 16:
                        hd, a = u // 2, u % 2
                        o = 64 * (hd % 2)
                        if u >= 2:
                            pe.wait_ge(*Sa.at("exp", 0, u - 2))
                        M(bank(4 + u % 2), m0["q"][o:o + 64, hd // 2, a * P:(a + 1) * P], m0["k"][o:o + 64, hd // 4],
                          start=True, stop=True).then_inc(*Sp.up("score", 0, u))
                    if 1 <= u <= 16:
                        v = u - 1
                        pe.wait_ge(*Sv.at("prob", 0, v))
                        if v >= 1:
                            pe.wait_ge(*Sa.at("prob_t", 0, v - 1))
                        for i in range(4):
                            mm = nc.tensor.transpose(bank(6)[:, i * P:(i + 1) * P], m0["prob"][:, v % 2, i * P:(i + 1) * P],
                                                     T1("ident"))
                        mm.then_inc(*Sp.up("turned", 0, v))
                    if u >= 2:
                        v = u - 2
                        hd = v // 2
                        pe.wait_ge(*Sa.at("prob_t", 0, v))
                        if v >= 2:
                            pe.wait_ge(*Sv.at("value", 0, v - 2))
                        o = 64 * (hd % 2)
                        for i in range(4):
                            mm = M(bank((7, 3)[v % 2])[o:o + 64, 0:P], m0["v"][:, i, 64 * (hd // 4):64 * (hd // 4) + 64],
                                   m0["prob_t"][:, v % 2, i * P:(i + 1) * P], start=i == 0, stop=i == 3)
                        mm.then_inc(*Sp.up("value", 0, v))

            def pool0():
                Sp = S("pool_pe")
                band = T2("band").rearrange("p (a g t) -> p a g t", a=TT, g=4)
                pe.wait_ge(*loaded("small"))
                wg = small_t[:, 0:512].rearrange("p (g d) -> p g d", g=4)

                def weights(g):
                    pe.wait_ge(*S("pool_act").at("mean", g))
                    if g >= 1:
                        pe.wait_ge(*S("pool_dve").at("out", g - 1))
                    M(bank(6, T), wg[:, g], m0["pooled"][:, g], start=True, stop=True).then_inc(*Sp.up("out", g))

                for g in range(4):
                    if g >= 2:
                        pe.wait_ge(*S("pool_act").at("mean", g - 2))
                    for a in range(TT):
                        mm = M(bank(4 + g % 2, T), m0["pt"][:, a, g * P:(g + 1) * P], band[:, a, g],
                               start=a == 0, stop=a == 1)
                    mm.then_inc(*Sp.up("mean", g))
                    if g >= 1:
                        weights(g - 1)
                weights(3)

            def mix_out(l, mix, *ready):
                for r in ready:
                    pe.wait_ge(*r)
                for j in range(2):
                    key = ("mix_out", l, j)
                    pe.wait_ge(*has_landed(key))
                    for a in range(TT):
                        mm = project(bank(2 * a + j), lambda k: mix[:, k, a * P:(a + 1) * P], lambda k: slot(key)[:, k])
                    mm.then_inc(used, 1)

            def mixer1():
                ut = m1["ut"]
                pe.wait_ge(*S("mod_dve").at("columns", 1))
                turn("mix1", h, S("post_dve").at("h", 0, 1, 1))
                turned("mix1")
                for n, j in enumerate((2, 4, 3, 5, 0, 1)):
                    key = ("conv_in", j)
                    pe.wait_ge(*has_landed(key))
                    if n == 2:
                        pe.wait_ge(*S("conv_act").at("c", 3))
                    if n == 3:
                        pe.wait_ge(*S("conv_dve").at("z", 3))
                    if n == 4:
                        pe.wait_ge(*S("conv_act").at("c", 7))
                    if n == 5:
                        pe.wait_ge(*S("conv_dve").at("z", 7))
                    b0 = (0, 2, 0, 2, 0, 2)[n]
                    for i in range(4):
                        mm = project(bank(b0 + i // 2)[:, i % 2 * T:i % 2 * T + T],
                                     lambda k: slot(key)[:, k, i * P:(i + 1) * P], lambda k: ut[:, k])
                    mm.then_inc(used, 1)

            def ffn(l):
                Sa, Sp, Sv = S("ffn_act"), S("ffn_pe"), S("ffn_dve")
                pe.wait_ge(*loaded("router", l + 1))
                router = small_t[:, 512:640].rearrange("p (k e) -> p k e", k=KD)
                turned(f"ffn{l}")
                for a in range(TT):
                    mm = project(bank(0)[:, a * E:(a + 1) * E], lambda k: ff["ut"][:, k, a * P:(a + 1) * P], lambda k: router[:, k])
                mm.then_inc(*Sp.up("logits", l))
                pe.wait_ge(*Sv.at("share", l, 1))
                for a in range(TT):
                    mm = nc.tensor.transpose(bank(1)[0:E, a * P:(a + 1) * P], ff["ex"][:, a], T1("ident"))
                mm.then_inc(*Sp.up("shares", l))
                pe.wait_ge(*Sv.at("spread", l))
                M(bank(0), T1("ones")[0:E], ff["di"][0:E], start=True, stop=True).then_inc(*Sp.up("rows", l))
                for g in range(NG):
                    M(ps_t[:, HALF + g:HALF + g + 1], ff["di"][0:E, g * EG:(g + 1) * EG], T1("ones")[0:E, 0:1],
                      start=True, stop=True)
                pe.wait_ge(*Sv.at("spread_gates", l))
                for g in range(NG):
                    mm = M(ps_t[:, HALF + 4 + g:HALF + 5 + g], ff["dg"][0:E, g * EG:(g + 1) * EG], T1("ones")[0:E, 0:1],
                           start=True, stop=True)
                mm.then_inc(*Sp.up("cols", l))
                pe.wait_ge(*Sv.at("pick", l, 1))
                for k in range(KD):
                    if k >= 4:
                        pe.wait_ge(*(Sa if k % 2 == 0 else Sv).at("xe", l, k - 4))
                    for a in range(TT):
                        mm = M(bank(4 + k % 4), h[:, a, k * P:(k + 1) * P], ff["pick"][:, a], start=a == 0, stop=a == 1)
                    mm.then_inc(*Sp.up("gather", l, k))
                pe.wait_ge(*Sa.at("xe", l, 6))
                pe.wait_ge(*Sv.at("xe", l, 7))
                pe.wait_ge(*Sv.at("cols", l))
                pe.wait_ge(*Sv.at("pick", l, 1))
                Sx, Sax, Svx, Spl = (S(f"expert{l}_{e}") for e in ("pe", "act", "dve", "pool"))
                base = number[("expert", l, 0)]

                def streamed(g, m, k):
                    i = base + m * KD + k
                    pe.wait_ge(landed[i % RING], g * (16 * 3 * KD // RING) + 16 * (i // RING + 1))
                    return ring[:, i % RING * SLOT:i % RING * SLOT + EG * D].rearrange("p (e f) -> p e f", e=EG)

                def products(b, x, k, wk):
                    for half in range(2):
                        for e in range(EG):
                            mm = M(bank(b + half)[32 * e:32 * e + 32], x[:, k, 32 * e:32 * e + 32],
                                   wk[:, e, half * HALF:(half + 1) * HALF], start=k == 0, stop=k == KD - 1,
                                   tile_position=(0, 32 * e))
                    return mm

                Sx.open_loop()
                with pe.Fori(0, NG) as g:
                    pe.wait_ge(*Spl.turn(g, "xg"))
                    for m in range(2):
                        for k in range(KD):
                            mm = products(2 * m, ff["xg"], k, streamed(g, m, k))
                            mm.then_inc(used, 1)
                    for b in range(2):
                        pe.wait_ge(*Svx.turn(g, "hidden", b))
                        for i in range(4):
                            k = 4 * b + i
                            mm = nc.tensor.transpose(bank(6 + b)[:, i * P:(i + 1) * P], ff["hg"][:, k * P:(k + 1) * P],
                                                     T1("ident"))
                        mm.then_inc(*Sx.up("turned", b))
                    for k in range(KD):
                        if k % 4 == 0:
                            pe.wait_ge(*Sax.turn(g, "ht", k // 4))
                        mm = products(4, ff["ht"], k, streamed(g, 2, k))
                        mm.then_inc(used, 1)
                Sx.close_loop(NG)
                pe.wait_ge(*Svx.turn(NG - 1, "ye"))
                for a in range(TT):
                    for half in range(2):
                        for g in range(NG):
                            mm = M(bank(2 * a + half), ff["put"][:, g, a * P:(a + 1) * P],
                                   ff["ye"][:, g, half * HALF:(half + 1) * HALF], start=g == 0, stop=g == NG - 1)
                    mm.then_inc(*Sp.up("y", l, a))

            def second(l):
                Sa, Sp, Sv, So = S("second_act"), S("second_pe"), S("second_dve"), S("second_pool")
                ht = s2["ht"]
                if l == 0:
                    pe.wait_ge(*S("post_dve").at("t", 1, 1, 1))
                turn(f"sec{l}", xn_tok, Sv.at("normed", l, 1))
                turned(f"sec{l}")

                def tiles(key, banks, lhs0=0, n=4):
                    for i in range(n):
                        mm = project(bank(banks[i // 2])[:, i % 2 * T:i % 2 * T + T],
                                     lambda k: slot(key)[:, k, lhs0 + i * P:lhs0 + (i + 1) * P], lambda k: ht[:, k])
                    return mm

                for n in range(3):
                    key = ("in", l, "rkv", n)
                    pe.wait_ge(*has_landed(key))
                    tiles(key, (2 * n, 2 * n + 1)).then_inc(used, 1)
                key = ("in", l, "lora")
                pe.wait_ge(*has_landed(key))
                tiles(key, (6,), n=1).then_inc(used, 1)
                key = ("in", l, "gate_c")
                pe.wait_ge(*has_landed(key))
                pe.wait_ge(*Sa.at("raw", l, 0))
                tiles(key, (0, 1)).then_inc(used, 1)
                pe.wait_ge(*loaded("small2", 3 * l + 3))
                lora = small_t[:, 0:512]
                if l:
                    pe.wait_ge(*Sv.at("mixed", 1, 2))
                    pe.wait_ge(*Sa.at("raw", 1, 2))
                    vdw = small_t[:, 512:640].rearrange("p (k n) -> p k n", k=4)
                    project(bank(2, T)[0:32], lambda k: vdw[:, k], lambda k: s2["rkv"][:, 2, k], 4).then_inc(*Sp.up("v_down"))
                    pe.wait_ge(*Sa.at("v_down"))
                    for j in range(4):
                        mm = M(bank(4 + j // 2)[:, j % 2 * T:j % 2 * T + T], small_t[0:32, 640 + j * P:640 + (j + 1) * P],
                               s2["vd"][0:32], start=True, stop=True)
                    mm.then_inc(*Sp.up("v_up"))
                for p in range(2):
                    recurrence(l, p, lora)
                attention_parts(l, tiles)

            def recurrence(l, p, lora):
                Sa, Sp, Sv, So = S("rwkv_act"), S("rwkv_pe"), S("rwkv_dve"), S("rwkv_pool")
                K = (l, p)
                pairs = [(tt, jj) for tt in range(2) for jj in range(2)]
                pe.wait_ge(*S("second_act").at("tanh", l))
                pe.wait_ge(*S("second_act").at("gate_c", l, 1))
                if l:
                    pe.wait_ge(*S("second_act").at("nu", 3))
                if p:
                    pe.wait_ge(*Sv.at("o", l, 0))
                for o, b in ((0, 0), (64, 1)):
                    for jj in range(2):
                        mm = M(bank(b)[:, jj * T:jj * T + T], lora[o:o + 64, (2 * p + jj) * P:(2 * p + jj + 1) * P],
                               s2["wal"][o:o + 64], start=True, stop=True)
                mm.then_inc(*Sp.up("lora", *K))
                pe.wait_ge(*Sa.at("kk_sq", *K))
                M(bank(2), T1("head_ones"), rw["tmp"], start=True, stop=True).then_inc(*Sp.up("kk_sum", *K))
                pe.wait_ge(*Sv.at("rk", *K, 1))
                pe.wait_ge(*Sa.at("kk_root", *K))
                M(bank(3), T1("head_ones"), rw["tmp"], start=True, stop=True).then_inc(*Sp.up("rk_sum", *K))
                src = (lambda tt, jj: s2["rkv"][:, 2, 2 * p + jj, tt * P:(tt + 1) * P],
                       lambda tt, jj: rw["bh"][:, jj, tt * P:(tt + 1) * P],
                       lambda tt, jj: rw["kh"][:, jj, tt * P:(tt + 1) * P],
                       lambda tt, jj: rw["kr"][:, jj, tt, 0])
                if l:
                    pe.wait_ge(*S("second_dve").at("blend", 1))
                pe.wait_ge(*So.at("hats", *K, 1))
                pe.wait_ge(*Sv.at("bt", *K))
                for i in range(4):
                    for r, (tt, jj) in enumerate(pairs):
                        mm = nc.tensor.transpose(bank(4 + i)[:, r * P:(r + 1) * P], src[i](tt, jj), T1("ident"))
                    mm.then_inc(*Sp.up("tok", *K, i))
                pe.wait_ge(*Sv.at("kt", *K))
                pe.wait_ge(*Sa.at("a", *K, 1))
                pe.wait_ge(*Sv.at("bonus", *K))
                for n, x, b in (("gram_b", "bt", 0), ("gram_k", "kt", 4)):
                    if b:
                        pe.wait_ge(*Sa.at("tok", *K, 3, 1))
                    for r, (tt, jj) in enumerate(pairs):
                        for hh in range(2):
                            o = 64 * hh
                            mm = M(bank(b + 2 * hh + r // 2)[:, r % 2 * 256:r % 2 * 256 + 256],
                                   rw[x][o:o + 64, jj, tt * P:(tt + 1) * P],
                                   rw["kr"][o:o + 64, jj, tt].rearrange("p x n -> p (x n)"), start=True, stop=True)
                    mm.then_inc(*Sp.up(n, *K))
                pe.wait_ge(*Sv.at("gb", *K, 1))
                for r, (tt, jj) in enumerate(pairs):
                    for hh in range(2):
                        o = 64 * hh
                        mm = M(bank(hh)[:, r * P:(r + 1) * P], rw["kr"][o:o + 64, jj, tt, 0], rw["bt"][o:o + 64, jj, tt * P:(tt + 1) * P],
                               start=True, stop=True)
                mm.then_inc(*Sp.up("gram_a", *K))
                inv, inv_t, prod = rw["inv"], rw["inv_t"], rw["prod"]
                for n in range(1, LEVELS):
                    pe.wait_ge(*So.at("level", *K, n))
                    for hh in range(2):
                        pe.wait_ge(*Sv.at("inv", *K, n - 1, hh))
                        for q in range(4 * hh, 4 * hh + 4):
                            mm = M(bank(2 + hh)[:, q % 4 * P:q % 4 * P + P], rw[f"lev{n % 2}"][:, q], inv[:, q],
                                   start=True, stop=True)
                        mm.then_inc(*Sp.up("step", *K, n, hh))
                    for hh in range(2):
                        pe.wait_ge(*Sa.at("step", *K, n, hh))
                        pe.wait_ge(*Sv.at("inv_t", *K, n - 1, hh))
                        if n < LEVELS - 1:
                            for q in range(4 * hh, 4 * hh + 4):
                                mm = M(bank(4 + hh)[:, q % 4 * P:q % 4 * P + P], inv_t[:, q], prod[:, q], start=True, stop=True)
                            mm.then_inc(*Sp.up("inv", *K, n, hh))
                        for q in range(4 * hh, 4 * hh + 4):
                            mm = M(bank(6 + hh)[:, q % 4 * P:q % 4 * P + P], prod[:, q], inv_t[:, q], start=True, stop=True)
                        mm.then_inc(*Sp.up("inv_t", *K, n, hh))
                vt, bht, kht, gh, wk = rw["v_tok"], rw["bh_tok"], rw["kh_tok"], rw["prod"], rw["wk"]
                pe.wait_ge(*Sv.at("gk", *K, 1))
                for q in range(8):
                    mm = M(bank(0)[:, q * 64:q * 64 + 64], rw["gk"][:, q, 0:P], vt[:, q], start=True, stop=True)
                mm.then_inc(*Sp.up("w1", *K))
                pe.wait_ge(*Sa.at("w1", *K))
                for hh in range(2):
                    pe.wait_ge(*Sv.at("inv_t", *K, LEVELS - 1, hh))
                    for q in range(4 * hh, 4 * hh + 4):
                        mm = M(bank(2 + hh)[:, q % 4 * P:q % 4 * P + P], inv_t[:, q], wk[:, q], start=True, stop=True)
                    mm.then_inc(*Sp.up("gh", *K, hh))
                pe.wait_ge(*Sv.at("gh", *K, 1))
                for r, (tt, jj) in enumerate(pairs):
                    for hh in range(2):
                        q, o, c = 4 * hh + r, 64 * hh, jj * T + tt * P
                        M(bank(4)[o:o + 64, c:c + P], gh[:, q, 0:64], rw["gb"][:, q, P:2 * P], start=True, stop=False)
                        M(bank(4)[o:o + 64, c:c + P], vt[:, q], rw["gk"][:, q, P:2 * P], start=False, stop=True)
                        mm = M(bank(5)[o:o + 64, c:c + P], gh[:, q, 64:P], rw["gb"][:, q, P:2 * P], start=True, stop=True)
                mm.then_inc(*Sp.up("y0", *K))
                for c in (1, 3, 2):
                    tt, o = c // 2, 64 * (c % 2)
                    for jj in range(2):
                        for hh in range(2):
                            q, oo = 4 * hh + 2 * tt + jj, 64 * hh
                            x = (c // 2 * 2 + jj) * 64 if c % 2 else jj * 64
                            mm = M(bank(6 if c % 2 else 7)[oo:oo + 64, x:x + 64], gh[o:o + 64, q, 64:P], bht[o:o + 64, q],
                                   start=True, stop=True)
                mm.then_inc(*Sp.up("pm", *K))
                for c in (0, 2, 1):
                    tt, o = c // 2, 64 * (c % 2)
                    for jj in range(2):
                        for hh in range(2):
                            q, oo = 4 * hh + 2 * tt + jj, 64 * hh
                            x = jj * 64 if c % 2 else (c // 2 * 2 + jj) * 64
                            b = bank(1 if c % 2 else 0)[oo:oo + 64, x:x + 64]
                            M(b, bht[o:o + 64, q], gh[o:o + 64, q, 0:64], start=True, stop=False)
                            mm = M(b, kht[o:o + 64, q], vt[o:o + 64, q], start=False, stop=True)
                mm.then_inc(*Sp.up("carried", *K))
                st = rw["state"]
                pe.wait_ge(*Sv.at("z", *K))
                pe.wait_ge(*Sa.at("pm", *K, 1))
                pe.wait_ge(*Sa.at("carried", *K, 1))
                for c in range(1, 4):
                    pe.wait_ge(*Sv.at("state", *K, c))
                    if c < 3:
                        for jj in range(2):
                            for hh in range(2):
                                o = 64 * hh
                                mm = M(bank(6 + hh)[o:o + 64, jj * 64:jj * 64 + 64], rw["pm"][o:o + 64, c, jj],
                                       st[o:o + 64, c, jj], start=True, stop=True)
                        mm.then_inc(*Sp.up("move", *K, c))
                    for jj in range(2):
                        for hh in range(2):
                            o = 64 * hh
                            x = jj * T + c * CH
                            mm = M(bank(2 + hh)[o:o + 64, x:x + CH], st[o:o + 64, c, jj], rw["z"][o:o + 64, jj, c * CH:(c + 1) * CH],
                                   start=True, stop=True)
                mm.then_inc(*Sp.up("read", *K))
                pe.wait_ge(*Sv.at("y", *K))
                M(bank(4), T1("head_ones"), rw["y"].rearrange("p j t -> p (j t)"), start=True, stop=True
                  ).then_inc(*Sp.up("gn_mean", *K))
                pe.wait_ge(*Sa.at("gn_sq", *K))
                M(bank(5), T1("head_ones"), rw["tmp2"], start=True, stop=True).then_inc(*Sp.up("gn_sum", *K))

            def attention_parts(l, tiles):
                Sa, Sp, Sv = S("second_act"), S("second_pe"), S("second_dve")
                Nd = S("norm_dve")
                ht = s2["ht"]
                pe.wait_ge(*S("rwkv_dve").at("o", l, 1))

                def norm2(i):
                    u = ("sec", l, i)
                    r0, r1, n, _, _, ones = unit(l, i)
                    pe.wait_ge(*S("norm_act").at("sq", u))
                    if before(u):
                        pe.wait_ge(*S("norm_act").at("sd", before(u)))
                    wt = T1(ones)[r0:r1, 0:r1 - r0]
                    if i == 0:
                        M(bank(2, T), wt, at2["sq"][:, 0:T], start=True, stop=False)
                        mm = M(bank(2, T), wt, at2["sq"][:, T:2 * T], start=False, stop=True)
                    else:
                        mm = M(bank(2, n)[r0:r1], wt, at2["sq"][r0:r1, 0:n], start=True, stop=True)
                    mm.then_inc(*S("norm_pe").up("sum", u))

                def swap2(i):
                    u = ("sec", l, i)
                    r0, r1, n = unit(l, i)[:3]
                    pe.wait_ge(*Nd.at("xn", u))
                    if i > 2:
                        pe.wait_ge(*Nd.at("t2", ("sec", l, i - 1)))
                    M(bank(7, n)[r0:r1], T2("swap", second_at)[r0:r1, r0:r1], at2["xn"][r0:r1, 0:n], start=True, stop=True
                      ).then_inc(*S("norm_pe").up("swap", u))

                key = ("in", l, "latent")
                pe.wait_ge(*has_landed(key))
                tiles(key, (0,), n=2)
                project(bank(1, T), lambda k: slot(key)[:, k, C_KV:K_R], lambda k: ht[:, k])
                project(bank(3, T)[64:96], lambda k: slot(key)[:, k, K_R:G_A], lambda k: ht[:, k]).then_inc(used, 1)
                for i in range(3):
                    norm2(i)
                swap2(2)
                key = ("uq", l)
                pe.wait_ge(*has_landed(key))
                pe.wait_ge(*Nd.at("out", ("sec", l, 0)))
                for hd in range(H2):
                    mm = project(bank((4, 5, 6, 0)[hd // 2])[0:96, hd % 2 * T:hd % 2 * T + T],
                                 lambda k: slot(key)[:, k, hd * 96:(hd + 1) * 96], lambda k: at2["cq"][:, k], 2)
                mm.then_inc(used, 1)
                norm2(3)
                for i in range(4, 7):
                    norm2(i)
                    swap2(i - 1)
                swap2(6)
                key = ("ukv", l)
                pe.wait_ge(*has_landed(key))
                pe.wait_ge(*Nd.at("out", ("sec", l, 6)))
                wk = slot(key)[:, 0].rearrange("p (h n) -> p h n", h=H2)
                for hd in range(H2):
                    M(bank((1, 3, 4, 5)[hd // 2])[0:64, hd % 2 * T:hd % 2 * T + T], wk[:, hd, 0:64], at2["ckv"], start=True, stop=True)
                for a in range(TT):
                    mm = M(bank((6, 0)[a]), at2["ckv"][:, a * P:(a + 1) * P], wk[:, :, 64:P], start=True, stop=True)
                mm.then_inc(used, 1)
                for i in range(7, 11):
                    norm2(i)
                key = ("in", l, "gate_a")
                pe.wait_ge(*has_landed(key))
                pe.wait_ge(*Nd.at("out", ("sec", l, 10)))
                tiles(key, (3, 4)).then_inc(used, 1)
                pe.wait_ge(*Sv.at("values", l, 0, 1))
                pe.wait_ge(*Sa.at("gate_a", l, 1))
                attention2(l, 0)
                pe.wait_ge(*S("att_dve").at("value", 1, l, 0, 7))
                for n, key in enumerate((("in", l, "fq"), ("in", l, "fk"))):
                    pe.wait_ge(*has_landed(key))
                    tiles(key, ((0, 1), (3, 4))[n]).then_inc(used, 1)
                key = ("in", l, "fv")
                pe.wait_ge(*has_landed(key))
                for a in range(TT):
                    mm = project(bank(5 + a), lambda k: ht[:, k, a * P:(a + 1) * P], lambda k: slot(key)[:, k])
                mm.then_inc(used, 1)
                for i in range(11, 15):
                    norm2(i)
                key = ("in", l, "ff_gate_b")
                pe.wait_ge(*has_landed(key))
                pe.wait_ge(*Nd.at("out", ("sec", l, 14)))
                project(bank(7, T)[0:8], lambda k: slot(key)[:, k, 0:8], lambda k: ht[:, k])
                tiles(key, (0, 1), lhs0=8).then_inc(used, 1)
                pe.wait_ge(*Sv.at("ncum", l))
                pe.wait_ge(*Sv.at("values", l, 1, 1))
                pe.wait_ge(*Sa.at("gate_b", l, 1))
                attention2(l, 1)
                outs = (at2["oa"], at2["ob"], s2["oc"])
                pe.wait_ge(*S("att_dve").at("value", 1, l, 1, 7))
                for b in range(3):
                    key = ("proj", l, b)
                    pe.wait_ge(*has_landed(key))
                    if b:
                        pe.wait_ge(*Sv.at("weighed", l, b - 1, 3))
                    for i in range(KD):
                        mm = project(bank(i // 2)[:, i % 2 * T:i % 2 * T + T], lambda k: slot(key)[:, k, i * P:(i + 1) * P],
                                     lambda k: outs[b][:, k], 4)
                    mm.then_inc(used, 1)
                    for j in range(2):
                        key = ("in", l, "merge", b, j)
                        pe.wait_ge(*has_landed(key))
                        if b:
                            pe.wait_ge(*Sa.at("merge", l, b - 1, 2 * j + 1))
                        tiles(key, (4 + 2 * j, 5 + 2 * j)).then_inc(used, 1)
                pe.wait_ge(*Sv.at("merged", l, 2, 3))
                for j in range(2):
                    key = ("out", l, j)
                    pe.wait_ge(*has_landed(key))
                    for a in range(TT):
                        mm = project(bank(2 * a + j), lambda k: merged[:, k, a * P:(a + 1) * P], lambda k: slot(key)[:, k])
                    mm.then_inc(used, 1)

            def attention2(l, br):
                Sa, Sp, Sv = S("att_act"), S("att_pe"), S("att_dve")
                for u in range(10):
                    if u < 8:
                        if u >= 2:
                            pe.wait_ge(*Sv.at("score", 1, l, br, u - 2))
                        if br == 0:
                            rows, j = slice(0, 96), u
                        else:
                            rows, j = slice(64 * (u % 2), 64 * (u % 2) + 64), u // 2
                        for a in range(TT):
                            n = (a + 1) * P
                            dst = bank(u % 2)[:, a * P:a * P + n]
                            mm = M(dst, at2["q"][rows, j, a * P:(a + 1) * P], at2["k"][rows, j, 0:n], start=True, stop=br == 0)
                            if br:
                                sel = T1("ident")[:, u:u + 1]
                                M(dst, at2["cum"][:, a * P:(a + 1) * P], sel.to_broadcast([P, n]), start=False, stop=False)
                                mm = M(dst, sel.to_broadcast([P, P]), at2["ncum"][:, 0:n], start=False, stop=True)
                        mm.then_inc(*Sp.up("score", 1, l, br, u))
                    if 1 <= u <= 8:
                        v = u - 1
                        pe.wait_ge(*Sv.at("prob", 1, l, br, v, 1))
                        if v >= 2:
                            pe.wait_ge(*Sa.at("prob_t", 1, l, br, v - 2))
                        for i in range(3):
                            mm = nc.tensor.transpose(bank(5 + v % 2)[:, i * P:(i + 1) * P], at2["prob"][:, v % 2, i * P:(i + 1) * P],
                                                     T1("ident"))
                        mm.then_inc(*Sp.up("turned", 1, l, br, v))
                    if u >= 2:
                        v = u - 2
                        o = 64 * (v % 2)
                        pe.wait_ge(*Sa.at("prob_t", 1, l, br, v))
                        if v >= 2:
                            pe.wait_ge(*Sv.at("value", 1, l, br, v - 2))
                        dst, pt = bank(3 + v % 2)[o:o + 64], at2["prob_t"][:, v % 2]
                        vals = lambda a: at2["v"][:, a, v * 64:v * 64 + 64]
                        M(dst[:, 0:P], vals(0), pt[:, 0:P], start=True, stop=True)
                        M(dst[:, P:2 * P], vals(0), pt[:, P:2 * P], start=True, stop=False)
                        M(dst[:, P:2 * P], vals(1), pt[:, 2 * P:3 * P], start=False, stop=True
                          ).then_inc(*Sp.up("value", 1, l, br, v))

            modulation(0)
            if upto >= 1:
                mixer0()
            if upto >= 2:
                attention0()
                pe.wait_ge(*S("att_dve").at("value", 0, 15))
                pool0()
                mix_out(0, m0["mix"], S("pool_dve").at("out", 3))
            if upto >= 3:
                turn("ffn0", h, S("post_dve").at("h", 0, 0, 1))
                ffn(0)
            if upto >= 4:
                modulation(1)
            if upto >= 5:
                mixer1()
                mix_out(1, m1["mix"], S("conv_dve").at("mix", 7))
            if upto >= 6:
                turn("ffn1", h, S("post_dve").at("h", 1, 0, 1))
                ffn(1)
            if upto >= 7:
                second(0)
            if upto >= 8:
                second(1)

        @block.vector
        def _(ve):
            V = nc.vector

            def modulation(l):
                Sv, Sp, Sa = S("mod_dve"), S("mod_pe"), S("mod_act")
                if l == 0:
                    V.memset(md["condT"], 0.0).then_inc(*Sv.up("zero"))
                    ve.wait_ge(*Sv.at("zero"))
                    ve.wait_ge(*Sa.at("sigmoid"))
                    o = par_at["cond"][0]
                    V.tensor_tensor(md["condT"][:, :, 0:2], par[:, o:o + 16].rearrange("p (c k) -> p k c", c=2),
                                    md["sig"].rearrange("p (c k) -> p k c", c=2), ALU.mult).then_inc(*Sv.up("cond"))
                ve.wait_ge(*loaded("gate_bias", 2 * l + 2))
                for j in (4, 5, 10, 11):
                    half, m = j % 2, j // 6
                    ve.wait_ge(*Sp.at("fold", l, j))
                    g = gate[:, m, half * HALF:(half + 1) * HALF]
                    V.tensor_tensor(g, bank(2 + half), g, ALU.add).then_inc(*Sv.up("gate", l, j))
                for m in range(4):
                    o = par_at[f"b_mod{l}{(0, 1, 3, 4)[m]}"][0]
                    V.scalar_tensor_tensor(out=modcol[:, m], in0=bank(4, 64).rearrange("p (m k c) -> p m k c", m=4, k=KD)[:, m],
                                           scalar=float(m % 2), in1=par[:, o:o + KD].unsqueeze(2).to_broadcast([P, KD, 2]),
                                           op0=ALU.add, op1=ALU.add).then_inc(*Sv.up("columns" if m == 3 else "column", l, *([m] if m < 3 else [])))

            def turned(name, dst, scale, bias):
                for pair in (1, 3):
                    ve.wait_ge(*S("turn_pe").at(name, pair))
                    for i in range(2):
                        k = 2 * pair + i
                        src = bank(4 + pair)[:, i * T:(i + 1) * T]
                        if bias is None:
                            V.tensor_scalar(dst[:, k], src, scale(k), None, ALU.mult).then_inc(*S("turn_dve").up(name, k))
                        else:
                            V.tensor_scalar(dst[:, k], src, scale(k), bias(k), ALU.mult, ALU.add
                                            ).then_inc(*S("turn_dve").up(name, k))

            def norm(u, x, rows, n, gain, dst, bufs, rope=None, last_swap=None):
                Sv, Sa, Sp = S("norm_dve"), S("norm_act"), S("norm_pe")
                ve.wait_ge(*Sa.at("sd", u))
                if u[-1] > 0:
                    ve.wait_ge(*Sv.at("out", u[:-1] + (u[-1] - 1,)))
                V.reciprocal(bufs["t1"][0:rows, 0:n], bufs["sd"][0:rows, 0:n]).then_inc(*Sv.up("rs", u))
                ve.wait_ge(*Sv.at("rs", u))
                o = rope[2] if rope else n
                if o:
                    V.scalar_tensor_tensor(out=dst[0:rows, 0:o], in0=x[0:rows, 0:o], scalar=gain, in1=bufs["t1"][0:rows, 0:o],
                                           op0=ALU.mult, op1=ALU.mult).then_inc(*Sv.up("out" if not rope else "plain", u))
                if not rope:
                    return
                if last_swap is not None:
                    ve.wait_ge(*Sp.at("swap", last_swap))
                m = n - o
                V.scalar_tensor_tensor(out=bufs["xn"][0:rows, 0:m], in0=x[0:rows, o:n], scalar=gain,
                                       in1=bufs["t1"][0:rows, o:n], op0=ALU.mult, op1=ALU.mult).then_inc(*Sv.up("xn", u))
                ve.wait_ge(*Sv.at("xn", u))
                tiles = m // T
                both = lambda ap: ap[0:rows].rearrange("p (j t) -> p j t", j=tiles)
                wide = lambda ap: ap[0:rows].unsqueeze(1).to_broadcast([rows, tiles, T])
                V.tensor_tensor(both(bufs["t1"][:, 0:m]), both(bufs["xn"][:, 0:m]), wide(rope[0]), ALU.mult
                                ).then_inc(*Sv.up("t1", u))
                ve.wait_ge(*Sp.at("swap", u))
                V.tensor_tensor(both(bufs["t2"][:, 0:m]), both(bank(7, m)), wide(rope[1]), ALU.mult
                                ).then_inc(*Sv.up("t2", u))
                ve.wait_ge(*Sv.at("t2", u))
                V.tensor_tensor(dst[0:rows, o:n], bufs["t1"][0:rows, 0:m], bufs["t2"][0:rows, 0:m], ALU.add
                                ).then_inc(*Sv.up("out", u))

            def mixer0():
                Sv = S("turn_dve")
                q2 = m0["q"].rearrange("p (u j) t -> p u (j t)", u=2)
                ve.wait_ge(*consumed(("mix_in", 1)))
                V.tensor_copy(m0["v"], bank(5).rearrange("p (a n) -> p a n", a=4)).then_inc(*Sv.up("values"))
                ve.wait_ge(*consumed(("mix_in", 2)))
                for a in range(TT):
                    V.tensor_copy(m0["pt"][:, a], bank(6 - a)).then_inc(*Sv.up("pool_in", a))
                ve.wait_ge(*loaded("tables_first"))
                for u in range(4):
                    norm(("first", u), bank((0, 1, 3, 4)[u]), P, 512, PC("q_g" if u < 2 else "k_g"),
                         q2[:, u] if u < 2 else m0["k"][:, u - 2], m0, (T2("cos"), T2("sin"), 0 if u < 2 else T),
                         ("first", u - 1) if u else None)

            def attention0():
                Sv, Sp, Sa = S("att_dve"), S("att_pe"), S("att_act")
                st = m0["stat"]
                for u in range(18):
                    if u < 16:
                        ve.wait_ge(*Sp.at("score", 0, u))
                        V.tensor_reduce(st[:, 16 + u:17 + u], bank(4 + u % 2), AX_X, ALU.max).then_inc(*Sv.up("row_max", 0, u))
                        ve.wait_ge(*Sv.at("row_max", 0, u))
                        V.tensor_scalar(st[:, u:u + 1], st[:, 16 + u:17 + u], -0.125, None, ALU.mult
                                        ).then_inc(*Sv.up("max", 0, u))
                    if 1 <= u <= 16:
                        v = u - 1
                        ve.wait_ge(*Sa.at("exp", 0, v))
                        V.reciprocal(st[:, 48 + v:49 + v], st[:, 32 + v:33 + v]).then_inc(*Sv.up("inverse", 0, v))
                        ve.wait_ge(*Sv.at("inverse", 0, v))
                        V.tensor_scalar(m0["prob"][:, v % 2], m0["prob"][:, v % 2], st[:, 48 + v:49 + v], None, ALU.mult
                                        ).then_inc(*Sv.up("prob", 0, v))
                    if u >= 2:
                        v = u - 2
                        hd, a = v // 2, v % 2
                        o = 64 * (hd % 2)
                        ve.wait_ge(*Sp.at("value", 0, v))
                        V.tensor_copy(m0["mix"][o:o + 64, hd // 2, a * P:(a + 1) * P], bank((7, 3)[v % 2])[o:o + 64, 0:P]
                                      ).then_inc(*Sv.up("value", 0, v))

            def pool0():
                for g in range(4):
                    ve.wait_ge(*S("pool_pe").at("out", g))
                    V.tensor_scalar(m0["mix"][:, 4 + g], bank(6, T), PC("pool_scale", g), None, ALU.mult
                                    ).then_inc(*S("pool_dve").up("out", g))

            def post_norm(l, part, ready):
                Sv = S("post_dve")
                ve.wait_ge(*loaded("ln", 2 * (2 * l + part) + 2))
                for a in range(TT):
                    k = (l, part, a)
                    t, st, mv, rs = pn["t"][:, a], pn["st"][:, a], pn["mv"][:, a], pn["rs"][:, a]
                    ve.wait_ge(*ready(a))
                    V.tensor_tensor(t, ps_t[:, 2 * a * HALF:(2 * a + 2) * HALF], gate[:, part], ALU.mult).then_inc(*Sv.up("t", *k))
                    ve.wait_ge(*Sv.at("t", *k))
                    V.scalar_tensor_tensor(out=t, in0=h[:, a], scalar=ALPHA, in1=t, op0=ALU.mult, op1=ALU.add
                                           ).then_inc(*Sv.up("sum", *k))
                    ve.wait_ge(*Sv.at("sum", *k))
                    for i in range(2):
                        V.bn_stats(st[:, 6 * i:6 * i + 6], t[:, i * HALF:(i + 1) * HALF]).then_inc(*Sv.up("stats", i, *k))
                    ve.wait_ge(*Sv.at("stats", 1, *k))
                    V.bn_aggr(mv, st).then_inc(*Sv.up("var", *k))
                    ve.wait_ge(*S("post_act").at("sd", *k))
                    V.reciprocal(rs[:, 1:2], rs[:, 0:1]).then_inc(*Sv.up("rs", *k))
                    ve.wait_ge(*Sv.at("rs", *k))
                    V.tensor_scalar(t, t, mv[:, 0:1], rs[:, 1:2], ALU.subtract, ALU.mult).then_inc(*Sv.up("centred", *k))
                    ve.wait_ge(*Sv.at("centred", *k))
                    V.tensor_tensor(t, t, ln[:, 0], ALU.mult).then_inc(*Sv.up("gained", *k))
                    ve.wait_ge(*Sv.at("gained", *k))
                    V.tensor_tensor(h[:, a], t, ln[:, 1], ALU.add).then_inc(*Sv.up("h", *k))

            def conv1():
                Sv = S("conv_dve")
                V.memset(m1["z"][:, :, 0:1], 0.0).then_inc(*Sv.up("edge0"))
                V.memset(m1["z"][:, :, 257:258], 0.0).then_inc(*Sv.up("edge1"))
                for j in range(8):
                    ve.wait_ge(*consumed(("conv_in", 4 + j // 4)))
                    ve.wait_ge(*S("conv_act").at("c", j))
                    V.tensor_tensor(m1["z"][:, j, 1:257], bank(2 + j % 4 // 2)[:, j % 2 * T:j % 2 * T + T], m1["c"][:, j],
                                    ALU.mult).then_inc(*Sv.up("z", j))
                ve.wait_ge(*Sv.at("z", 7))
                for i in range(3):
                    for j in range(8):
                        if i == 0:
                            V.tensor_scalar(m1["conv"][:, j], m1["z"][:, j, 0:T], PC("conv_w", j), None, ALU.mult
                                            ).then_inc(*Sv.up("tap", i, j))
                        else:
                            ve.wait_ge(*Sv.at("tap", i - 1, j))
                            V.scalar_tensor_tensor(out=m1["conv"][:, j], in0=m1["z"][:, j, i:i + T], scalar=PC("conv_w", i * KD + j),
                                                   in1=m1["conv"][:, j], op0=ALU.mult, op1=ALU.add).then_inc(*Sv.up("tap", i, j))
                for j in range(8):
                    ve.wait_ge(*consumed(("conv_in", j // 4)))
                    ve.wait_ge(*Sv.at("tap", 2, j))
                    V.tensor_tensor(m1["mix"][:, j], bank(j // 2)[:, j % 2 * T:j % 2 * T + T], m1["conv"][:, j], ALU.mult
                                    ).then_inc(*Sv.up("mix", j))

            def ffn(l):
                Sa, Sp, Sv = S("ffn_act"), S("ffn_pe"), S("ffn_dve")
                wk, vals, st = ff["wk"][0:E], ff["vals"][0:E], ff["st"]
                ve.wait_ge(*Sp.at("logits", l))
                V.tensor_reduce(st[:, 0:2], bank(0, 2 * E).rearrange("p (a e) -> p a e", a=TT), AX_X, ALU.max
                                ).then_inc(*Sv.up("row_max", l))
                ve.wait_ge(*Sv.at("row_max", l))
                V.tensor_scalar(st[:, 2:4], st[:, 0:2], -1.0, None, ALU.mult).then_inc(*Sv.up("neg_max", l))
                ve.wait_ge(*Sa.at("ex", l, 1))
                V.reciprocal(st[:, 6:8], st[:, 4:6]).then_inc(*Sv.up("inverse", l))
                ve.wait_ge(*Sv.at("inverse", l))
                for a in range(TT):
                    V.tensor_scalar(ff["ex"][:, a], ff["ex"][:, a], st[:, 6 + a:7 + a], None, ALU.mult
                                    ).then_inc(*Sv.up("share", l, a))
                ve.wait_ge(*Sp.at("shares", l))
                V.tensor_copy(wk, bank(1, T)[0:E]).then_inc(*Sv.up("wk", l, 0))
                for r in range(4):
                    ve.wait_ge(*Sv.at("wk", l, r))
                    m8 = vals[:, 8 * r:8 * r + 8]
                    V.max(m8, wk).then_inc(*Sv.up("max8", l, r))
                    ve.wait_ge(*Sv.at("max8", l, r))
                    V.max_index(idx_u[0:E, 8 * r:8 * r + 8], m8, wk).then_inc(*Sv.up("index", l, r))
                    if r < 3:
                        ve.wait_ge(*Sv.at("index", l, r))
                        V.match_replace(wk, m8, wk, -1.0).then_inc(*Sv.up("wk", l, r + 1))
                ve.wait_ge(*Sv.at("index", l, 3))
                V.tensor_copy(ff["idf"][0:E], idx_u[0:E, :]).then_inc(*Sv.up("values", l))
                ve.wait_ge(*Sv.at("values", l))
                own = T2("own_expert")[0:E].rearrange("p (e s) -> p e s", e=E)
                V.tensor_tensor(ff["di"][0:E], own, ff["idf"][0:E].unsqueeze(1).to_broadcast([E, E, CAP]), ALU.mult
                                ).then_inc(*Sv.up("spread", l))
                V.tensor_tensor(ff["dg"][0:E], own, vals.unsqueeze(1).to_broadcast([E, E, CAP]), ALU.mult
                                ).then_inc(*Sv.up("spread_gates", l))
                ve.wait_ge(*Sp.at("rows", l))
                for a in range(TT):
                    V.tensor_scalar(ff["pick"][:, a], bank(0), T2("token")[:, a:a + 1], None, ALU.is_equal
                                    ).then_inc(*Sv.up("pick", l, a))
                ve.wait_ge(*Sp.at("cols", l))
                V.tensor_copy(ff["cols"], bank(1, 8)).then_inc(*Sv.up("cols", l))
                for k in range(1, KD, 2):
                    ve.wait_ge(*Sp.at("gather", l, k))
                    V.tensor_scalar(ff["xe"][:, k], bank(4 + k % 4), modcol[:, 3, k, 0:1], modcol[:, 2, k, 0:1],
                                    ALU.mult, ALU.add).then_inc(*Sv.up("xe", l, k))
                ve.wait_ge(*Sv.at("cols", l))
                for g in range(NG):
                    V.tensor_scalar(ff["put"][:, g], T2("iota"), ff["cols"][:, g:g + 1], ff["cols"][:, 4 + g:5 + g],
                                    ALU.is_equal, ALU.mult).then_inc(*Sv.up("put", l, g))
                Sx, Sax, Spx = (S(f"expert{l}_{e}") for e in ("dve", "act", "pe"))
                base = number[("expert", l, 0)]
                Sx.open_loop()
                with ve.Fori(0, NG) as g:
                    ve.wait_ge(used, g * (3 * KD) + (base + 2 * KD))
                    ve.wait_ge(*Sax.turn(g, "silu"))
                    for b in range(2):
                        V.tensor_tensor(ff["hg"][:, b * HALF:(b + 1) * HALF], bank(2 + b), ff["hg"][:, b * HALF:(b + 1) * HALF],
                                        ALU.mult).then_inc(*Sx.up("hidden", b))
                    ve.wait_ge(used, g * (3 * KD) + (base + 3 * KD))
                    V.tensor_copy(ff["ye"][:, bass.ds(g, 1)].rearrange("p a n -> p (a n)"), ps_t[:, 4 * HALF:6 * HALF]
                                  ).then_inc(*Sx.up("ye"))
                Sx.close_loop(NG)

            def second(l):
                Sa, Sp, Sv, So = S("second_act"), S("second_pe"), S("second_dve"), S("second_pool")
                st = at2["stat"]
                ve.wait_ge(*Sa.at("root", l))
                V.reciprocal(st[:, 44:46], st[:, 42:44]).then_inc(*Sv.up("rs", l))
                ve.wait_ge(*Sv.at("rs", l))
                for a in range(TT):
                    V.tensor_scalar(xn_tok[:, a], h[:, a], st[:, 44 + a:45 + a], None, ALU.mult).then_inc(*Sv.up("normed", l, a))
                for i in range(2):
                    if i == 0:
                        ve.wait_ge(*Sv.at("normed", l, 1))
                    V.memset(s2["raw"][:, i, :, 0:1], 0.0).then_inc(*Sv.up("edge", l, i))
                turned(f"sec{l}", s2["ht"], lambda k: PC(f"norm_g{l}", k), None)
                ve.wait_ge(*Sv.at("edge", l, 1))
                for n in range(4):
                    ve.wait_ge(*Sa.at("raw", l, n))
                    if n:
                        ve.wait_ge(*Sv.at("mixed", l, n - 1))
                    tiles = 4 if n < 3 else 1
                    raw, diff = s2["raw"][:, n % 2, 0:tiles], s2["diff"][:, 0:tiles]
                    V.tensor_tensor(diff, raw[:, :, 0:T], raw[:, :, 1:T + 1], ALU.subtract).then_inc(*Sv.up("diff", l, n))
                    ve.wait_ge(*Sv.at("diff", l, n))
                    for j in range(tiles):
                        dst = s2["rkv"][:, n, j] if n < 3 else s2["wal"]
                        ins = V.scalar_tensor_tensor(out=dst, in0=diff[:, j], scalar=PC(f"mu{l}", 4 * n + j), in1=raw[:, j, 1:T + 1],
                                                     op0=ALU.mult, op1=ALU.add)
                        ins.then_inc(*Sv.up(*(("mixed", l, n) if j == tiles - 1 else ("mixing", l, n, j))))
                if l == 0:
                    ve.wait_ge(*Sv.at("mixed", l, 2))
                    V.tensor_copy(v_first, s2["rkv"][:, 2]).then_inc(*Sv.up("v_first"))
                else:
                    ve.wait_ge(*Sv.at("mixed", l, 3))
                    V.tensor_tensor(s2["diff"], v_first, s2["rkv"][:, 2], ALU.subtract).then_inc(*Sv.up("towards"))
                    ve.wait_ge(*Sv.at("towards"))
                    ve.wait_ge(*Sa.at("nu", 3))
                    V.tensor_tensor(s2["diff"], s2["diff"], s2["nu"], ALU.mult).then_inc(*Sv.up("by_nu"))
                    ve.wait_ge(*Sv.at("by_nu"))
                    V.tensor_tensor(s2["rkv"][:, 2], s2["rkv"][:, 2], s2["diff"], ALU.add).then_inc(*Sv.up("blend", 1))
                    ve.wait_ge(*Sv.at("blend", 1))
                for p in range(2):
                    recurrence(l, p)
                attention_parts(l)

            def recurrence(l, p):
                Sa, Sp, Sv, So = S("rwkv_act"), S("rwkv_pe"), S("rwkv_dve"), S("rwkv_pool")
                K = (l, p)
                r, k, v = (s2["rkv"][:, i, 2 * p:2 * p + 2].rearrange("p j t -> p (j t)") for i in range(3))
                half = lambda ap, jj: ap[:, jj * T:jj * T + T]

                def mul(dst, a, b, *key):
                    V.tensor_tensor(dst, a, b, ALU.mult).then_inc(*Sv.up(*key))

                if p == 0:
                    ve.wait_ge(*S("second_dve").at("mixed", l, 3))
                for jj in range(2):
                    if p == 0:
                        ve.wait_ge(*S("second_act").at("nu", 3) if l else S("second_act").at("raw", l, 3))
                    V.tensor_scalar(half(rw["kk"], jj), half(k, jj), PC(f"k_k{l}", 2 * p + jj), None, ALU.mult
                                    ).then_inc(*Sv.up("kk0", *K, jj))
                ve.wait_ge(*Sa.at("a", *K, 1))
                V.tensor_scalar(rw["lw"], rw["lw"], -DECAY, None, ALU.mult).then_inc(*Sv.up("lw", *K))
                for jj in range(2):
                    V.tensor_scalar(half(rw["kmod"], jj), half(rw["a"], jj), 1.0, PC(f"k_a{l}", 2 * p + jj), ALU.subtract, ALU.mult
                                    ).then_inc(*Sv.up("kmod0", *K, jj))
                ve.wait_ge(*Sv.at("lw", *K))
                V.tensor_tensor_scan(rw["L"], T2("carry", second_at), rw["lw"], 0.0, ALU.mult, ALU.add).then_inc(*Sv.up("L", *K))
                ve.wait_ge(*Sv.at("kmod0", *K, 1))
                V.scalar_tensor_tensor(out=rw["kmod"], in0=rw["kmod"], scalar=1.0, in1=k, op0=ALU.add, op1=ALU.mult
                                       ).then_inc(*Sv.up("kmod", *K))
                ve.wait_ge(*Sv.at("L", *K))
                chunks = rw["L"].rearrange("p (c t) -> p c t", c=8)
                V.tensor_tensor(rw["eLm"], rw["L"], rw["lw"], ALU.subtract).then_inc(*Sv.up("before", *K))
                V.tensor_tensor(rw["eH"].rearrange("p (c t) -> p c t", c=8), chunks[:, :, CH - 1:CH].to_broadcast([P, 8, CH]), chunks,
                                ALU.subtract).then_inc(*Sv.up("exponents", *K))
                ve.wait_ge(*Sa.at("kk_root", *K))
                V.tensor_scalar(rw["tmp"], rw["tmp"], 1e-12, None, ALU.max).then_inc(*Sv.up("kk_floor", *K))
                ve.wait_ge(*Sv.at("kk_floor", *K))
                V.reciprocal(rw["tmp"], rw["tmp"]).then_inc(*Sv.up("kk_rs", *K))
                ve.wait_ge(*Sv.at("kk_rs", *K))
                mul(rw["kk"], rw["kk"], rw["tmp"], "kk", *K)
                ve.wait_ge(*Sv.at("kk", *K))
                mul(rw["a"], rw["kk"], rw["a"], "b", *K)
                for jj in range(2):
                    V.scalar_tensor_tensor(out=half(rw["tmp"], jj), in0=half(r, jj), scalar=PC(f"r_k{l}", 2 * p + jj),
                                           in1=half(rw["kmod"], jj), op0=ALU.mult, op1=ALU.mult).then_inc(*Sv.up("rk", *K, jj))
                by_tile = lambda ap: ap.rearrange("p (j a t) -> p j a t", j=2, a=2)
                ve.wait_ge(*Sa.at("eLm", *K))
                mul(rw["kr"][:, :, :, 0], by_tile(rw["kk"]), by_tile(rw["eLm"]), "kq", *K)
                ve.wait_ge(*Sa.at("eN", *K))
                ve.wait_ge(*Sv.at("b", *K))
                mul(rw["bt"].rearrange("p j t -> p (j t)"), rw["a"], rw["eN"], "bt", *K)
                mul(rw["kt"].rearrange("p j t -> p (j t)"), rw["kmod"], rw["eN"], "kt0", *K)
                ve.wait_ge(*Sa.at("eL", *K))
                mul(rw["kr"][:, :, :, 1], by_tile(r), by_tile(rw["eL"]), "kt", *K)
                ve.wait_ge(*Sp.at("rk_sum", *K))
                mul(rw["bonus"], bank(3), v, "bonus", *K)
                ve.wait_ge(*So.at("hats", *K, 1))
                ve.wait_ge(*Sv.at("kt", *K))
                mask = T2("upper", second_at).unsqueeze(1).to_broadcast([P, 4, 2 * P])
                for n, g, b in (("gram_b", "gb", 0), ("gram_k", "gk", 4)):
                    ve.wait_ge(*Sp.at(n, *K))
                    for hh in range(2):
                        src = ps_t[:, (b + 2 * hh) * HALF:(b + 2 * hh + 2) * HALF].rearrange("p (q n) -> p q n", q=4)
                        V.tensor_tensor(rw[g][:, 4 * hh:4 * hh + 4], src, mask, ALU.mult).then_inc(*Sv.up(g, *K, hh))
                ident = T1("ident").unsqueeze(1).to_broadcast([P, 4, P])
                neg = T2("neg_pair", second_at).unsqueeze(1).to_broadcast([P, 4, P])
                neg_t = T2("neg_pair_t", second_at).unsqueeze(1).to_broadcast([P, 4, P])
                inv, inv_t = rw["inv"], rw["inv_t"]
                ve.wait_ge(*Sp.at("gram_a", *K))
                hs = lambda hh: slice(4 * hh, 4 * hh + 4)
                for hh in range(2):
                    V.tensor_tensor(inv[:, hs(hh)], bank(hh).rearrange("p (q n) -> p q n", q=4), neg, ALU.mult
                                    ).then_inc(*Sv.up("inv0", *K, hh))
                for hh in range(2):
                    V.tensor_tensor(inv_t[:, hs(hh)], rw["gb"][:, hs(hh), 0:P], neg_t, ALU.mult).then_inc(*Sv.up("inv_t0", *K, hh))
                for hh in range(2):
                    ve.wait_ge(*Sv.at("inv0", *K, hh))
                    V.tensor_tensor(inv[:, hs(hh)], inv[:, hs(hh)], ident, ALU.add).then_inc(*Sv.up("inv", *K, 0, hh))
                for hh in range(2):
                    ve.wait_ge(*Sv.at("inv_t0", *K, hh))
                    V.tensor_tensor(inv_t[:, hs(hh)], inv_t[:, hs(hh)], ident, ALU.add).then_inc(*Sv.up("inv_t", *K, 0, hh))
                for n in range(1, LEVELS):
                    for hh in range(2):
                        for x, m, b in (("inv", inv, 4), ("inv_t", inv_t, 6)):
                            if x == "inv" and n == LEVELS - 1:
                                continue
                            ve.wait_ge(*Sp.at(x, *K, n, hh))
                            if x == "inv":
                                ve.wait_ge(*Sp.at("step", *K, n, hh))
                            ve.wait_ge(*Sp.at("inv_t", *K, n, hh))
                            ve.wait_ge(*Sv.at(x, *K, n - 1, hh))
                            V.tensor_tensor(m[:, hs(hh)], m[:, hs(hh)], bank(b + hh).rearrange("p (q n) -> p q n", q=4),
                                            ALU.subtract).then_inc(*Sv.up(x, *K, n, hh))
                gh = rw["prod"]
                for hh in range(2):
                    ve.wait_ge(*Sp.at("gh", *K, hh))
                    V.tensor_scalar(gh[:, hs(hh)], bank(2 + hh).rearrange("p (q n) -> p q n", q=4), -1.0, None, ALU.mult
                                    ).then_inc(*Sv.up("gh", *K, hh))
                ve.wait_ge(*Sp.at("y0", *K))
                V.tensor_tensor(rw["z"].rearrange("p j (a t) -> p j a t", a=2), bank(5).rearrange("p (j a t) -> p j a t", j=2, a=2),
                                rw["kr"][:, :, :, 1], ALU.add).then_inc(*Sv.up("z", *K))
                ve.wait_ge(*Sa.at("carried", *K, 1))
                stt, carried = rw["state"], rw["carried"]
                V.tensor_copy(stt[:, 1], carried[:, 0]).then_inc(*Sv.up("state", *K, 1))
                for c in (1, 2):
                    ve.wait_ge(*Sv.at("state", *K, c))
                    for jj in range(2):
                        x = jj * T + c * CH + CH - 1
                        V.scalar_tensor_tensor(out=stt[:, c + 1, jj], in0=stt[:, c, jj], scalar=rw["eL"][:, x:x + 1],
                                               in1=carried[:, c, jj], op0=ALU.mult, op1=ALU.add).then_inc(*Sv.up("decayed", *K, c, jj))
                    ve.wait_ge(*Sv.at("decayed", *K, c, 1))
                    ve.wait_ge(*Sp.at("move", *K, c))
                    for hh in range(2):
                        o = 64 * hh
                        V.tensor_tensor(stt[o:o + 64, c + 1], stt[o:o + 64, c + 1], bank(6 + hh, P)[o:o + 64].rearrange("p (j n) -> p j n", j=2),
                                        ALU.add).then_inc(*Sv.up(*(("state", *K, c + 1) if hh else ("state0", *K, c + 1))))
                ve.wait_ge(*Sp.at("read", *K))
                ve.wait_ge(*Sa.at("y0", *K))
                y = rw["y"]
                for hh in range(2):
                    o = 64 * hh
                    src = bank(2 + hh)[o:o + 64].rearrange("p (j t) -> p j t", j=2)[:, :, CH:T]
                    V.tensor_tensor(y[o:o + 64, :, CH:T], src, y[o:o + 64, :, CH:T], ALU.add
                                    ).then_inc(*Sv.up(*(("y", *K) if hh else ("y_low", *K))))
                yf = y.rearrange("p j t -> p (j t)")
                ve.wait_ge(*Sv.at("y", *K))
                ve.wait_ge(*Sp.at("gn_mean", *K))
                V.scalar_tensor_tensor(out=yf, in0=bank(4), scalar=-1.0 / 64, in1=yf, op0=ALU.mult, op1=ALU.add
                                       ).then_inc(*Sv.up("centred", *K))
                ve.wait_ge(*Sa.at("gn_root", *K))
                V.reciprocal(rw["tmp2"], rw["tmp2"]).then_inc(*Sv.up("gn_rs", *K))
                ve.wait_ge(*Sv.at("gn_rs", *K))
                mul(yf, yf, rw["tmp2"], "scaled", *K)
                ve.wait_ge(*Sv.at("scaled", *K))
                for jj in range(2):
                    V.tensor_scalar(half(yf, jj), half(yf, jj), PC(f"lnx_g{l}", 2 * p + jj), PC(f"lnx_b{l}", 2 * p + jj),
                                    ALU.mult, ALU.add).then_inc(*Sv.up("affine", *K, jj))
                ve.wait_ge(*Sv.at("affine", *K, 1))
                V.tensor_tensor(yf, yf, rw["bonus"], ALU.add).then_inc(*Sv.up("with_bonus", *K))
                ve.wait_ge(*Sv.at("with_bonus", *K))
                oc = s2["oc"][:, 2 * p:2 * p + 2].rearrange("p j t -> p (j t)")
                mul(oc, oc, yf, "o", *K)
                ve.wait_ge(*Sv.at("o", *K))

            def attention_parts(l):
                Sa, Sp, Sv = S("second_act"), S("second_pe"), S("second_dve")
                Nd = S("norm_dve")

                def norm2(i):
                    u = ("sec", l, i)
                    r0, r1, n, _, b, _ = unit(l, i)
                    ve.wait_ge(*S("norm_act").at("sd", u))
                    if before(u):
                        ve.wait_ge(*Nd.at("out", before(u)))
                    m = T if i == 0 else n
                    rs = at2["t1"][r0:r1, 0:m]
                    V.reciprocal(rs, at2["sd"][r0:r1, 0:m]).then_inc(*Nd.up("rs", u))
                    ve.wait_ge(*Nd.at("rs", u))
                    x = bank(b, n)[r0:r1]

                    def scaled(dst, src, gain, by, last):
                        V.scalar_tensor_tensor(out=dst, in0=src, scalar=gain, in1=by, op0=ALU.mult, op1=ALU.mult
                                               ).then_inc(*Nd.up(last, u))

                    if i == 0:
                        for j in range(2):
                            scaled(at2["cq"][:, j], x[:, j * T:j * T + T], PC(f"qa_g{l}", j), rs, "out" if j else "plain")
                    elif i == 1:
                        scaled(at2["ckv"], x, PC(f"kva_g{l}"), rs, "out")
                    elif i < 7:
                        gain = par[r0:r1, par_at[(f"mk_g{l}" if i == 2 else f"mq_g{l}")][0]:][:, 0:1]
                        xn, t1, t2 = (at2[x_][r0:r1, 0:n] for x_ in ("xn", "t1", "t2"))
                        scaled(xn, x, gain, rs, "xn")
                        ve.wait_ge(*Nd.at("xn", u))
                        tiles = n // T
                        both = lambda ap: ap.rearrange("p (j t) -> p j t", j=tiles)
                        wide = lambda name: T2(name, second_at)[r0:r1].unsqueeze(1).to_broadcast([r1 - r0, tiles, T])
                        V.tensor_tensor(both(t1), both(xn), wide("cos"), ALU.mult).then_inc(*Nd.up("t1", u))
                        ve.wait_ge(*S("norm_pe").at("swap", u))
                        V.tensor_tensor(both(t2), both(bank(7, n)[r0:r1]), wide("sin"), ALU.mult).then_inc(*Nd.up("t2", u))
                        ve.wait_ge(*Nd.at("t2", u))
                        if i == 2:
                            for hd in range(H2):
                                V.tensor_tensor(at2["k"][r0:r1, hd], t1, t2, ALU.add).then_inc(*Nd.up("out" if hd == 7 else "copy", u))
                        else:
                            j = 2 * (i - 3)
                            V.tensor_tensor(at2["q"][r0:r1, j:j + 2], both(t1), both(t2), ALU.add).then_inc(*Nd.up("out", u))
                    elif i < 11:
                        j = 2 * (i - 7)
                        scaled(at2["k"][0:64, j:j + 2].rearrange("p j t -> p (j t)"), x, PC(f"mk_g{l}", 0, 64), rs, "out")
                    else:
                        j, t = (i - 11) % 2 * 2, ("q", "k")[(i - 11) // 2]
                        scaled(at2[t][:, j:j + 2].rearrange("p j t -> p (j t)"), x, PC(f"f{t}_g{l}"), rs, "out")

                for i in range(11):
                    norm2(i)
                for a in range(TT):
                    V.tensor_copy(at2["v"][:, a], bank((6, 0)[a])).then_inc(*Sv.up("values", l, 0, a))
                attention2(l, 0, 96.0 ** -0.5)
                ve.wait_ge(*consumed(("in", l, "fv")))
                for a in range(TT):
                    V.tensor_copy(at2["v"][:, a], bank(5 + a)).then_inc(*Sv.up("values", l, 1, a))
                for i in range(11, 15):
                    norm2(i)
                V.memset(at2["cum"], 0.0).then_inc(*Sv.up("zero", l, 0))
                V.memset(at2["ncum"], 0.0).then_inc(*Sv.up("zero", l, 1))
                f = at2["ff"][0:8]
                ve.wait_ge(*Sa.at("log", l))
                V.tensor_scalar(f[:, 1], bank(7, T)[0:8], PC(f"fb{l}", 0, 8), 0.0, ALU.add, ALU.min).then_inc(*Sv.up("low", l))
                ve.wait_ge(*Sv.at("low", l))
                V.tensor_tensor(f[:, 2], f[:, 1], f[:, 0], ALU.subtract).then_inc(*Sv.up("log_f", l))
                ve.wait_ge(*Sv.at("log_f", l))
                V.tensor_tensor_scan(f[:, 3], T1("ones")[0:8, 0:1].to_broadcast([8, T]), f[:, 2], 0.0, ALU.mult, ALU.add
                                     ).then_inc(*Sv.up("scan", l))
                ve.wait_ge(*Sv.at("scan", l))
                ve.wait_ge(*Sv.at("zero", l, 1))
                V.tensor_scalar(at2["cum"][0:8], f[:, 3], 8.0, None, ALU.mult).then_inc(*Sv.up("cum", l))
                V.tensor_scalar(at2["ncum"][0:8], f[:, 3], -8.0, None, ALU.mult).then_inc(*Sv.up("ncum", l))
                attention2(l, 1, 0.125)
                for b in range(3):
                    for i in range(4):
                        ve.wait_ge(*Sa.at("merge", l, b, i))
                        m2 = merged[:, 2 * i:2 * i + 2].rearrange("p j t -> p (j t)")
                        dst = m2 if b == 0 else at2["mt"]
                        if b:
                            x = 4 * b + i - 1
                            if x >= 4:
                                ve.wait_ge(*Sv.at("merged", l, x // 4, x % 4))
                        V.tensor_tensor(dst, bank(i), at2["sg"][:, i % 2], ALU.mult).then_inc(*Sv.up("weighed", l, b, i))
                        ve.wait_ge(*Sv.at("weighed", l, b, i))
                        if b:
                            V.tensor_tensor(m2, m2, at2["mt"], ALU.add).then_inc(*Sv.up("merged", l, b, i))
                for a in range(TT):
                    ve.wait_ge(*consumed(("out", l, 1)))
                    V.tensor_tensor(h[:, a], ps_t[:, 2 * a * HALF:(2 * a + 2) * HALF], h[:, a], ALU.add
                                    ).then_inc(*Sv.up("residual", l, a))

            def attention2(l, br, scale):
                Sa, Sp, Sv = S("att_act"), S("att_pe"), S("att_dve")
                st, o2 = at2["stat"], at2["oa" if br == 0 else "ob"]
                K = (1, l, br)
                for u in range(10):
                    if u < 8:
                        c = 4 * (u % 2)
                        sc_ = at2["score"][:, u % 2]
                        ve.wait_ge(*Sp.at("score", *K, u))
                        if u >= 2:
                            ve.wait_ge(*Sa.at("exp", *K, u - 2, 1))
                        V.scalar_tensor_tensor(out=sc_, in0=bank(u % 2, 384), scalar=scale, in1=T2("causal", second_at),
                                               op0=ALU.mult, op1=ALU.add).then_inc(*Sv.up("score", *K, u))
                        ve.wait_ge(*Sv.at("score", *K, u))
                        V.tensor_reduce(st[:, 16:17], sc_[:, 0:P], AX_X, ALU.max).then_inc(*Sv.up("row_max", *K, u, 0))
                        V.tensor_reduce(st[:, 17:18], sc_[:, P:384], AX_X, ALU.max).then_inc(*Sv.up("row_max", *K, u, 1))
                        ve.wait_ge(*Sv.at("row_max", *K, u, 1))
                        V.tensor_scalar(st[:, c:c + 2], st[:, 16:18], -1.0, None, ALU.mult).then_inc(*Sv.up("max", *K, u))
                        ve.wait_ge(*Sv.at("max", *K, u))
                    if 1 <= u <= 8:
                        v = u - 1
                        c = 8 + 4 * (v % 2)
                        ve.wait_ge(*Sa.at("exp", *K, v, 1))
                        V.reciprocal(st[:, 18:20], st[:, c:c + 2]).then_inc(*Sv.up("inverse", *K, v))
                        ve.wait_ge(*Sv.at("inverse", *K, v))
                        pr = at2["prob"][:, v % 2]
                        V.tensor_scalar(pr[:, 0:P], pr[:, 0:P], st[:, 18:19], None, ALU.mult).then_inc(*Sv.up("prob", *K, v, 0))
                        V.tensor_scalar(pr[:, P:384], pr[:, P:384], st[:, 19:20], None, ALU.mult).then_inc(*Sv.up("prob", *K, v, 1))
                        ve.wait_ge(*Sv.at("prob", *K, v, 1))
                    if u >= 2:
                        v = u - 2
                        o = 64 * (v % 2)
                        ve.wait_ge(*Sp.at("value", *K, v))
                        if v == 0:
                            ve.wait_ge(*S("second_act").at("gate_a" if br == 0 else "gate_b", l, 1))
                        V.tensor_tensor(o2[o:o + 64, v // 2], bank(3 + v % 2, T)[o:o + 64], o2[o:o + 64, v // 2], ALU.mult
                                        ).then_inc(*Sv.up("value", *K, v))

            modulation(0)
            if upto >= 1:
                turned("ctx", m0["uc"], lambda k: modcol[:, 1, k, 1:2], lambda k: modcol[:, 0, k, 1:2])
                turned("mix0", m0["ut"], lambda k: modcol[:, 1, k, 0:1], lambda k: modcol[:, 0, k, 0:1])
                mixer0()
            if upto >= 2:
                attention0()
                pool0()
                post_norm(0, 0, lambda a: consumed(("mix_out", 0, 1)))
            if upto >= 3:
                turned("ffn0", ff["ut"], lambda k: modcol[:, 3, k, 0:1], lambda k: modcol[:, 2, k, 0:1])
                ffn(0)
                post_norm(0, 1, lambda a: S("ffn_pe").at("y", 0, a))
            if upto >= 4:
                modulation(1)
            if upto >= 5:
                turned("mix1", m1["ut"], lambda k: modcol[:, 1, k, 0:1], lambda k: modcol[:, 0, k, 0:1])
                conv1()
                post_norm(1, 0, lambda a: consumed(("mix_out", 1, 1)))
            if upto >= 6:
                turned("ffn1", ff["ut"], lambda k: modcol[:, 3, k, 0:1], lambda k: modcol[:, 2, k, 0:1])
                ffn(1)
                post_norm(1, 1, lambda a: S("ffn_pe").at("y", 1, a))
            if upto >= 7:
                second(0)
            if upto >= 8:
                second(1)

        @block.gpsimd
        def _(po):
            G = nc.gpsimd

            def gate_bias(l):
                if l:
                    po.wait_ge(*S("post_dve").at("t", 0, 1, 1))
                for i, m in enumerate((2, 5)):
                    po.dma_start(gate[:, i], w["b_mod"][l:l + 1, m * D:(m + 1) * D].to_broadcast([P, D])
                                 ).then_inc(loaded("gate_bias")[0], 16)

            def ln_params(l, part, last):
                if last is not None:
                    po.wait_ge(*last)
                for i, n in enumerate(("ln_mix_g", "ln_mix_b") if part == 0 else ("ln_ffn_g", "ln_ffn_b")):
                    po.dma_start(ln[:, i], w[n][l:l + 1, :].to_broadcast([P, D])).then_inc(loaded("ln")[0], 16)

            def router(l):
                if l:
                    po.wait_ge(*S("ffn_pe").at("logits", 0))
                po.dma_start(small_t[:, 512:640].rearrange("p (k e) -> p k e", k=KD),
                             w["w_router"][l].rearrange("(k p) e -> p k e", p=P)).then_inc(loaded("router")[0], 16)

            def ffn(l):
                Sx = S(f"expert{l}_pool")
                base = number[("expert", l, 0)]
                po.wait_ge(*S("ffn_act").at("xe", l, 6))
                po.wait_ge(*S("ffn_dve").at("xe", l, 7))
                Sx.open_loop()
                with po.Fori(0, NG) as g:
                    po.wait_ge(used, g * (3 * KD) + (base - KD))
                    G.tensor_copy(ff["xg"], ff["xe"][:, :, bass.ds(g * P, P)]).then_inc(*Sx.up("xg"))
                Sx.close_loop(NG)

            def second(l):
                Sv, So = S("second_dve"), S("second_pool")
                if l == 0:
                    po.wait_ge(*S("ffn_dve").at("put", 1, 3))
                    po.dma_start(tab2[:, 0:n_second], w["tables_second"]).then_inc(loaded("tables_second")[0], 16)
                    po.wait_ge(*S("ffn_pe").at("logits", 1))
                else:
                    po.wait_ge(*S("rwkv_pe").at("lora", 0, 1))
                for dst, src in ((small_t[:, 0:512], w["rwkv_lora"][l]),
                                 (small_t[:, 512:640].rearrange("p (k n) -> p k n", k=4),
                                  w["rwkv_v_down_2"][0].rearrange("(k p) n -> p k n", p=P)),
                                 (small_t[0:32, 640:1152], w["rwkv_v_up_2"][0])):
                    po.dma_start(dst, src).then_inc(loaded("small2")[0], 16)
                for p in range(2):
                    K = (l, p)
                    Ra, Rp, Rv, Ro = S("rwkv_act"), S("rwkv_pe"), S("rwkv_dve"), S("rwkv_pool")
                    flat = lambda ap: ap.rearrange("p j t -> p (j t)")
                    po.wait_ge(*Ra.at("eH", *K))
                    po.wait_ge(*Rv.at("b", *K))
                    G.tensor_tensor(flat(rw["bh"]), rw["a"], rw["eH"], ALU.mult).then_inc(*Ro.up("hats", *K, 0))
                    G.tensor_tensor(flat(rw["kh"]), rw["kmod"], rw["eH"], ALU.mult).then_inc(*Ro.up("hats", *K, 1))
                    for n in range(1, LEVELS):
                        if n == 1:
                            po.wait_ge(*Rv.at("gb", *K, 1))
                            po.wait_ge(*Rp.at("gram_a", *K))
                            po.wait_ge(*Rp.at("gram_k", *K))
                        if n >= 3:
                            po.wait_ge(*Rp.at("step", *K, n - 2, 1))
                        G.tensor_tensor(rw[f"lev{n % 2}"], rw["gb"][:, :, 0:P],
                                        T2(f"level{n}", second_at).unsqueeze(1).to_broadcast([P, 8, P]), ALU.mult
                                        ).then_inc(*Ro.up("level", *K, n))

            gate_bias(0)
            ln_params(0, 0, None)
            router(0)
            if upto >= 3:
                ffn(0)
                ln_params(0, 1, S("post_dve").at("h", 0, 0, 1))
            if upto >= 4:
                gate_bias(1)
                ln_params(1, 0, S("post_dve").at("h", 0, 1, 1))
                router(1)
            if upto >= 6:
                ffn(1)
                ln_params(1, 1, S("post_dve").at("h", 1, 0, 1))
            if upto >= 7:
                second(0)
            if upto >= 8:
                second(1)


def host_arrays(inp):
    a = {n: np.ascontiguousarray(inp[n]) for n in INPUTS if n in inp}
    a["tables"], a["tables_first"], a["tables_second"] = common_tables()[0], first_tables()[0], second_tables()[0]
    a["params"] = param_columns(inp)[0]
    a["rwkv_lora"] = np.concatenate([inp["rwkv_w_up_2"], inp["rwkv_a_up_2"]], 1)
    return a


def declare(nc, arrays):
    w = {n: nc.dram_tensor("in_" + n, arrays[n].shape, F32, kind="ExternalInput").ap() for n in INPUTS}
    return w, nc.dram_tensor("out_0", (1, T, D), F32, kind="ExternalOutput").ap()


def kernel(**inputs):
    import concourse.bacc as bacc
    from concourse.bass_utils import run_bass_kernel_spmd

    arrays = host_arrays({n: np.asarray(a) for n, a in inputs.items()})
    marks = {}
    for _ in range(2):
        nc = bacc.Bacc("TRN2", target_bir_lowering=False, num_devices=1)
        w, out = declare(nc, arrays)
        two_block_program(nc, w, out, marks)
    r = run_bass_kernel_spmd(nc, [{"in_" + n: a for n, a in arrays.items()}], core_ids=[0])
    return r.results[0]["out_0"]
```

```python
from contextlib import ExitStack

import numpy as np

import concourse.bass as bass
from concourse import mybir

F32 = mybir.dt.float32
U32 = mybir.dt.uint32
ALU = mybir.AluOpType
ACT = mybir.ActivationFunctionType
AX_X = mybir.AxisListType.X

P = 128
T = 256
TT = T // P
D = 1024
KD = D // P
E = 16
CAP = 2 * T // E
EG = 4
NG = E // EG
HALF = 512
ALPHA = 4.0 ** 0.25
EPS = 1e-6
GN_EPS = 64e-5
RING = 4
ARENA = 24832
SLOT = 8 * 520
CH = 64
DECAY = 0.606531
NEG = -1e30
LEVELS = 6
H2 = 8

C_Q, C_KV, K_R, G_A, F_Q, F_K, F_V, F_F, G_B = 0, 256, 384, 416, 928, 1440, 1952, 2464, 2472
SH, G_C, MG = 2984, 4648, 5160


def _put(parts, offsets, name, a):
    a = np.asarray(a, np.float32)
    a = a.reshape(a.shape[0], -1)
    full = np.zeros((P, a.shape[1]), np.float32)
    full[:a.shape[0]] = a
    offsets[name] = (sum(x.shape[1] for x in parts), a.shape[1])
    parts.append(full)


def common_tables():
    parts, at = [], {}
    _put(parts, at, "ident", np.eye(P))
    _put(parts, at, "head_ones", np.kron(np.eye(2), np.ones((64, 64))))
    _put(parts, at, "ones", np.ones((P, P)))
    strip = np.arange(P) % 32
    _put(parts, at, "sum_row0", np.repeat((strip == 0)[:, None], P, 1))
    _put(parts, at, "sum_cols", np.stack([strip == 0, strip == 1], 1))
    _put(parts, at, "eps", np.full((P, 1), EPS))
    _put(parts, at, "gn_eps", np.full((P, 1), GN_EPS))
    return np.concatenate(parts, 1), at


def first_tables():
    parts, at = [], {}
    swap = np.zeros((P, P))
    for i in range(0, P, 2):
        swap[i + 1, i] = -1
        swap[i, i + 1] = 1
    _put(parts, at, "swap", swap)
    inv = np.float32(10000.0) ** (-np.arange(0, 32, 2, dtype=np.float32) / np.float32(32))
    row, col = np.arange(T) // 64, np.arange(T) % 64
    ang = np.concatenate([row[:, None].astype(np.float32) * inv, col[:, None].astype(np.float32) * inv], 1)
    ang = np.tile(np.repeat(ang, 2, 1).T, (2, 1))
    _put(parts, at, "cos", np.cos(ang))
    _put(parts, at, "sin", np.sin(ang))
    band = np.zeros((TT, P, 4, T))
    for g, w in enumerate((2, 4, 8, 16)):
        for t in range(T):
            lo, hi = max(t - w // 2, 0), min(t + w // 2, T)
            for s in range(lo, hi):
                band[s // P, s % P, g, t] += 1.0 / (hi - lo)
            band[t // P, t % P, g, t] -= 1.0
    _put(parts, at, "band", band.transpose(1, 0, 2, 3))
    _put(parts, at, "iota", np.repeat(np.arange(T)[None], P, 0))
    _put(parts, at, "token", np.stack([np.arange(P), np.arange(P) + P], 1))
    _put(parts, at, "own_expert", np.kron(np.eye(E), np.ones((1, CAP))))
    return np.concatenate(parts, 1), at


def second_tables():
    parts, at = [], {}
    swap = np.zeros((96, 96))
    for i in range(16):
        swap[64 + 16 + i, 64 + i] = -1
        swap[64 + i, 64 + 16 + i] = 1
    _put(parts, at, "swap", swap)
    inv = np.float32(10000.0) ** (-np.arange(0, 32, 2, dtype=np.float32) / np.float32(32))
    ang = (np.arange(T, dtype=np.float32)[:, None] * inv).T
    c, s = np.ones((96, T)), np.zeros((96, T))
    c[64:80] = c[80:96] = np.cos(ang)
    s[64:80] = s[80:96] = np.sin(ang)
    _put(parts, at, "cos", c)
    _put(parts, at, "sin", s)
    causal = np.where(np.arange(P)[None] <= np.arange(P)[:, None], 0.0, NEG)
    _put(parts, at, "causal", np.concatenate([causal, np.zeros((P, P)), causal], 1))
    i, t = np.arange(P)[:, None], np.arange(P)[None]
    same = i // CH == t // CH
    _put(parts, at, "upper", np.concatenate([same & (i < t), same & (i <= t)], 1))
    _put(parts, at, "neg_pair", -1.0 * (same & (i // 2 == t // 2) & (i > t)))
    _put(parts, at, "neg_pair_t", -1.0 * (same & (i // 2 == t // 2) & (i < t)))
    for n in range(1, LEVELS):
        b = 2 ** n
        _put(parts, at, f"level{n}", (i // (2 * b) == t // (2 * b)) & (i // b + 1 == t // b))
    _put(parts, at, "carry", np.repeat((np.arange(2 * T)[None] % CH != 0), P, 0))
    return np.concatenate(parts, 1), at


def param_columns(inp=None):
    f = (lambda n: inp[n]) if inp is not None else (lambda n: None)
    parts, at = [], {}

    def col(name, a, tiles, rows=P):
        a = np.zeros((tiles, rows), np.float32) if a is None else np.asarray(a).reshape(tiles, rows)
        _put(parts, at, name, a.T)

    def sub(a, *i):
        return None if a is None else np.asarray(a)[i]

    col("cond", None if inp is None else np.stack([f("c")[0], f("c_ctx")]), 2 * KD)
    for layer in range(2):
        b = sub(f("b_mod"), layer)
        for m in (0, 1, 3, 4):
            col(f"b_mod{layer}{m}", None if b is None else b[m * D:(m + 1) * D], KD)
    two = lambda a: None if a is None else np.tile(a, 2)
    col("q_g", two(sub(f("q_norm_g"), 0)), 1)
    col("k_g", two(sub(f("k_norm_g"), 0)), 1)
    col("pool_scale", sub(f("pool_scale"), 0), 4)
    col("conv_w", sub(f("conv_w"), 0), 3 * KD)
    for layer in range(2):
        g = lambda n: sub(f(n + "_2"), layer)
        col(f"norm_g{layer}", g("norm_g"), KD)
        col(f"qa_g{layer}", g("mla_qa_g"), 2)
        col(f"kva_g{layer}", g("mla_kva_g"), 1)
        col(f"mq_g{layer}", g("mla_q_g"), 1, 96)
        kn, kr = g("mla_knope_g"), g("mla_krope_g")
        col(f"mk_g{layer}", None if kn is None else np.concatenate([kn, kr]), 1, 96)
        col(f"fb{layer}", g("fox_b_f"), 1, 8)
        col(f"fq_g{layer}", two(g("fox_q_g")), 1)
        col(f"fk_g{layer}", two(g("fox_k_g")), 1)
        col(f"mu{layer}", g("rwkv_mu"), 13)
        for n in ("w0", "a0", "k_k", "k_a", "r_k", "lnx_g", "lnx_b"):
            col(f"{n}{layer}", g("rwkv_" + n), 4)
    col("v0", sub(f("rwkv_v0_2"), 0), 4)
    return np.concatenate(parts, 1), at


class Signal:

    def __init__(self, handle, marks):
        self.handle, self.marks, self.value, self.period = handle, marks, 0, 0

    def up(self, *key):
        self.value += 1
        self.marks[key] = self.value
        return self.handle, 1

    def at(self, *key):
        return self.handle, self.marks.get(key, 1)

    def turn(self, g, *key):
        return self.handle, g * self.marks.get("period", 1) + self.marks.get(key, 1)

    def open_loop(self):
        self.start = self.value

    def close_loop(self, turns):
        self.marks["period"] = self.value - self.start
        self.value += (turns - 1) * (self.value - self.start)


INPUTS = ["x", "ctx", "b_mod", "ln_mix_g", "ln_mix_b", "ln_ffn_g", "ln_ffn_b", "w_mod", "w_mix_in", "w_pool_grp",
          "w_mix_out", "w_conv_in", "w_conv_out", "w_router", "w_exp_gate", "w_exp_up", "w_exp_down", "w_in_2",
          "mla_w_uq_2", "mla_w_ukv_2", "rwkv_lora", "rwkv_v_down_2", "rwkv_v_up_2", "w_pa_2", "w_pb_2", "w_pc_2",
          "w_out_2", "tables", "tables_first", "tables_second", "params"]


def weight_stream(w):
    order = []

    def rows(a):
        return a.rearrange("(k p) n -> p k n", p=P)

    def add(key, src):
        order.append((key, src))

    def modulation(layer):
        for j in range(12):
            add(("mod", layer, j), rows(w["w_mod"][layer, :, j * HALF:(j + 1) * HALF]))

    modulation(0)
    for layer in range(2):
        if layer == 0:
            for j, (a, b) in enumerate(((0, 512), (512, 768), (768, 1280))):
                add(("mix_in", j), rows(w["w_mix_in"][0, :, a:b]))
            modulation(1)
            for j in range(2):
                add(("mix_out", 0, j), rows(w["w_mix_out"][0, :, j * HALF:(j + 1) * HALF]))
        else:
            for j in (2, 4, 3, 5, 0, 1):
                add(("conv_in", j), rows(w["w_conv_in"][0, :, j * HALF:(j + 1) * HALF]))
            for j in range(2):
                add(("mix_out", 1, j), rows(w["w_conv_out"][0, :, j * HALF:(j + 1) * HALF]))
        for s in range(3 * KD * NG):
            add(("expert", layer, s), None)
    for layer in range(2):
        wi = w["w_in_2"][layer]
        for j in range(3):
            add(("in", layer, "rkv", j), rows(wi[:, SH + j * HALF:SH + (j + 1) * HALF]))
        add(("in", layer, "lora"), rows(wi[:, SH + 3 * HALF:SH + 3 * HALF + P]))
        add(("in", layer, "gate_c"), rows(wi[:, G_C:G_C + HALF]))
        add(("in", layer, "gate_a"), rows(wi[:, G_A:G_A + HALF]))

        def merge(b, j):
            a = MG + b * D + j * HALF
            add(("in", layer, "merge", b, j), rows(wi[:, a:a + HALF]))

        merge(0, 0)
        add(("in", layer, "latent"), rows(wi[:, C_Q:G_A]))
        add(("uq", layer), rows(w["mla_w_uq_2"][layer]))
        merge(0, 1)
        add(("ukv", layer), rows(w["mla_w_ukv_2"][layer]))
        merge(1, 0)
        merge(1, 1)
        add(("in", layer, "fq"), rows(wi[:, F_Q:F_Q + HALF]))
        add(("in", layer, "fk"), rows(wi[:, F_K:F_K + HALF]))
        add(("in", layer, "fv"), rows(wi[:, F_V:F_V + HALF]))
        add(("in", layer, "ff_gate_b"), rows(wi[:, F_F:SH]))
        merge(2, 0)
        merge(2, 1)
        for b, n in enumerate(("w_pa_2", "w_pb_2", "w_pc_2")):
            add(("proj", layer, b), rows(w[n][layer]))
        for j in range(2):
            add(("out", layer, j), rows(w["w_out_2"][layer][:, j * HALF:(j + 1) * HALF]))
    return order


def two_block_program(nc, w, out, marks):
    order = weight_stream(w)
    number = {key: n for n, (key, _) in enumerate(order)}
    view = {key: src for key, src in order}
    tab_at, first_at, second_at, par_at = (f()[1] for f in (common_tables, first_tables, second_tables, param_columns))
    n_tab, n_first, n_second, n_par = (w[n].shape[1] for n in ("tables", "tables_first", "tables_second", "params"))

    with ExitStack() as ctx:
        def sb(name, cols, dt=F32):
            return ctx.enter_context(nc.sbuf_tensor(name, [P, cols], dt))

        ring = sb("ring", RING * SLOT)
        h_t = sb("h", TT * D)
        h = h_t[:, :].rearrange("p (a d) -> p a d", a=TT)
        ln_t = sb("ln", 2 * D)
        ln = ln_t[:, :].rearrange("p (a d) -> p a d", a=2)
        gate_t = sb("gate", 2 * D)
        gate = gate_t[:, :].rearrange("p (a d) -> p a d", a=2)
        tab = sb("tab", n_tab)
        tab2 = sb("tab2", max(n_first, n_second))
        par = sb("par", n_par)
        small_t = sb("small", 1152)
        arena = sb("arena", ARENA)
        ps_t = ctx.enter_context(nc.psum_tensor("ps", [P, 8 * HALF], F32))

        def bank(b, n=HALF):
            return ps_t[:, b * HALF:b * HALF + n]

        def T1(name):
            o, n = tab_at[name]
            return tab[:, o:o + n]

        def T2(name, which=first_at):
            o, n = which[name]
            return tab2[:, o:o + n]

        def PC(name, i=0, rows=P):
            o, _ = par_at[name]
            return par[0:rows, o + i:o + i + 1]

        class Scratch:
            def __init__(self, at=0):
                self.top = at

            def take(self, cols, *dims):
                v = arena[:, self.top:self.top + cols]
                self.top += cols
                assert self.top <= ARENA, self.top
                if len(dims) == 1:
                    v = v.rearrange("p (a n) -> p a n", a=dims[0])
                if len(dims) == 2:
                    v = v.rearrange("p (a b n) -> p a b n", a=dims[0], b=dims[1])
                if len(dims) == 3:
                    v = v.rearrange("p (a b c n) -> p a b c n", a=dims[0], b=dims[1], c=dims[2])
                return v

        signals = {}

        def S(name):
            if name not in signals:
                handle = ctx.enter_context(nc.semaphore(name))
                signals[name] = Signal(handle, marks.setdefault(name, {}))
            return signals[name]

        landed = [ctx.enter_context(nc.semaphore(f"weights_landed{s}")) for s in range(RING)]
        used = ctx.enter_context(nc.semaphore("weights_used"))

        def slot(key, *dims):
            s = number[key] % RING
            src = view[key]
            k, n = (src.shape[1], src.shape[2]) if src is not None else (EG, D)
            return ring[:, s * SLOT:s * SLOT + k * n].rearrange("p (k n) -> p k n", k=k)

        def has_landed(key):
            n = number[key]
            return landed[n % RING], 16 * (n // RING + 1)

        def consumed(key):
            return used, number[key] + 1

        loads = {}

        def loaded(name, n=1):
            if name not in loads:
                loads[name] = ctx.enter_context(nc.semaphore("loaded_" + name))
            return loads[name], 16 * n

        sc = Scratch()
        m0 = dict(xc=sc.take(2048, TT), ut=sc.take(2048, KD), uc=sc.take(2048, KD), q=sc.take(1024, 4),
                  k=sc.take(1024, 2), v=sc.take(512, 4), pt=sc.take(1024, TT), mix=sc.take(2048, KD),
                  sq=sc.take(512), sd=sc.take(512), xn=sc.take(512), t1=sc.take(512), t2=sc.take(512),
                  prob=sc.take(1024, 2), prob_t=sc.take(1024, 2), stat=sc.take(64), pooled=sc.take(1024, 4))
        sc = Scratch()
        m1 = dict(ut=sc.take(2048, KD), c=sc.take(2048, KD), z=sc.take(KD * 258, KD), conv=sc.take(2048, KD),
                  mix=sc.take(2048, KD))
        sc = Scratch()
        ff = dict(ut=sc.take(2048, KD), wk=sc.take(256), vals=sc.take(32), ex=sc.take(32, TT), st=sc.take(16), idf=sc.take(32), di=sc.take(512, E), dg=sc.take(512, E),
                  cols=sc.take(8), pick=sc.take(1024, TT), put=sc.take(1024, NG),
                  pick_g=sc.take(256, TT), put_g=sc.take(256), xg=sc.take(1024, KD), hg=sc.take(1024), ht=sc.take(1024, KD),
                  ye=sc.take(1024), acc=sc.take(2048, TT))
        idx_u = ctx.enter_context(nc.sbuf_tensor("idx", [P, CAP], U32))
        sc = Scratch(21300)
        md = dict(part=sc.take(1024, 2), condT=sc.take(256, KD), sig=sc.take(16))
        modcol_t = sb("modcol", 128)
        modcol = modcol_t[:, :].rearrange("p (l m k c) -> p l m k c", l=2, m=4, k=KD)
        sc = Scratch(22600)
        gates = [gate, sc.take(2048, 2)]
        sc = Scratch(19200)
        pn = dict(t=sc.take(2048, TT), st=sc.take(24, TT), mv=sc.take(4, TT), rs=sc.take(4, TT))

        LATE = 7

        def mod_bank(l, j):
            return 0 if l else (0, 3)[j % 2]

        sc = Scratch()
        s2 = dict(ht=sc.take(2048, KD), oc=sc.take(1024, 4))
        low = sc.top
        s2.update(rkv=sc.take(3072, 3, 4), wal=sc.take(256))
        raw0 = sc.top
        s2.update(raw=sc.take(2 * 4 * 257, 2, 4), diff=sc.take(1024, 4), vd=sc.take(256), nu=sc.take(1024, 4))
        v_first = gate_t[:, 0:1024].rearrange("p (j t) -> p j t", j=4)
        merged = ln_t[:, :].rearrange("p (k t) -> p k t", k=KD)
        xn_tok = ln
        sc = Scratch(raw0)
        rw = {}
        x0 = sc.top
        for n in ("lw", "L", "a", "kk", "kmod", "eLm", "eN", "eH", "tmp"):
            rw[n] = sc.take(512)
        sg = Scratch(x0)
        rw.update(gb=sg.take(2048, 8), gk=sg.take(2048, 8))
        rw.update(eL=sc.take(512), kr=sc.take(1024, 2, 2, 2))
        b0 = sc.top
        rw.update(bt=sc.take(512, 2), kt=sc.take(512, 2), bh=sc.take(512, 2), kh=sc.take(512, 2), bonus=sc.take(512))
        rw.update(inv=sc.take(1024, 8), inv_t=sc.take(1024, 8), prod=sc.take(1024, 8), lev0=sc.take(1024, 8),
                  wk=sc.take(1024, 8), v_tok=sc.take(512, 8), bh_tok=sc.take(512, 8), kh_tok=sc.take(512, 8))
        sg = Scratch(b0)
        rw["lev1"] = sg.take(1024, 8)
        sg = Scratch(b0)
        rw.update(y=sg.take(512, 2), z=sg.take(512, 2), pm=sg.take(512, 4, 2), state=sg.take(512, 4, 2))
        rw["carried"] = rw["wk"].rearrange("p a n -> p (a n)")[:, 0:512].rearrange("p (c j n) -> p c j n", c=4, j=2)
        rw["tmp2"] = rw["inv"].rearrange("p a n -> p (a n)")[:, 0:512]
        keep = Scratch(21760)
        oa, gates_kept = keep.take(1024, 4), keep.take(2048, KD)
        sc = Scratch(low)
        at2 = dict(oa=oa, ob=sc.take(1024, 4), cq=sc.take(512, 2), ckv=sc.take(256), q=sc.take(2048, 8),
                   k=sc.take(2048, 8), v=sc.take(1024, TT), sq=sc.take(512), sd=sc.take(512), xn=sc.take(512),
                   t1=sc.take(512), t2=sc.take(512), score=sc.take(768, 2), prob=sc.take(768, 2), prob_t=sc.take(768, 2),
                   stat=sc.take(64), ff=sc.take(1024, 4), cum=sc.take(256), ncum=sc.take(256),
                   mt=sc.take(512))
        merge_gate = [gates_kept, sc.take(2048, KD), sc.take(2048, KD)]
        UNITS = 15

        def before(u):
            _, l, i = u
            return ("sec", l, i - 1) if i else (("sec", l - 1, UNITS - 1) if l else None)

        def unit(l, i):
            if i == 0:
                return 0, 128, 512, 256, 0, "ones"
            if i == 1:
                return 0, 128, 256, 128, 1, "ones"
            if i == 2:
                return 64, 96, 256, 32, 7, "ones"
            if i < 7:
                return 0, 96, 512, 96, (4, 5, 6, 0)[i - 3], "ones"
            if i < 11:
                return 0, 64, 512, 64, (1, 3, 4, 5)[i - 7], "ones"
            return 0, 128, 512, 64, (0, 1, 3, 4)[i - 11], "head_ones"

        def unit_source(l, i):
            r0, r1, n, _, b, _ = unit(l, i)
            return (ps_t[:, b * HALF + T:b * HALF + T + n] if i == 2 else bank(b, n))[r0:r1]

        def unit_ready(l, i):
            return consumed((("in", l, "latent") if i < 3 else ("uq", l) if i < 7 else ("ukv", l) if i < 11 else
                             ("in", l, "fq") if i < 13 else ("in", l, "fk")))

        block = ctx.enter_context(nc.Block())

        @block.sync
        def _(sp):
            n = 0
            while n < len(order):
                key, src = order[n]
                if key[0] == "expert":
                    layer = key[1]
                    with sp.Fori(0, NG) as g:
                        for m, name in enumerate(("w_exp_gate", "w_exp_up", "w_exp_down")):
                            wv = w[name][layer].rearrange("(g e) (k p) f -> g p k e f", e=EG, p=P)
                            for k in range(KD):
                                i = n + m * KD + k
                                s = i % RING
                                sp.wait_ge(used, g * (3 * KD) + (i - RING + 1))
                                sp.dma_start(ring[:, s * SLOT:s * SLOT + EG * D].rearrange("p (e f) -> p e f", e=EG),
                                             wv[bass.ds(g, 1), :, k].rearrange("a p e f -> p (a e) f")
                                             ).then_inc(landed[s], 16)
                    n += 3 * KD * NG
                    continue
                if n >= RING:
                    sp.wait_ge(used, n - RING + 1)
                sp.dma_start(slot(key), src).then_inc(landed[n % RING], 16)
                n += 1
            sp.wait_ge(*S("second_dve").at("residual", 1, 1))
            sp.dma_start(out[0].rearrange("(a p) d -> p a d", p=P), h).then_inc(loaded("result")[0], 16)
            sp.wait_ge(*loaded("result"))

        @block.scalar
        def _(act):
            A = nc.scalar.activation
            act.dma_start(par[:, :], w["params"]).then_inc(loaded("params")[0], 16)
            act.dma_start(tab[:, :], w["tables"]).then_inc(loaded("tables")[0], 16)
            act.dma_start(h, w["x"][0].rearrange("(a p) d -> p a d", p=P)).then_inc(loaded("x")[0], 16)

            def condition():
                act.wait_ge(*loaded("params"))
                o = par_at["cond"][0]
                A(md["sig"], par[:, o:o + 16], ACT.Sigmoid).then_inc(*S("mod_act").up("sigmoid"))

            def mod_part(l, j):
                act.wait_ge(*consumed(("mod", l, j)))
                if j >= 2:
                    act.wait_ge(*S("mod_pe").at("fold", l, j - 2))
                A(md["part"][:, j % 2], bank(mod_bank(l, j)), ACT.Copy).then_inc(*S("mod_act").up("part", l, j))

            def turned(name, dst, scale, bias):
                for pair in (0, 2):
                    act.wait_ge(*S("turn_pe").at(name, pair))
                    for i in range(2):
                        k = 2 * pair + i
                        src = bank(4 + pair)[:, i * T:(i + 1) * T]
                        if bias is None:
                            A(dst[:, k], src, ACT.Copy, scale=scale(k)).then_inc(*S("turn_act").up(name, k))
                        else:
                            A(dst[:, k], src, ACT.Identity, scale=scale(k), bias=bias(k)).then_inc(*S("turn_act").up(name, k))

            def norm(u, ready, x, rows, n, width, bufs, eps="eps"):
                Sn, Sp, Sv = S("norm_act"), S("norm_pe"), S("norm_dve")
                act.wait_ge(*ready)
                if u[-1] > 0:
                    act.wait_ge(*Sp.at("sum", u[:-1] + (u[-1] - 1,)))
                A(bufs["sq"][0:rows, 0:n], x, ACT.Square).then_inc(*Sn.up("sq", u))
                act.wait_ge(*Sp.at("sum", u))
                if u[-1] > 0:
                    act.wait_ge(*Sv.at("rs", u[:-1] + (u[-1] - 1,)))
                A(bufs["sd"][0:rows, 0:n], bank(2)[0:rows, 0:n], ACT.Sqrt, scale=1.0 / width,
                  bias=T1(eps)[0:rows]).then_inc(*Sn.up("sd", u))

            def attention0():
                Sa, Sp, Sv = S("att_act"), S("att_pe"), S("att_dve")
                st = m0["stat"]
                for u in range(17):
                    if 3 <= u <= 14:
                        mod_part(1, u - 3)
                    if u < 16:
                        act.wait_ge(*Sv.at("max", 0, u))
                        if u >= 2:
                            act.wait_ge(*Sp.at("turned", 0, u - 2))
                        A(m0["prob"][:, u % 2], bank(4 + u % 2), ACT.Exp, scale=0.125, bias=st[:, u:u + 1],
                          accum_out=st[:, 32 + u:33 + u]).then_inc(*Sa.up("exp", 0, u))
                    if u >= 1:
                        act.wait_ge(*Sp.at("turned", 0, u - 1))
                        if u >= 3:
                            act.wait_ge(*Sp.at("value", 0, u - 3))
                        A(m0["prob_t"][:, (u - 1) % 2], bank(6), ACT.Copy).then_inc(*Sa.up("prob_t", 0, u - 1))

            def post_norm(l, part):
                for a in range(TT):
                    act.wait_ge(*S("post_dve").at("var", l, part, a))
                    A(pn["rs"][:, a, 0:1], pn["mv"][:, a, 1:2], ACT.Sqrt, bias=T1("eps")
                      ).then_inc(*S("post_act").up("sd", l, part, a))

            def ffn(l):
                Sa, Sp, Sv = S("ffn_act"), S("ffn_pe"), S("ffn_dve")
                act.wait_ge(*Sv.at("neg_max", l))
                for a in range(TT):
                    A(ff["ex"][:, a], bank(0)[:, a * E:(a + 1) * E], ACT.Exp, bias=ff["st"][:, 2 + a:3 + a],
                      accum_out=ff["st"][:, 4 + a:5 + a]).then_inc(*Sa.up("ex", l, a))
                Sx, Spx = S(f"expert{l}_act"), S(f"expert{l}_pe")
                base = number[("expert", l, 0)]
                Sx.open_loop()
                with act.Fori(0, NG) as g:
                    act.wait_ge(*Spx.turn(g, "gather", 0))
                    for k in range(KD // 2):
                        A(ff["xg"][:, k], bank(6)[:, k * P:(k + 1) * P], ACT.Identity, scale=modcol[:, l, 3, k, 0:1],
                          bias=modcol[:, l, 2, k, 0:1]).then_inc(*Sx.up("xg", k))
                    act.wait_ge(used, g * (3 * KD) + (base + KD))
                    A(ff["hg"], ps_t[:, 0:2 * HALF], ACT.Silu).then_inc(*Sx.up("silu"))
                    for b in range(2):
                        act.wait_ge(*Spx.turn(g, "turned", b))
                        A(ff["ht"][:, 4 * b:4 * b + 4], bank(6 + b).rearrange("p (k n) -> p k n", k=4), ACT.Copy
                          ).then_inc(*Sx.up("ht", b))
                Sx.close_loop(NG)

            def open_gate(key, banks, function, dst):
                act.wait_ge(*consumed(key))
                for i in range(2):
                    A(dst[:, 2 * i:2 * i + 2], bank(banks[i]).rearrange("p (j t) -> p j t", j=2), function
                      ).then_inc(*S("gate_act").up(key, i))

            def second(l):
                Sa, Sp, Sv = S("second_act"), S("second_pe"), S("second_dve")
                for a in range(TT):
                    act.wait_ge(*(Sv.at("residual", l - 1, a) if l else S("post_dve").at("h", 1, 1, 1)))
                    if l and a == 0:
                        act.wait_ge(*consumed(("out", l - 1, 1)))
                    A(xn_tok[:, a], h[:, a], ACT.Square, accum_out=at2["stat"][:, 40 + a:41 + a]).then_inc(*Sa.up("square", l, a))
                act.wait_ge(*Sa.at("square", l, 1))
                A(at2["stat"][:, 42:44], at2["stat"][:, 40:42], ACT.Sqrt, scale=1.0 / D, bias=T1("eps")).then_inc(*Sa.up("root", l))
                turned(f"sec{l}", s2["ht"], lambda k: PC(f"norm_g{l}", k), None)
                for n in range(4):
                    act.wait_ge(*consumed(("in", l, "rkv", n) if n < 3 else ("in", l, "lora")))
                    act.wait_ge(*Sv.at("edge", l, n % 2))
                    if n >= 2:
                        act.wait_ge(*Sv.at("mixed", l, n - 2))
                    if n < 3:
                        src = ps_t[:, 2 * n * HALF:(2 * n + 2) * HALF].rearrange("p (j t) -> p j t", j=4)
                        A(s2["raw"][:, n % 2, :, 1:257], src, ACT.Copy).then_inc(*Sa.up("raw", l, n))
                    else:
                        A(s2["raw"][:, 1, 0, 1:257], bank(6, T), ACT.Copy).then_inc(*Sa.up("raw", l, n))
                act.wait_ge(*Sv.at("mixed", l, 3))
                A(s2["wal"][0:64], s2["wal"][0:64], ACT.Tanh).then_inc(*Sa.up("tanh", l))
                if l:
                    act.wait_ge(*Sp.at("v_down"))
                    A(s2["vd"][0:32], bank(2, T)[0:32], ACT.Copy).then_inc(*Sa.up("v_down"))
                    for j in range(4):
                        act.wait_ge(*Sp.at("v_up"))
                        A(s2["nu"][:, j], bank(4 + j // 2)[:, j % 2 * T:j % 2 * T + T], ACT.Sigmoid, bias=PC("v0", j)
                          ).then_inc(*Sa.up("nu", j))
                for p in range(2):
                    recurrence(l, p)
                attention_parts(l)

            def recurrence(l, p):
                Sa, Sp, Sv, So = S("rwkv_act"), S("rwkv_pe"), S("rwkv_dve"), S("rwkv_pool")
                K = (l, p)
                act.wait_ge(*Sp.at("lora", *K))
                if p or l:
                    act.wait_ge(*Sv.at("o", *((l, p - 1) if p else (l - 1, 1))))
                if p == 0:
                    act.wait_ge(*(S("second_dve").at("blend", 1) if l else S("second_dve").at("mixed", 0, 3)))
                for jj in range(2):
                    A(rw["lw"][:, jj * T:jj * T + T], bank(0)[:, jj * T:jj * T + T], ACT.Sigmoid, bias=PC(f"w0{l}", 2 * p + jj)
                      ).then_inc(*Sa.up("w", *K, jj))
                    A(rw["a"][:, jj * T:jj * T + T], bank(1)[:, jj * T:jj * T + T], ACT.Sigmoid, bias=PC(f"a0{l}", 2 * p + jj)
                      ).then_inc(*Sa.up("a", *K, jj))
                act.wait_ge(*Sv.at("kk0", *K, 1))
                A(rw["tmp"], rw["kk"], ACT.Square).then_inc(*Sa.up("kk_sq", *K))
                act.wait_ge(*Sp.at("kk_sum", *K))
                A(rw["tmp"], bank(2), ACT.Sqrt).then_inc(*Sa.up("kk_root", *K))
                act.wait_ge(*Sv.at("exponents", *K))
                A(rw["eLm"], rw["eLm"], ACT.Exp).then_inc(*Sa.up("eLm", *K))
                A(rw["eN"], rw["L"], ACT.Exp, scale=-1.0).then_inc(*Sa.up("eN", *K))
                A(rw["eL"], rw["L"], ACT.Exp).then_inc(*Sa.up("eL", *K))
                A(rw["eH"], rw["eH"], ACT.Exp).then_inc(*Sa.up("eH", *K))
                if p == 0:
                    open_gate(("in", l, "gate_c"), (4, 5), ACT.Silu, s2["oc"])
                else:
                    open_gate(("in", l, "merge", 0, 0), (4, 5), ACT.Sigmoid, merge_gate[0][:, 0:4])
                for i, (n, c) in enumerate((("v_tok", 0), ("bh_tok", 0), ("kh_tok", 0), ("wk", 64))):
                    act.wait_ge(*Sp.at("tok", *K, i))
                    for hh in range(2):
                        A(rw[n][:, 4 * hh:4 * hh + 4, c:c + 64],
                          bank(4 + i).rearrange("p (r h c) -> p r h c", r=4, h=2)[:, :, hh], ACT.Copy
                          ).then_inc(*Sa.up("tok", *K, i, hh))
                for n in range(1, LEVELS):
                    for hh in range(2):
                        act.wait_ge(*Sp.at("step", *K, n, hh))
                        A(rw["prod"][:, 4 * hh:4 * hh + 4], bank(2 + hh).rearrange("p (q n) -> p q n", q=4), ACT.Copy
                          ).then_inc(*Sa.up("step", *K, n, hh))
                act.wait_ge(*Sp.at("w1", *K))
                A(rw["wk"][:, :, 0:64], bank(0).rearrange("p (q n) -> p q n", q=8), ACT.Copy).then_inc(*Sa.up("w1", *K))
                act.wait_ge(*Sp.at("y0", *K))
                A(rw["y"], bank(4).rearrange("p (j t) -> p j t", j=2), ACT.Copy).then_inc(*Sa.up("y0", *K))
                act.wait_ge(*Sp.at("pm", *K))
                A(rw["pm"][:, 1:4:2], bank(6, 256).rearrange("p (c j n) -> p c j n", c=2, j=2), ACT.Copy
                  ).then_inc(*Sa.up("pm", *K, 0))
                A(rw["pm"][:, 2], bank(7, 128).rearrange("p (j n) -> p j n", j=2), ACT.Copy).then_inc(*Sa.up("pm", *K, 1))
                act.wait_ge(*Sp.at("carried", *K))
                A(rw["carried"][:, 0:3:2],
                  bank(0, 256).rearrange("p (c j n) -> p c j n", c=2, j=2), ACT.Copy).then_inc(*Sa.up("carried", *K, 0))
                A(rw["carried"][:, 1], bank(1, 128).rearrange("p (j n) -> p j n", j=2), ACT.Copy).then_inc(*Sa.up("carried", *K, 1))
                act.wait_ge(*Sv.at("centred", *K))
                A(rw["tmp2"], rw["y"].rearrange("p j t -> p (j t)"), ACT.Square).then_inc(*Sa.up("gn_sq", *K))
                act.wait_ge(*Sp.at("gn_sum", *K))
                A(rw["tmp2"], bank(5), ACT.Sqrt, scale=1.0 / 64, bias=T1("gn_eps")).then_inc(*Sa.up("gn_root", *K))
                if p == 0:
                    open_gate(("in", l, "gate_a"), (0, 1), ACT.Silu, at2["oa"])

            def attention_parts(l):
                Sa, Sp, Sv = S("second_act"), S("second_pe"), S("second_dve")

                def norm2(i):
                    u = ("sec", l, i)
                    r0, r1, n, width, b, _ = unit(l, i)
                    act.wait_ge(*unit_ready(l, i))
                    if before(u):
                        act.wait_ge(*S("norm_pe").at("sum", before(u)))
                    if i == 0:
                        act.wait_ge(*S("rwkv_dve").at("o", l, 1))
                    A(at2["sq"][r0:r1, 0:n], unit_source(l, i), ACT.Square).then_inc(*S("norm_act").up("sq", u))
                    act.wait_ge(*S("norm_pe").at("sum", u))
                    if before(u):
                        act.wait_ge(*S("norm_dve").at("rs", before(u)))
                    m = T if i == 0 else n
                    A(at2["sd"][r0:r1, 0:m], bank(2, m)[r0:r1], ACT.Sqrt, scale=1.0 / width, bias=T1("eps")[r0:r1]
                      ).then_inc(*S("norm_act").up("sd", u))

                for i in range(11):
                    norm2(i)
                    if i == 6:
                        open_gate(("in", l, "merge", 0, 1), (3, 1), ACT.Sigmoid, merge_gate[0][:, 4:8])
                attention2(l, 0)
                for i in range(11, 15):
                    norm2(i)
                act.wait_ge(*Sp.at("ff", l))
                A(at2["ff"][0:8, 0], bank(7, T)[0:8], ACT.Abs, bias=PC(f"fb{l}", 0, 8)).then_inc(*Sa.up("abs", l))
                act.wait_ge(*Sa.at("abs", l))
                A(at2["ff"][0:8, 0], at2["ff"][0:8, 0], ACT.Exp, scale=-1.0).then_inc(*Sa.up("exp", l))
                act.wait_ge(*Sa.at("exp", l))
                A(at2["ff"][0:8, 0], at2["ff"][0:8, 0], ACT.Ln, bias=1.0).then_inc(*Sa.up("log", l))
                open_gate(("in", l, "ff_gate_b"), (0, 1), ACT.Silu, at2["ob"])
                attention2(l, 1)

            def attention2(l, br):
                Sa, Sp, Sv = S("att_act"), S("att_pe"), S("att_dve")
                st = at2["stat"]
                for u in range(9):
                    if u < 8:
                        act.wait_ge(*Sv.at("max", 1, l, br, u))
                        if u >= 2:
                            act.wait_ge(*Sp.at("turned", 1, l, br, u - 2))
                        for a in range(TT):
                            o, n = (0, P) if a == 0 else (P, 2 * P)
                            A(at2["prob"][:, u % 2, o:o + n], at2["score"][:, u % 2, o:o + n], ACT.Exp,
                              bias=st[:, 4 * (u % 2) + a:4 * (u % 2) + a + 1],
                              accum_out=st[:, 8 + 4 * (u % 2) + a:9 + 4 * (u % 2) + a]).then_inc(*Sa.up("exp", 1, l, br, u, a))
                    if u >= 1:
                        v = u - 1
                        act.wait_ge(*Sp.at("turned", 1, l, br, v))
                        if v >= 2:
                            act.wait_ge(*Sp.at("value", 1, l, br, v - 2))
                        A(at2["prob_t"][:, v % 2], bank(5 + v % 2, 384), ACT.Copy).then_inc(*Sa.up("prob_t", 1, l, br, v))
                    if u >= 3 and u % 2 or u == 8:
                        q = (u - 2) // 2 if u < 8 else 3
                        act.wait_ge(*(consumed(("in", l, "merge", br + 1, q // 2)) if q % 2 else Sp.at("filled", l, br, q)))
                        A(merge_gate[br + 1][:, 2 * q:2 * q + 2], bank((7, 2)[q % 2]).rearrange("p (j t) -> p j t", j=2),
                          ACT.Sigmoid).then_inc(*S("gate_act").up("merge", l, br + 1, q))

            condition()
            for j in range(12):
                mod_part(0, j)
                if j == LATE:
                    act.dma_start(m0["xc"], w["ctx"][0].rearrange("(a p) d -> p a d", p=P)).then_inc(loaded("ctx")[0], 16)
                    act.dma_start(tab2[:, 0:n_first], w["tables_first"]).then_inc(loaded("tables_first")[0], 16)
                    act.dma_start(small_t[:, 0:512].rearrange("p (g d) -> p g d", g=4),
                                  w["w_pool_grp"][0].rearrange("g c d -> c g d")).then_inc(loaded("small")[0], 16)
            turned("ctx", m0["uc"], lambda k: modcol[:, 0, 1, k, 1:2], lambda k: modcol[:, 0, 0, k, 1:2])
            turned("mix0", m0["ut"], lambda k: modcol[:, 0, 1, k, 0:1], lambda k: modcol[:, 0, 0, k, 0:1])
            for u in range(4):
                norm(("first", u), consumed(("mix_in", u // 2)), bank((0, 1, 3, 4)[u]), P, 512, 64, m0)
            attention0()
            for g in range(4):
                act.wait_ge(*S("pool_pe").at("mean", g))
                A(m0["pooled"][:, g], bank(4 + g % 2, T), ACT.Copy).then_inc(*S("pool_act").up("mean", g))
            post_norm(0, 0)
            turned("ffn0", ff["ut"], lambda k: modcol[:, 0, 3, k, 0:1], lambda k: modcol[:, 0, 2, k, 0:1])
            ffn(0)
            post_norm(0, 1)
            turned("mix1", m1["ut"], lambda k: modcol[:, 1, 1, k, 0:1], lambda k: modcol[:, 1, 0, k, 0:1])
            for j in range(8):
                act.wait_ge(*consumed(("conv_in", 2 + j // 4)))
                A(m1["c"][:, j], bank(j % 4 // 2)[:, j % 2 * T:j % 2 * T + T], ACT.Copy
                  ).then_inc(*S("conv_act").up("c", j))
            post_norm(1, 0)
            turned("ffn1", ff["ut"], lambda k: modcol[:, 1, 3, k, 0:1], lambda k: modcol[:, 1, 2, k, 0:1])
            ffn(1)
            post_norm(1, 1)
            second(0)
            second(1)

        @block.tensor
        def _(pe):
            M = nc.tensor.matmul

            def mod_fold(l, j):
                m, half = j // 2, j % 2
                pe.wait_ge(*S("mod_act").at("part", l, j))
                if m in (2, 5):
                    if j > 4:
                        pe.wait_ge(*S("mod_dve").at("gate", l, {5: 4, 10: 5, 11: 10}[j]))
                    mm = M(bank(2), T1("sum_row0"), md["part"][:, half], start=True, stop=True)
                else:
                    c = (m if m < 2 else m - 1)
                    for i in range(4):
                        o = (c * KD + half * 4 + i) * 2
                        mm = M(ps_t[:, HALF + o:HALF + o + 2], md["part"][:, half, i * P:(i + 1) * P],
                               T1("sum_cols"), start=True, stop=True)
                mm.then_inc(*S("mod_pe").up("fold", l, j))

            def mod_chunk(l, j):
                key = ("mod", l, j)
                pe.wait_ge(*has_landed(key))
                before = j - 2 if l == 0 else j - 1
                if before >= 0:
                    pe.wait_ge(*S("mod_act").at("part", l, before))
                for k in range(KD):
                    o = k % 4 * 32
                    mm = M(bank(mod_bank(l, j))[o:o + 32], md["condT"][:, k], slot(key)[:, k], start=k < 4, stop=k >= 4,
                           tile_position=(0, o))
                mm.then_inc(used, 1)
                if j >= 1:
                    mod_fold(l, j - 1)

            def modulation(l):
                pe.wait_ge(*S("mod_dve").at("cond"))
                pe.wait_ge(*loaded("tables"))
                for j in range(12):
                    mod_chunk(l, j)
                mod_fold(l, 11)

            def turn(name, src, ready):
                pe.wait_ge(*ready)
                for pair in range(4):
                    for i in range(2):
                        for a in range(TT):
                            k = 2 * pair + i
                            mm = nc.tensor.transpose(bank(4 + pair)[:, i * T + a * P:i * T + a * P + P],
                                                     src[:, a, k * P:(k + 1) * P], T1("ident"))
                    mm.then_inc(*S("turn_pe").up(name, pair))

            def turned(name):
                pe.wait_ge(*S("turn_act").at(name, 5))
                pe.wait_ge(*S("turn_dve").at(name, 7))

            def project(dst, lhs, rhs, n=KD):
                for k in range(n):
                    mm = M(dst, lhs(k), rhs(k), start=k == 0, stop=k == n - 1)
                return mm

            def norm_sum(u, rows, n, bufs, weights="head_ones"):
                pe.wait_ge(*S("norm_act").at("sq", u))
                if u[-1] > 0:
                    pe.wait_ge(*S("norm_act").at("sd", u[:-1] + (u[-1] - 1,)))
                M(bank(2)[0:rows, 0:n], T1(weights)[0:rows, 0:rows], bufs["sq"][0:rows, 0:n], start=True, stop=True
                  ).then_inc(*S("norm_pe").up("sum", u))

            def norm_swap(u, last, rows, n, swap, bufs):
                pe.wait_ge(*S("norm_dve").at("xn", u))
                if last is not None:
                    pe.wait_ge(*S("norm_dve").at("t2", last))
                M(bank(7)[0:rows, 0:n], swap, bufs["xn"][0:rows, 0:n], start=True, stop=True
                  ).then_inc(*S("norm_pe").up("swap", u))

            def mixer0():
                ut, uc = m0["ut"], m0["uc"]
                pe.wait_ge(*S("mod_dve").at("columns", 0))
                pe.wait_ge(*loaded("ctx"))
                turn("ctx", m0["xc"], loaded("x"))
                turned("ctx")
                turn("mix0", h, loaded("x"))
                turned("mix0")
                key = ("mix_in", 0)
                pe.wait_ge(*has_landed(key))
                for j in range(4):
                    mm = project(bank(j // 2)[:, j % 2 * T:j % 2 * T + T], lambda k: slot(key)[:, k, j * P:(j + 1) * P],
                                 lambda k: ut[:, k])
                mm.then_inc(used, 1)
                key = ("mix_in", 1)
                pe.wait_ge(*has_landed(key))
                wkv = slot(key)
                pe.wait_ge(*loaded("tables_first"))
                nsum = lambda u: norm_sum(("first", u), P, 512, m0)
                nswap = lambda u: norm_swap(("first", u), ("first", u - 1) if u else None, P, T if u >= 2 else 512, T2("swap"), m0)
                for kv in range(2):
                    for o in (0, 64):
                        for i, u in enumerate((uc, ut)):
                            project(bank(3 + kv)[o:o + 64, i * T:(i + 1) * T], lambda k: wkv[:, k, 64 * kv:64 * kv + 64],
                                    lambda k: u[:, k])
                    if kv:
                        nswap(0)
                        nsum(1)
                    else:
                        nsum(0)
                for a in range(4):
                    u = uc if a < 2 else ut
                    mm = project(bank(5)[:, a * P:(a + 1) * P], lambda k: u[:, k, a % 2 * P:a % 2 * P + P],
                                 lambda k: wkv[:, k, P:2 * P])
                mm.then_inc(used, 1)
                nswap(1)
                nsum(2)
                key = ("mix_in", 2)
                pe.wait_ge(*has_landed(key))
                for a in range(TT):
                    if a == 1:
                        nswap(2)
                        nsum(3)
                        pe.wait_ge(*S("turn_dve").at("values"))
                    mm = project(bank(6 - a), lambda k: ut[:, k, a * P:(a + 1) * P], lambda k: slot(key)[:, k])
                mm.then_inc(used, 1)
                nswap(3)

            def attention0():
                Sa, Sp, Sv = S("att_act"), S("att_pe"), S("att_dve")
                pe.wait_ge(*S("norm_dve").at("out", ("first", 3)))
                pe.wait_ge(*S("turn_dve").at("pool_in", 1))
                for u in range(18):
                    if u < 16:
                        hd, a = u // 2, u % 2
                        o = 64 * (hd % 2)
                        if u >= 2:
                            pe.wait_ge(*Sa.at("exp", 0, u - 2))
                        M(bank(4 + u % 2), m0["q"][o:o + 64, hd // 2, a * P:(a + 1) * P], m0["k"][o:o + 64, hd // 4],
                          start=True, stop=True).then_inc(*Sp.up("score", 0, u))
                    if 2 <= u <= 13:
                        mod_chunk(1, u - 2)
                    if u == 14:
                        mod_fold(1, 11)
                    if 1 <= u <= 16:
                        v = u - 1
                        pe.wait_ge(*Sv.at("prob", 0, v))
                        if v >= 1:
                            pe.wait_ge(*Sa.at("prob_t", 0, v - 1))
                        for i in range(4):
                            mm = nc.tensor.transpose(bank(6)[:, i * P:(i + 1) * P], m0["prob"][:, v % 2, i * P:(i + 1) * P],
                                                     T1("ident"))
                        mm.then_inc(*Sp.up("turned", 0, v))
                    if u >= 2:
                        v = u - 2
                        hd = v // 2
                        pe.wait_ge(*Sa.at("prob_t", 0, v))
                        if v >= 2:
                            pe.wait_ge(*Sv.at("value", 0, v - 2))
                        o = 64 * (hd % 2)
                        for i in range(4):
                            mm = M(bank((7, 3)[v % 2])[o:o + 64, 0:P], m0["v"][:, i, 64 * (hd // 4):64 * (hd // 4) + 64],
                                   m0["prob_t"][:, v % 2, i * P:(i + 1) * P], start=i == 0, stop=i == 3)
                        mm.then_inc(*Sp.up("value", 0, v))

            def pool0():
                Sp = S("pool_pe")
                band = T2("band").rearrange("p (a g t) -> p a g t", a=TT, g=4)
                pe.wait_ge(*loaded("small"))
                wg = small_t[:, 0:512].rearrange("p (g d) -> p g d", g=4)

                def weights(g):
                    pe.wait_ge(*S("pool_act").at("mean", g))
                    if g >= 1:
                        pe.wait_ge(*S("pool_dve").at("out", g - 1))
                    M(bank(6, T), wg[:, g], m0["pooled"][:, g], start=True, stop=True).then_inc(*Sp.up("out", g))

                for g in range(4):
                    if g >= 2:
                        pe.wait_ge(*S("pool_act").at("mean", g - 2))
                    for a in range(TT):
                        mm = M(bank(4 + g % 2, T), m0["pt"][:, a, g * P:(g + 1) * P], band[:, a, g],
                               start=a == 0, stop=a == 1)
                    mm.then_inc(*Sp.up("mean", g))
                    if g >= 1:
                        weights(g - 1)
                weights(3)

            def mix_out(l, mix, *ready):
                for r in ready:
                    pe.wait_ge(*r)
                for j in range(2):
                    key = ("mix_out", l, j)
                    pe.wait_ge(*has_landed(key))
                    for a in range(TT):
                        mm = project(bank(2 * a + j), lambda k: mix[:, k, a * P:(a + 1) * P], lambda k: slot(key)[:, k])
                    mm.then_inc(used, 1)

            def mixer1():
                ut = m1["ut"]
                pe.wait_ge(*S("mod_dve").at("columns", 1))
                turn("mix1", h, S("post_dve").at("h", 0, 1, 1))
                turned("mix1")
                for n, j in enumerate((2, 4, 3, 5, 0, 1)):
                    key = ("conv_in", j)
                    pe.wait_ge(*has_landed(key))
                    if n == 2:
                        pe.wait_ge(*S("conv_act").at("c", 3))
                    if n == 3:
                        pe.wait_ge(*S("conv_dve").at("z", 3))
                    if n == 4:
                        pe.wait_ge(*S("conv_act").at("c", 7))
                    if n == 5:
                        pe.wait_ge(*S("conv_dve").at("z", 7))
                    b0 = (0, 2, 0, 2, 0, 2)[n]
                    for i in range(4):
                        mm = project(bank(b0 + i // 2)[:, i % 2 * T:i % 2 * T + T],
                                     lambda k: slot(key)[:, k, i * P:(i + 1) * P], lambda k: ut[:, k])
                    mm.then_inc(used, 1)

            def ffn(l):
                Sa, Sp, Sv = S("ffn_act"), S("ffn_pe"), S("ffn_dve")
                pe.wait_ge(*loaded("router", l + 1))
                router = small_t[:, 512:640].rearrange("p (k e) -> p k e", k=KD)
                turned(f"ffn{l}")
                for a in range(TT):
                    mm = project(bank(0)[:, a * E:(a + 1) * E], lambda k: ff["ut"][:, k, a * P:(a + 1) * P], lambda k: router[:, k])
                mm.then_inc(*Sp.up("logits", l))
                pe.wait_ge(*Sv.at("share", l, 1))
                for a in range(TT):
                    mm = nc.tensor.transpose(bank(1)[0:E, a * P:(a + 1) * P], ff["ex"][:, a], T1("ident"))
                mm.then_inc(*Sp.up("shares", l))
                pe.wait_ge(*Sv.at("spread", l))
                M(bank(0), T1("ones")[0:E], ff["di"][0:E], start=True, stop=True).then_inc(*Sp.up("rows", l))
                for g in range(NG):
                    M(ps_t[:, HALF + g:HALF + g + 1], ff["di"][0:E, g * EG:(g + 1) * EG], T1("ones")[0:E, 0:1],
                      start=True, stop=True)
                pe.wait_ge(*Sv.at("spread_gates", l))
                for g in range(NG):
                    mm = M(ps_t[:, HALF + 4 + g:HALF + 5 + g], ff["dg"][0:E, g * EG:(g + 1) * EG], T1("ones")[0:E, 0:1],
                           start=True, stop=True)
                mm.then_inc(*Sp.up("cols", l))
                Sx, Sax, Svx, Spl = (S(f"expert{l}_{e}") for e in ("pe", "act", "dve", "pool"))
                base = number[("expert", l, 0)]

                def streamed(g, m, k):
                    i = base + m * KD + k
                    pe.wait_ge(landed[i % RING], g * (16 * 3 * KD // RING) + 16 * (i // RING + 1))
                    return ring[:, i % RING * SLOT:i % RING * SLOT + EG * D].rearrange("p (e f) -> p e f", e=EG)

                def products(b, x, k, wk):
                    for half in range(2):
                        for e in range(EG):
                            mm = M(bank(b + half)[32 * e:32 * e + 32], x[:, k, 32 * e:32 * e + 32],
                                   wk[:, e, half * HALF:(half + 1) * HALF], start=k == 0, stop=k == KD - 1,
                                   tile_position=(0, 32 * e))
                    return mm

                Sx.open_loop()
                with pe.Fori(0, NG) as g:
                    pe.wait_ge(*Spl.turn(g, "pick"))
                    for k in range(KD):
                        for a in range(TT):
                            mm = M(bank(6 + k // 4)[:, k % 4 * P:k % 4 * P + P], h[:, a, k * P:(k + 1) * P], ff["pick_g"][:, a],
                                   start=a == 0, stop=a == 1)
                        if k % 4 == 3:
                            mm.then_inc(*Sx.up("gather", k // 4))
                    pe.wait_ge(*Sax.turn(g, "xg", 3))
                    pe.wait_ge(*Svx.turn(g, "xg", 7))
                    for m in range(2):
                        for k in range(KD):
                            mm = products(2 * m, ff["xg"], k, streamed(g, m, k))
                            mm.then_inc(used, 1)
                    for b in range(2):
                        pe.wait_ge(*Svx.turn(g, "hidden", b))
                        for i in range(4):
                            k = 4 * b + i
                            mm = nc.tensor.transpose(bank(6 + b)[:, i * P:(i + 1) * P], ff["hg"][:, k * P:(k + 1) * P],
                                                     T1("ident"))
                        mm.then_inc(*Sx.up("turned", b))
                    for k in range(KD):
                        if k % 4 == 0:
                            pe.wait_ge(*Sax.turn(g, "ht", k // 4))
                        mm = products(4, ff["ht"], k, streamed(g, 2, k))
                        mm.then_inc(used, 1)
                    pe.wait_ge(*Svx.turn(g, "ye"))
                    pe.wait_ge(*Spl.turn(g, "put"))
                    for half in range(2):
                        for a in range(TT):
                            mm = M(bank(2 * a + half), ff["put_g"][:, a * P:(a + 1) * P], ff["ye"][:, half * HALF:(half + 1) * HALF],
                                   start=True, stop=True)
                        mm.then_inc(*Sx.up("y", half))
                Sx.close_loop(NG)

            def gate_tile(key, banks, i):
                if i == 0:
                    pe.wait_ge(*has_landed(key))
                lhs0 = 8 if key[2] == "ff_gate_b" else 0
                mm = project(bank(banks[i // 2])[:, i % 2 * T:i % 2 * T + T],
                             lambda k: slot(key)[:, k, lhs0 + i * P:lhs0 + (i + 1) * P], lambda k: s2["ht"][:, k])
                if i == 3:
                    mm.then_inc(used, 1)
                return mm

            def second(l):
                Sa, Sp, Sv = S("second_act"), S("second_pe"), S("second_dve")
                ht = s2["ht"]
                if l == 0:
                    pe.wait_ge(*S("post_dve").at("t", 1, 1, 1))
                turn(f"sec{l}", xn_tok, Sv.at("normed", l, 1))
                turned(f"sec{l}")

                def tiles(key, banks, lhs0=0, n=4):
                    for i in range(n):
                        mm = project(bank(banks[i // 2])[:, i % 2 * T:i % 2 * T + T],
                                     lambda k: slot(key)[:, k, lhs0 + i * P:lhs0 + (i + 1) * P], lambda k: ht[:, k])
                    return mm

                for n in range(3):
                    key = ("in", l, "rkv", n)
                    pe.wait_ge(*has_landed(key))
                    tiles(key, (2 * n, 2 * n + 1)).then_inc(used, 1)
                key = ("in", l, "lora")
                pe.wait_ge(*has_landed(key))
                tiles(key, (6,), n=1).then_inc(used, 1)
                pe.wait_ge(*loaded("small2", 3 * l + 3))
                lora = small_t[:, 0:512]
                if l:
                    pe.wait_ge(*Sv.at("mixed", 1, 2))
                    pe.wait_ge(*Sa.at("raw", 1, 2))
                    vdw = small_t[:, 512:640].rearrange("p (k n) -> p k n", k=4)
                    project(bank(2, T)[0:32], lambda k: vdw[:, k], lambda k: s2["rkv"][:, 2, k], 4).then_inc(*Sp.up("v_down"))
                    pe.wait_ge(*Sa.at("v_down"))
                    for j in range(4):
                        mm = M(bank(4 + j // 2)[:, j % 2 * T:j % 2 * T + T], small_t[0:32, 640 + j * P:640 + (j + 1) * P],
                               s2["vd"][0:32], start=True, stop=True)
                    mm.then_inc(*Sp.up("v_up"))
                for p in range(2):
                    recurrence(l, p, lora, ht)
                attention_parts(l, tiles)

            def recurrence(l, p, lora, ht):
                Sa, Sp, Sv, So = S("rwkv_act"), S("rwkv_pe"), S("rwkv_dve"), S("rwkv_pool")
                K = (l, p)
                pairs = [(tt, jj) for tt in range(2) for jj in range(2)]
                pe.wait_ge(*S("second_act").at("tanh", l))
                if l:
                    pe.wait_ge(*S("second_act").at("nu", 3))
                if p:
                    pe.wait_ge(*Sv.at("o", l, 0))
                    pe.wait_ge(*S("gate_act").at(("in", l, "gate_a"), 1))
                for o, b in ((0, 0), (64, 1)):
                    for jj in range(2):
                        mm = M(bank(b)[:, jj * T:jj * T + T], lora[o:o + 64, (2 * p + jj) * P:(2 * p + jj + 1) * P],
                               s2["wal"][o:o + 64], start=True, stop=True)
                mm.then_inc(*Sp.up("lora", *K))
                gate = ("in", l, "merge", 0, 0) if p else ("in", l, "gate_c")
                gate_tile(gate, (4, 5), 0)
                pe.wait_ge(*Sa.at("kk_sq", *K))
                M(bank(2), T1("head_ones"), rw["tmp"], start=True, stop=True).then_inc(*Sp.up("kk_sum", *K))
                for i in range(1, 4):
                    gate_tile(gate, (4, 5), i)
                pe.wait_ge(*Sv.at("rk", *K, 1))
                pe.wait_ge(*Sa.at("kk_root", *K))
                M(bank(3), T1("head_ones"), rw["tmp"], start=True, stop=True).then_inc(*Sp.up("rk_sum", *K))
                src = (lambda tt, jj: s2["rkv"][:, 2, 2 * p + jj, tt * P:(tt + 1) * P],
                       lambda tt, jj: rw["bh"][:, jj, tt * P:(tt + 1) * P],
                       lambda tt, jj: rw["kh"][:, jj, tt * P:(tt + 1) * P],
                       lambda tt, jj: rw["kr"][:, jj, tt, 0])
                if l:
                    pe.wait_ge(*S("second_dve").at("blend", 1))
                pe.wait_ge(*So.at("hats", *K, 1))
                pe.wait_ge(*Sv.at("bt", *K))
                pe.wait_ge(*S("gate_act").at(gate, 1))
                for i in range(4):
                    for r, (tt, jj) in enumerate(pairs):
                        mm = nc.tensor.transpose(bank(4 + i)[:, r * P:(r + 1) * P], src[i](tt, jj), T1("ident"))
                    mm.then_inc(*Sp.up("tok", *K, i))
                pe.wait_ge(*Sv.at("kt", *K))
                pe.wait_ge(*Sa.at("a", *K, 1))
                pe.wait_ge(*Sv.at("bonus", *K))
                for n, x, b in (("gram_b", "bt", 0), ("gram_k", "kt", 4)):
                    if b:
                        pe.wait_ge(*Sa.at("tok", *K, 3, 1))
                    for r, (tt, jj) in enumerate(pairs):
                        for hh in range(2):
                            o = 64 * hh
                            mm = M(bank(b + 2 * hh + r // 2)[:, r % 2 * 256:r % 2 * 256 + 256],
                                   rw[x][o:o + 64, jj, tt * P:(tt + 1) * P],
                                   rw["kr"][o:o + 64, jj, tt].rearrange("p x n -> p (x n)"), start=True, stop=True)
                    mm.then_inc(*Sp.up(n, *K))
                pe.wait_ge(*Sv.at("gb", *K, 1))
                for r, (tt, jj) in enumerate(pairs):
                    for hh in range(2):
                        o = 64 * hh
                        mm = M(bank(hh)[:, r * P:(r + 1) * P], rw["kr"][o:o + 64, jj, tt, 0], rw["bt"][o:o + 64, jj, tt * P:(tt + 1) * P],
                               start=True, stop=True)
                mm.then_inc(*Sp.up("gram_a", *K))
                inv, inv_t, prod = rw["inv"], rw["inv_t"], rw["prod"]
                for n in range(1, LEVELS):
                    pe.wait_ge(*So.at("level", *K, n))
                    for hh in range(2):
                        pe.wait_ge(*Sv.at("inv", *K, n - 1, hh))
                        for q in range(4 * hh, 4 * hh + 4):
                            mm = M(bank(2 + hh)[:, q % 4 * P:q % 4 * P + P], rw[f"lev{n % 2}"][:, q], inv[:, q],
                                   start=True, stop=True)
                        mm.then_inc(*Sp.up("step", *K, n, hh))
                    for hh in range(2):
                        pe.wait_ge(*Sa.at("step", *K, n, hh))
                        pe.wait_ge(*Sv.at("inv_t", *K, n - 1, hh))
                        if n < LEVELS - 1:
                            for q in range(4 * hh, 4 * hh + 4):
                                mm = M(bank(4 + hh)[:, q % 4 * P:q % 4 * P + P], inv_t[:, q], prod[:, q], start=True, stop=True)
                            mm.then_inc(*Sp.up("inv", *K, n, hh))
                        for q in range(4 * hh, 4 * hh + 4):
                            mm = M(bank(6 + hh)[:, q % 4 * P:q % 4 * P + P], prod[:, q], inv_t[:, q], start=True, stop=True)
                        mm.then_inc(*Sp.up("inv_t", *K, n, hh))
                vt, bht, kht, gh, wk = rw["v_tok"], rw["bh_tok"], rw["kh_tok"], rw["prod"], rw["wk"]
                pe.wait_ge(*Sv.at("gk", *K, 1))
                for q in range(8):
                    mm = M(bank(0)[:, q * 64:q * 64 + 64], rw["gk"][:, q, 0:P], vt[:, q], start=True, stop=True)
                mm.then_inc(*Sp.up("w1", *K))
                pe.wait_ge(*Sa.at("w1", *K))
                for hh in range(2):
                    pe.wait_ge(*Sv.at("inv_t", *K, LEVELS - 1, hh))
                    for q in range(4 * hh, 4 * hh + 4):
                        mm = M(bank(2 + hh)[:, q % 4 * P:q % 4 * P + P], inv_t[:, q], wk[:, q], start=True, stop=True)
                    mm.then_inc(*Sp.up("gh", *K, hh))
                pe.wait_ge(*Sv.at("gh", *K, 1))
                for r, (tt, jj) in enumerate(pairs):
                    for hh in range(2):
                        q, o, c = 4 * hh + r, 64 * hh, jj * T + tt * P
                        M(bank(4)[o:o + 64, c:c + P], gh[:, q, 0:64], rw["gb"][:, q, P:2 * P], start=True, stop=False)
                        M(bank(4)[o:o + 64, c:c + P], vt[:, q], rw["gk"][:, q, P:2 * P], start=False, stop=True)
                        mm = M(bank(5)[o:o + 64, c:c + P], gh[:, q, 64:P], rw["gb"][:, q, P:2 * P], start=True, stop=True)
                mm.then_inc(*Sp.up("y0", *K))
                for c in (1, 3, 2):
                    tt, o = c // 2, 64 * (c % 2)
                    for jj in range(2):
                        for hh in range(2):
                            q, oo = 4 * hh + 2 * tt + jj, 64 * hh
                            x = (c // 2 * 2 + jj) * 64 if c % 2 else jj * 64
                            mm = M(bank(6 if c % 2 else 7)[oo:oo + 64, x:x + 64], gh[o:o + 64, q, 64:P], bht[o:o + 64, q],
                                   start=True, stop=True)
                mm.then_inc(*Sp.up("pm", *K))
                for c in (0, 2, 1):
                    tt, o = c // 2, 64 * (c % 2)
                    for jj in range(2):
                        for hh in range(2):
                            q, oo = 4 * hh + 2 * tt + jj, 64 * hh
                            x = jj * 64 if c % 2 else (c // 2 * 2 + jj) * 64
                            b = bank(1 if c % 2 else 0)[oo:oo + 64, x:x + 64]
                            M(b, bht[o:o + 64, q], gh[o:o + 64, q, 0:64], start=True, stop=False)
                            mm = M(b, kht[o:o + 64, q], vt[o:o + 64, q], start=False, stop=True)
                mm.then_inc(*Sp.up("carried", *K))
                st = rw["state"]

                def fill(i):
                    if p == 0:
                        gate_tile(("in", l, "gate_a"), (0, 1), i)
                        return
                    key = ("in", l, "latent")
                    if i == 0:
                        pe.wait_ge(*has_landed(key))
                    if i < 2:
                        project(bank(0)[:, i * T:i * T + T], lambda k: slot(key)[:, k, i * P:(i + 1) * P], lambda k: ht[:, k])
                    elif i == 2:
                        project(bank(1, T), lambda k: slot(key)[:, k, C_KV:K_R], lambda k: ht[:, k])
                    else:
                        project(bank(7)[64:96, T:2 * T], lambda k: slot(key)[:, k, K_R:G_A], lambda k: ht[:, k]).then_inc(used, 1)

                pe.wait_ge(*Sv.at("z", *K))
                pe.wait_ge(*Sa.at("pm", *K, 1))
                pe.wait_ge(*Sa.at("carried", *K, 1))
                for c in range(1, 4):
                    pe.wait_ge(*Sv.at("state", *K, c))
                    if c < 3:
                        for jj in range(2):
                            for hh in range(2):
                                o = 64 * hh
                                mm = M(bank(6 + hh)[o:o + 64, jj * 64:jj * 64 + 64], rw["pm"][o:o + 64, c, jj],
                                       st[o:o + 64, c, jj], start=True, stop=True)
                        mm.then_inc(*Sp.up("move", *K, c))
                    for jj in range(2):
                        for hh in range(2):
                            o = 64 * hh
                            x = jj * T + c * CH
                            mm = M(bank(2 + hh)[o:o + 64, x:x + CH], st[o:o + 64, c, jj], rw["z"][o:o + 64, jj, c * CH:(c + 1) * CH],
                                   start=True, stop=True)
                    if c < 3:
                        fill(c - 1)
                mm.then_inc(*Sp.up("read", *K))
                fill(2)
                pe.wait_ge(*Sv.at("y", *K))
                M(bank(4), T1("head_ones"), rw["y"].rearrange("p j t -> p (j t)"), start=True, stop=True
                  ).then_inc(*Sp.up("gn_mean", *K))
                fill(3)
                pe.wait_ge(*Sa.at("gn_sq", *K))
                M(bank(5), T1("head_ones"), rw["tmp2"], start=True, stop=True).then_inc(*Sp.up("gn_sum", *K))

            def attention_parts(l, tiles):
                Sa, Sp, Sv = S("second_act"), S("second_pe"), S("second_dve")
                Nd = S("norm_dve")
                ht = s2["ht"]
                pe.wait_ge(*S("rwkv_dve").at("o", l, 1))

                def norm2(i):
                    u = ("sec", l, i)
                    r0, r1, n, _, _, ones = unit(l, i)
                    pe.wait_ge(*S("norm_act").at("sq", u))
                    if before(u):
                        pe.wait_ge(*S("norm_act").at("sd", before(u)))
                    wt = T1(ones)[r0:r1, 0:r1 - r0]
                    if i == 0:
                        M(bank(2, T), wt, at2["sq"][:, 0:T], start=True, stop=False)
                        mm = M(bank(2, T), wt, at2["sq"][:, T:2 * T], start=False, stop=True)
                    else:
                        mm = M(bank(2, n)[r0:r1], wt, at2["sq"][r0:r1, 0:n], start=True, stop=True)
                    mm.then_inc(*S("norm_pe").up("sum", u))

                def swap2(i):
                    u = ("sec", l, i)
                    r0, r1, n = unit(l, i)[:3]
                    pe.wait_ge(*Nd.at("xn", u))
                    if i > 2:
                        pe.wait_ge(*Nd.at("t2", ("sec", l, i - 1)))
                    M(bank(7, n)[r0:r1], T2("swap", second_at)[r0:r1, r0:r1], at2["xn"][r0:r1, 0:n], start=True, stop=True
                      ).then_inc(*S("norm_pe").up("swap", u))

                gate = ("in", l, "merge", 0, 1)
                for i in range(3):
                    norm2(i)
                    if i < 2:
                        gate_tile(gate, (3, 1), i)
                key = ("uq", l)
                pe.wait_ge(*has_landed(key))
                pe.wait_ge(*Nd.at("out", ("sec", l, 0)))
                for hd in range(H2):
                    mm = project(bank((4, 5, 6, 0)[hd // 2])[0:96, hd % 2 * T:hd % 2 * T + T],
                                 lambda k: slot(key)[:, k, hd * 96:(hd + 1) * 96], lambda k: at2["cq"][:, k], 2)
                mm.then_inc(used, 1)
                swap2(2)
                norm2(3)
                for i in range(4, 7):
                    norm2(i)
                    swap2(i - 1)
                    if i < 6:
                        gate_tile(gate, (3, 1), i - 2)
                swap2(6)
                key = ("ukv", l)
                pe.wait_ge(*has_landed(key))
                pe.wait_ge(*Nd.at("out", ("sec", l, 6)))
                pe.wait_ge(*S("gate_act").at(gate, 1))
                wk = slot(key)[:, 0].rearrange("p (h n) -> p h n", h=H2)
                for hd in range(H2):
                    M(bank((1, 3, 4, 5)[hd // 2])[0:64, hd % 2 * T:hd % 2 * T + T], wk[:, hd, 0:64], at2["ckv"], start=True, stop=True)
                for a in range(TT):
                    mm = M(bank((6, 0)[a]), at2["ckv"][:, a * P:(a + 1) * P], wk[:, :, 64:P], start=True, stop=True)
                mm.then_inc(used, 1)
                for i in range(7, 11):
                    norm2(i)
                    if i in (7, 9):
                        merge_tile(l, 1, (i - 7) // 2)
                pe.wait_ge(*Nd.at("out", ("sec", l, 10)))
                pe.wait_ge(*Sv.at("values", l, 0, 1))
                attention2(l, 0)
                pe.wait_ge(*S("att_dve").at("value", 1, l, 0, 7))
                key = ("in", l, "fq")
                pe.wait_ge(*has_landed(key))
                tiles(key, (0, 1)).then_inc(used, 1)
                key = ("in", l, "fk")
                pe.wait_ge(*has_landed(key))
                tiles(key, (3,), n=2)
                norm2(11)
                for i in range(2, 4):
                    mm = project(bank(4)[:, i % 2 * T:i % 2 * T + T], lambda k: slot(key)[:, k, i * P:(i + 1) * P],
                                 lambda k: ht[:, k])
                mm.then_inc(used, 1)
                norm2(12)
                key = ("in", l, "fv")
                pe.wait_ge(*has_landed(key))
                for a in range(TT):
                    mm = project(bank(5 + a), lambda k: ht[:, k, a * P:(a + 1) * P], lambda k: slot(key)[:, k])
                    if a == 0:
                        norm2(13)
                mm.then_inc(used, 1)
                norm2(14)
                key = ("in", l, "ff_gate_b")
                pe.wait_ge(*has_landed(key))
                project(bank(7, T)[0:8], lambda k: slot(key)[:, k, 0:8], lambda k: ht[:, k]).then_inc(*Sp.up("ff", l))
                pe.wait_ge(*Nd.at("out", ("sec", l, 12)))
                for i in range(4):
                    gate_tile(key, (0, 1), i)
                pe.wait_ge(*Nd.at("out", ("sec", l, 14)))
                pe.wait_ge(*Sv.at("ncum", l))
                pe.wait_ge(*Sv.at("values", l, 1, 1))
                pe.wait_ge(*S("gate_act").at(key, 1))
                attention2(l, 1)
                outs = (at2["oa"], at2["ob"], s2["oc"])
                pe.wait_ge(*S("att_dve").at("value", 1, l, 1, 7))
                pe.wait_ge(*S("gate_act").at("merge", l, 2, 3))
                for b in range(3):
                    key = ("proj", l, b)
                    pe.wait_ge(*has_landed(key))
                    for i in range(KD):
                        if b == 2 and i % 2 == 0:
                            pe.wait_ge(*Sv.at("weighed", l, 0, i // 2))
                        mm = project(bank(4 * (b % 2) + i // 2)[:, i % 2 * T:i % 2 * T + T],
                                     lambda k: slot(key)[:, k, i * P:(i + 1) * P], lambda k: outs[b][:, k], 4)
                    mm.then_inc(used, 1)
                pe.wait_ge(*Sv.at("merged", l, 2, 3))
                for j in range(2):
                    key = ("out", l, j)
                    pe.wait_ge(*has_landed(key))
                    for a in range(TT):
                        mm = project(bank(2 * a + j), lambda k: merged[:, k, a * P:(a + 1) * P], lambda k: slot(key)[:, k])
                    mm.then_inc(used, 1)

            def merge_tile(l, b, n):
                q = n // 2
                key = ("in", l, "merge", b, n // 4)
                if n % 4 == 0:
                    pe.wait_ge(*has_landed(key))
                if n >= 4 and n % 2 == 0:
                    pe.wait_ge(*S("gate_act").at("merge", l, b, q - 2))
                mm = project(bank((7, 2)[q % 2])[:, n % 2 * T:n % 2 * T + T],
                             lambda k: slot(key)[:, k, n % 4 * P:(n % 4 + 1) * P], lambda k: s2["ht"][:, k])
                if n % 4 == 3:
                    mm.then_inc(used, 1)
                elif n % 4 == 1:
                    mm.then_inc(*S("att_pe").up("filled", l, b - 1, q))

            def attention2(l, br):
                Sa, Sp, Sv = S("att_act"), S("att_pe"), S("att_dve")
                for u in range(10):
                    if u < 8:
                        if u >= 2:
                            pe.wait_ge(*Sv.at("score", 1, l, br, u - 2))
                        if br == 0:
                            rows, j = slice(0, 96), u
                        else:
                            rows, j = slice(64 * (u % 2), 64 * (u % 2) + 64), u // 2
                        for a in range(TT):
                            n = (a + 1) * P
                            dst = bank(u % 2)[:, a * P:a * P + n]
                            mm = M(dst, at2["q"][rows, j, a * P:(a + 1) * P], at2["k"][rows, j, 0:n], start=True, stop=br == 0)
                            if br:
                                sel = T1("ident")[:, u:u + 1]
                                M(dst, at2["cum"][:, a * P:(a + 1) * P], sel.to_broadcast([P, n]), start=False, stop=False)
                                mm = M(dst, sel.to_broadcast([P, P]), at2["ncum"][:, 0:n], start=False, stop=True)
                        mm.then_inc(*Sp.up("score", 1, l, br, u))
                    if (1 if br else 3) <= u <= 8:
                        merge_tile(l, br + 1, u - 1)
                    if 1 <= u <= 8:
                        v = u - 1
                        pe.wait_ge(*Sv.at("prob", 1, l, br, v, 1))
                        if v >= 2:
                            pe.wait_ge(*Sa.at("prob_t", 1, l, br, v - 2))
                        for i in range(3):
                            mm = nc.tensor.transpose(bank(5 + v % 2)[:, i * P:(i + 1) * P], at2["prob"][:, v % 2, i * P:(i + 1) * P],
                                                     T1("ident"))
                        mm.then_inc(*Sp.up("turned", 1, l, br, v))
                    if u >= 2:
                        v = u - 2
                        o = 64 * (v % 2)
                        pe.wait_ge(*Sa.at("prob_t", 1, l, br, v))
                        if v >= 2:
                            pe.wait_ge(*Sv.at("value", 1, l, br, v - 2))
                        dst, pt = bank(3 + v % 2)[o:o + 64], at2["prob_t"][:, v % 2]
                        vals = lambda a: at2["v"][:, a, v * 64:v * 64 + 64]
                        M(dst[:, 0:P], vals(0), pt[:, 0:P], start=True, stop=True)
                        M(dst[:, P:2 * P], vals(0), pt[:, P:2 * P], start=True, stop=False)
                        M(dst[:, P:2 * P], vals(1), pt[:, 2 * P:3 * P], start=False, stop=True
                          ).then_inc(*Sp.up("value", 1, l, br, v))

            modulation(0)
            mixer0()
            attention0()
            pe.wait_ge(*S("att_dve").at("value", 0, 15))
            pool0()
            mix_out(0, m0["mix"], S("pool_dve").at("out", 3))
            turn("ffn0", h, S("post_dve").at("h", 0, 0, 1))
            ffn(0)
            mixer1()
            mix_out(1, m1["mix"], S("conv_dve").at("mix", 7))
            turn("ffn1", h, S("post_dve").at("h", 1, 0, 1))
            ffn(1)
            second(0)
            second(1)

        @block.vector
        def _(ve):
            V = nc.vector

            def condition():
                Sv = S("mod_dve")
                V.memset(md["condT"], 0.0).then_inc(*Sv.up("zero"))
                ve.wait_ge(*Sv.at("zero"))
                ve.wait_ge(*S("mod_act").at("sigmoid"))
                o = par_at["cond"][0]
                V.tensor_tensor(md["condT"][:, :, 0:2], par[:, o:o + 16].rearrange("p (c k) -> p k c", c=2),
                                md["sig"].rearrange("p (c k) -> p k c", c=2), ALU.mult).then_inc(*Sv.up("cond"))

            def mod_gate(l, j):
                if j == 4:
                    ve.wait_ge(*loaded(f"gate_bias{l}", 2))
                ve.wait_ge(*S("mod_pe").at("fold", l, j))
                g = gates[l][:, j // 6, j % 2 * HALF:(j % 2 + 1) * HALF]
                V.tensor_tensor(g, bank(2), g, ALU.add).then_inc(*S("mod_dve").up("gate", l, j))

            def mod_columns(l):
                Sv = S("mod_dve")
                ve.wait_ge(*S("mod_pe").at("fold", l, 11))
                for m in range(4):
                    o = par_at[f"b_mod{l}{(0, 1, 3, 4)[m]}"][0]
                    V.scalar_tensor_tensor(out=modcol[:, l, m], in0=bank(1, 64).rearrange("p (m k c) -> p m k c", m=4, k=KD)[:, m],
                                           scalar=float(m % 2), in1=par[:, o:o + KD].unsqueeze(2).to_broadcast([P, KD, 2]),
                                           op0=ALU.add, op1=ALU.add).then_inc(*Sv.up(*(("columns", l) if m == 3 else ("column", l, m))))

            def turned(name, dst, scale, bias):
                for pair in (1, 3):
                    ve.wait_ge(*S("turn_pe").at(name, pair))
                    for i in range(2):
                        k = 2 * pair + i
                        src = bank(4 + pair)[:, i * T:(i + 1) * T]
                        if bias is None:
                            V.tensor_scalar(dst[:, k], src, scale(k), None, ALU.mult).then_inc(*S("turn_dve").up(name, k))
                        else:
                            V.tensor_scalar(dst[:, k], src, scale(k), bias(k), ALU.mult, ALU.add
                                            ).then_inc(*S("turn_dve").up(name, k))

            def norm(u, x, rows, n, gain, dst, bufs, rope=None, last_swap=None):
                Sv, Sa, Sp = S("norm_dve"), S("norm_act"), S("norm_pe")
                ve.wait_ge(*Sa.at("sd", u))
                if u[-1] > 0:
                    ve.wait_ge(*Sv.at("out", u[:-1] + (u[-1] - 1,)))
                V.reciprocal(bufs["t1"][0:rows, 0:n], bufs["sd"][0:rows, 0:n]).then_inc(*Sv.up("rs", u))
                ve.wait_ge(*Sv.at("rs", u))
                o = rope[2] if rope else n
                if o:
                    V.scalar_tensor_tensor(out=dst[0:rows, 0:o], in0=x[0:rows, 0:o], scalar=gain, in1=bufs["t1"][0:rows, 0:o],
                                           op0=ALU.mult, op1=ALU.mult).then_inc(*Sv.up("out" if not rope else "plain", u))
                if not rope:
                    return
                if last_swap is not None:
                    ve.wait_ge(*Sp.at("swap", last_swap))
                m = n - o
                V.scalar_tensor_tensor(out=bufs["xn"][0:rows, 0:m], in0=x[0:rows, o:n], scalar=gain,
                                       in1=bufs["t1"][0:rows, o:n], op0=ALU.mult, op1=ALU.mult).then_inc(*Sv.up("xn", u))
                ve.wait_ge(*Sv.at("xn", u))
                tiles = m // T
                both = lambda ap: ap[0:rows].rearrange("p (j t) -> p j t", j=tiles)
                wide = lambda ap: ap[0:rows].unsqueeze(1).to_broadcast([rows, tiles, T])
                V.tensor_tensor(both(bufs["t1"][:, 0:m]), both(bufs["xn"][:, 0:m]), wide(rope[0]), ALU.mult
                                ).then_inc(*Sv.up("t1", u))
                ve.wait_ge(*Sp.at("swap", u))
                V.tensor_tensor(both(bufs["t2"][:, 0:m]), both(bank(7, m)), wide(rope[1]), ALU.mult
                                ).then_inc(*Sv.up("t2", u))
                ve.wait_ge(*Sv.at("t2", u))
                V.tensor_tensor(dst[0:rows, o:n], bufs["t1"][0:rows, 0:m], bufs["t2"][0:rows, 0:m], ALU.add
                                ).then_inc(*Sv.up("out", u))

            def mixer0():
                Sv = S("turn_dve")
                q2 = m0["q"].rearrange("p (u j) t -> p u (j t)", u=2)
                ve.wait_ge(*loaded("tables_first"))
                for u in range(4):
                    if u == 2:
                        ve.wait_ge(*consumed(("mix_in", 1)))
                        V.tensor_copy(m0["v"], bank(5).rearrange("p (a n) -> p a n", a=4)).then_inc(*Sv.up("values"))
                    norm(("first", u), bank((0, 1, 3, 4)[u]), P, 512, PC("q_g" if u < 2 else "k_g"),
                         q2[:, u] if u < 2 else m0["k"][:, u - 2], m0, (T2("cos"), T2("sin"), 0 if u < 2 else T),
                         ("first", u - 1) if u else None)
                ve.wait_ge(*consumed(("mix_in", 2)))
                for a in range(TT):
                    V.tensor_copy(m0["pt"][:, a], bank(6 - a)).then_inc(*Sv.up("pool_in", a))

            def attention0():
                Sv, Sp, Sa = S("att_dve"), S("att_pe"), S("att_act")
                st = m0["stat"]
                for u in range(18):
                    if u < 16:
                        ve.wait_ge(*Sp.at("score", 0, u))
                        V.tensor_reduce(st[:, 16 + u:17 + u], bank(4 + u % 2), AX_X, ALU.max).then_inc(*Sv.up("row_max", 0, u))
                        ve.wait_ge(*Sv.at("row_max", 0, u))
                        V.tensor_scalar(st[:, u:u + 1], st[:, 16 + u:17 + u], -0.125, None, ALU.mult
                                        ).then_inc(*Sv.up("max", 0, u))
                    if 1 <= u <= 16:
                        v = u - 1
                        ve.wait_ge(*Sa.at("exp", 0, v))
                        V.reciprocal(st[:, 48 + v:49 + v], st[:, 32 + v:33 + v]).then_inc(*Sv.up("inverse", 0, v))
                        ve.wait_ge(*Sv.at("inverse", 0, v))
                        V.tensor_scalar(m0["prob"][:, v % 2], m0["prob"][:, v % 2], st[:, 48 + v:49 + v], None, ALU.mult
                                        ).then_inc(*Sv.up("prob", 0, v))
                    if u >= 2:
                        v = u - 2
                        hd, a = v // 2, v % 2
                        o = 64 * (hd % 2)
                        ve.wait_ge(*Sp.at("value", 0, v))
                        V.tensor_copy(m0["mix"][o:o + 64, hd // 2, a * P:(a + 1) * P], bank((7, 3)[v % 2])[o:o + 64, 0:P]
                                      ).then_inc(*Sv.up("value", 0, v))
                    if u - 3 in (4, 5, 10, 11):
                        mod_gate(1, u - 3)
                mod_columns(1)

            def pool0():
                for g in range(4):
                    ve.wait_ge(*S("pool_pe").at("out", g))
                    V.tensor_scalar(m0["mix"][:, 4 + g], bank(6, T), PC("pool_scale", g), None, ALU.mult
                                    ).then_inc(*S("pool_dve").up("out", g))

            def post_norm(l, part, ready):
                Sv = S("post_dve")
                ve.wait_ge(*loaded("ln", 2 * (2 * l + part) + 2))
                for half in range(2):
                    cols = slice(half * HALF, (half + 1) * HALF)
                    ve.wait_ge(*ready(half))
                    for a in range(TT):
                        k = (l, part, a, half)
                        t = pn["t"][:, a, cols]
                        y = ff["acc"][:, a, cols] if part else bank(2 * a + half)
                        V.tensor_tensor(t, y, gates[l][:, part, cols], ALU.mult
                                        ).then_inc(*Sv.up(*(("t", l, part, 1) if a and half else ("weighed", *k))))
                    for a in range(TT):
                        k = (l, part, a, half)
                        t = pn["t"][:, a, cols]
                        ve.wait_ge(*(Sv.at("t", l, part, 1) if a and half else Sv.at("weighed", *k)))
                        V.scalar_tensor_tensor(out=t, in0=h[:, a, cols], scalar=ALPHA, in1=t, op0=ALU.mult, op1=ALU.add
                                               ).then_inc(*Sv.up("sum", *k))
                    for a in range(TT):
                        k = (l, part, a, half)
                        ve.wait_ge(*Sv.at("sum", *k))
                        V.bn_stats(pn["st"][:, a, 6 * half:6 * half + 6], pn["t"][:, a, cols]).then_inc(*Sv.up("stats", *k))
                for a in range(TT):
                    ve.wait_ge(*Sv.at("stats", l, part, a, 1))
                    V.bn_aggr(pn["mv"][:, a], pn["st"][:, a]).then_inc(*Sv.up("var", l, part, a))
                for a in range(TT):
                    k = (l, part, a)
                    t, mv, rs = pn["t"][:, a], pn["mv"][:, a], pn["rs"][:, a]
                    ve.wait_ge(*Sv.at("var", *k))
                    V.scalar_tensor_tensor(out=t, in0=t, scalar=mv[:, 0:1], in1=ln[:, 0], op0=ALU.subtract, op1=ALU.mult
                                           ).then_inc(*Sv.up("gained", *k))
                    ve.wait_ge(*S("post_act").at("sd", *k))
                    V.reciprocal(rs[:, 1:2], rs[:, 0:1]).then_inc(*Sv.up("rs", *k))
                    ve.wait_ge(*Sv.at("rs", *k))
                    V.scalar_tensor_tensor(out=h[:, a], in0=t, scalar=rs[:, 1:2], in1=ln[:, 1], op0=ALU.mult, op1=ALU.add
                                           ).then_inc(*Sv.up("h", *k))

            def conv1():
                Sv = S("conv_dve")
                V.memset(m1["z"][:, :, 0:1], 0.0).then_inc(*Sv.up("edge0"))
                V.memset(m1["z"][:, :, 257:258], 0.0).then_inc(*Sv.up("edge1"))
                for j in range(8):
                    ve.wait_ge(*consumed(("conv_in", 4 + j // 4)))
                    ve.wait_ge(*S("conv_act").at("c", j))
                    V.tensor_tensor(m1["z"][:, j, 1:257], bank(2 + j % 4 // 2)[:, j % 2 * T:j % 2 * T + T], m1["c"][:, j],
                                    ALU.mult).then_inc(*Sv.up("z", j))
                ve.wait_ge(*Sv.at("z", 7))
                for i in range(3):
                    for j in range(8):
                        if i == 0:
                            V.tensor_scalar(m1["conv"][:, j], m1["z"][:, j, 0:T], PC("conv_w", j), None, ALU.mult
                                            ).then_inc(*Sv.up("tap", i, j))
                        else:
                            ve.wait_ge(*Sv.at("tap", i - 1, j))
                            V.scalar_tensor_tensor(out=m1["conv"][:, j], in0=m1["z"][:, j, i:i + T], scalar=PC("conv_w", i * KD + j),
                                                   in1=m1["conv"][:, j], op0=ALU.mult, op1=ALU.add).then_inc(*Sv.up("tap", i, j))
                for j in range(8):
                    ve.wait_ge(*consumed(("conv_in", j // 4)))
                    ve.wait_ge(*Sv.at("tap", 2, j))
                    V.tensor_tensor(m1["mix"][:, j], bank(j // 2)[:, j % 2 * T:j % 2 * T + T], m1["conv"][:, j], ALU.mult
                                    ).then_inc(*Sv.up("mix", j))

            def ffn(l):
                Sa, Sp, Sv = S("ffn_act"), S("ffn_pe"), S("ffn_dve")
                wk, vals, st = ff["wk"][0:E], ff["vals"][0:E], ff["st"]
                ve.wait_ge(*Sp.at("logits", l))
                V.tensor_reduce(st[:, 0:2], bank(0, 2 * E).rearrange("p (a e) -> p a e", a=TT), AX_X, ALU.max
                                ).then_inc(*Sv.up("row_max", l))
                ve.wait_ge(*Sv.at("row_max", l))
                V.tensor_scalar(st[:, 2:4], st[:, 0:2], -1.0, None, ALU.mult).then_inc(*Sv.up("neg_max", l))
                ve.wait_ge(*Sa.at("ex", l, 1))
                V.reciprocal(st[:, 6:8], st[:, 4:6]).then_inc(*Sv.up("inverse", l))
                ve.wait_ge(*Sv.at("inverse", l))
                for a in range(TT):
                    V.tensor_scalar(ff["ex"][:, a], ff["ex"][:, a], st[:, 6 + a:7 + a], None, ALU.mult
                                    ).then_inc(*Sv.up("share", l, a))
                ve.wait_ge(*Sp.at("shares", l))
                V.tensor_copy(wk, bank(1, T)[0:E]).then_inc(*Sv.up("wk", l, 0))
                for r in range(4):
                    ve.wait_ge(*Sv.at("wk", l, r))
                    m8 = vals[:, 8 * r:8 * r + 8]
                    V.max(m8, wk).then_inc(*Sv.up("max8", l, r))
                    ve.wait_ge(*Sv.at("max8", l, r))
                    V.max_index(idx_u[0:E, 8 * r:8 * r + 8], m8, wk).then_inc(*Sv.up("index", l, r))
                    if r < 3:
                        ve.wait_ge(*Sv.at("index", l, r))
                        V.match_replace(wk, m8, wk, -1.0).then_inc(*Sv.up("wk", l, r + 1))
                ve.wait_ge(*Sv.at("index", l, 3))
                V.tensor_copy(ff["idf"][0:E], idx_u[0:E, :]).then_inc(*Sv.up("values", l))
                ve.wait_ge(*Sv.at("values", l))
                own = T2("own_expert")[0:E].rearrange("p (e s) -> p e s", e=E)
                V.tensor_tensor(ff["di"][0:E], own, ff["idf"][0:E].unsqueeze(1).to_broadcast([E, E, CAP]), ALU.mult
                                ).then_inc(*Sv.up("spread", l))
                V.tensor_tensor(ff["dg"][0:E], own, vals.unsqueeze(1).to_broadcast([E, E, CAP]), ALU.mult
                                ).then_inc(*Sv.up("spread_gates", l))
                ve.wait_ge(*Sp.at("rows", l))
                for a in range(TT):
                    V.tensor_scalar(ff["pick"][:, a], bank(0), T2("token")[:, a:a + 1], None, ALU.is_equal
                                    ).then_inc(*Sv.up("pick", l, a))
                ve.wait_ge(*Sp.at("cols", l))
                V.tensor_copy(ff["cols"], bank(1, 8)).then_inc(*Sv.up("cols", l))
                ve.wait_ge(*Sv.at("cols", l))
                for g in range(NG):
                    V.tensor_scalar(ff["put"][:, g], T2("iota"), ff["cols"][:, g:g + 1], ff["cols"][:, 4 + g:5 + g],
                                    ALU.is_equal, ALU.mult).then_inc(*Sv.up("put", l, g))
                Sx, Sax, Spx = (S(f"expert{l}_{e}") for e in ("dve", "act", "pe"))
                base = number[("expert", l, 0)]
                V.memset(ff["acc"], 0.0).then_inc(*Sx.up("acc_zero"))
                Sx.open_loop()
                with ve.Fori(0, NG) as g:
                    ve.wait_ge(*Spx.turn(g, "gather", 1))
                    for k in range(KD // 2, KD):
                        V.tensor_scalar(ff["xg"][:, k], bank(7)[:, k % 4 * P:k % 4 * P + P], modcol[:, l, 3, k, 0:1],
                                        modcol[:, l, 2, k, 0:1], ALU.mult, ALU.add).then_inc(*Sx.up("xg", k))
                    ve.wait_ge(used, g * (3 * KD) + (base + 2 * KD))
                    ve.wait_ge(*Sax.turn(g, "silu"))
                    for b in range(2):
                        V.tensor_tensor(ff["hg"][:, b * HALF:(b + 1) * HALF], bank(2 + b), ff["hg"][:, b * HALF:(b + 1) * HALF],
                                        ALU.mult).then_inc(*Sx.up("hidden", b))
                    ve.wait_ge(used, g * (3 * KD) + (base + 3 * KD))
                    V.tensor_copy(ff["ye"], ps_t[:, 4 * HALF:6 * HALF]).then_inc(*Sx.up("ye"))
                    for half in range(2):
                        ve.wait_ge(*Spx.turn(g, "y", half))
                        for a in range(TT):
                            dst = ff["acc"][:, a, half * HALF:(half + 1) * HALF]
                            V.tensor_tensor(dst, bank(2 * a + half), dst, ALU.add
                                            ).then_inc(*Sx.up(*(("acc", half) if a else ("acc_first", half))))
                Sx.close_loop(NG)

            def second(l):
                Sa, Sp, Sv = S("second_act"), S("second_pe"), S("second_dve")
                st = at2["stat"]
                ve.wait_ge(*Sa.at("root", l))
                V.reciprocal(st[:, 44:46], st[:, 42:44]).then_inc(*Sv.up("rs", l))
                ve.wait_ge(*Sv.at("rs", l))
                for a in range(TT):
                    V.tensor_scalar(xn_tok[:, a], h[:, a], st[:, 44 + a:45 + a], None, ALU.mult).then_inc(*Sv.up("normed", l, a))
                for i in range(2):
                    if i == 0:
                        ve.wait_ge(*Sv.at("normed", l, 1))
                    V.memset(s2["raw"][:, i, :, 0:1], 0.0).then_inc(*Sv.up("edge", l, i))
                turned(f"sec{l}", s2["ht"], lambda k: PC(f"norm_g{l}", k), None)
                ve.wait_ge(*Sv.at("edge", l, 1))
                for n in range(4):
                    ve.wait_ge(*Sa.at("raw", l, n))
                    if n:
                        ve.wait_ge(*Sv.at("mixed", l, n - 1))
                    tiles = 4 if n < 3 else 1
                    raw, diff = s2["raw"][:, n % 2, 0:tiles], s2["diff"][:, 0:tiles]
                    V.tensor_tensor(diff, raw[:, :, 0:T], raw[:, :, 1:T + 1], ALU.subtract).then_inc(*Sv.up("diff", l, n))
                    ve.wait_ge(*Sv.at("diff", l, n))
                    for j in range(tiles):
                        dst = s2["rkv"][:, n, j] if n < 3 else s2["wal"]
                        ins = V.scalar_tensor_tensor(out=dst, in0=diff[:, j], scalar=PC(f"mu{l}", 4 * n + j), in1=raw[:, j, 1:T + 1],
                                                     op0=ALU.mult, op1=ALU.add)
                        ins.then_inc(*Sv.up(*(("mixed", l, n) if j == tiles - 1 else ("mixing", l, n, j))))
                if l == 0:
                    ve.wait_ge(*Sv.at("mixed", l, 2))
                    V.tensor_copy(v_first, s2["rkv"][:, 2]).then_inc(*Sv.up("v_first"))
                else:
                    ve.wait_ge(*Sv.at("mixed", l, 3))
                    V.tensor_tensor(s2["diff"], v_first, s2["rkv"][:, 2], ALU.subtract).then_inc(*Sv.up("towards"))
                    ve.wait_ge(*Sv.at("towards"))
                    ve.wait_ge(*Sa.at("nu", 3))
                    V.tensor_tensor(s2["diff"], s2["diff"], s2["nu"], ALU.mult).then_inc(*Sv.up("by_nu"))
                    ve.wait_ge(*Sv.at("by_nu"))
                    V.tensor_tensor(s2["rkv"][:, 2], s2["rkv"][:, 2], s2["diff"], ALU.add).then_inc(*Sv.up("blend", 1))
                    ve.wait_ge(*Sv.at("blend", 1))
                for p in range(2):
                    recurrence(l, p)
                attention_parts(l)

            def recurrence(l, p):
                Sa, Sp, Sv, So = S("rwkv_act"), S("rwkv_pe"), S("rwkv_dve"), S("rwkv_pool")
                K = (l, p)
                r, k, v = (s2["rkv"][:, i, 2 * p:2 * p + 2].rearrange("p j t -> p (j t)") for i in range(3))
                half = lambda ap, jj: ap[:, jj * T:jj * T + T]

                def mul(dst, a, b, *key):
                    V.tensor_tensor(dst, a, b, ALU.mult).then_inc(*Sv.up(*key))

                if p == 0:
                    ve.wait_ge(*S("second_dve").at("mixed", l, 3))
                for jj in range(2):
                    if p == 0:
                        ve.wait_ge(*S("second_act").at("nu", 3) if l else S("second_act").at("raw", l, 3))
                    V.tensor_scalar(half(rw["kk"], jj), half(k, jj), PC(f"k_k{l}", 2 * p + jj), None, ALU.mult
                                    ).then_inc(*Sv.up("kk0", *K, jj))
                ve.wait_ge(*Sa.at("a", *K, 1))
                V.tensor_scalar(rw["lw"], rw["lw"], -DECAY, None, ALU.mult).then_inc(*Sv.up("lw", *K))
                for jj in range(2):
                    V.tensor_scalar(half(rw["kmod"], jj), half(rw["a"], jj), 1.0, PC(f"k_a{l}", 2 * p + jj), ALU.subtract, ALU.mult
                                    ).then_inc(*Sv.up("kmod0", *K, jj))
                ve.wait_ge(*Sv.at("lw", *K))
                V.tensor_tensor_scan(rw["L"], T2("carry", second_at), rw["lw"], 0.0, ALU.mult, ALU.add).then_inc(*Sv.up("L", *K))
                ve.wait_ge(*Sv.at("kmod0", *K, 1))
                V.scalar_tensor_tensor(out=rw["kmod"], in0=rw["kmod"], scalar=1.0, in1=k, op0=ALU.add, op1=ALU.mult
                                       ).then_inc(*Sv.up("kmod", *K))
                ve.wait_ge(*Sv.at("L", *K))
                chunks = rw["L"].rearrange("p (c t) -> p c t", c=8)
                V.tensor_tensor(rw["eLm"], rw["L"], rw["lw"], ALU.subtract).then_inc(*Sv.up("before", *K))
                V.tensor_tensor(rw["eH"].rearrange("p (c t) -> p c t", c=8), chunks[:, :, CH - 1:CH].to_broadcast([P, 8, CH]), chunks,
                                ALU.subtract).then_inc(*Sv.up("exponents", *K))
                ve.wait_ge(*Sa.at("kk_root", *K))
                V.tensor_scalar(rw["tmp"], rw["tmp"], 1e-12, None, ALU.max).then_inc(*Sv.up("kk_floor", *K))
                ve.wait_ge(*Sv.at("kk_floor", *K))
                V.reciprocal(rw["tmp"], rw["tmp"]).then_inc(*Sv.up("kk_rs", *K))
                ve.wait_ge(*Sv.at("kk_rs", *K))
                mul(rw["kk"], rw["kk"], rw["tmp"], "kk", *K)
                ve.wait_ge(*Sv.at("kk", *K))
                mul(rw["a"], rw["kk"], rw["a"], "b", *K)
                for jj in range(2):
                    V.scalar_tensor_tensor(out=half(rw["tmp"], jj), in0=half(r, jj), scalar=PC(f"r_k{l}", 2 * p + jj),
                                           in1=half(rw["kmod"], jj), op0=ALU.mult, op1=ALU.mult).then_inc(*Sv.up("rk", *K, jj))
                by_tile = lambda ap: ap.rearrange("p (j a t) -> p j a t", j=2, a=2)
                ve.wait_ge(*Sa.at("eLm", *K))
                mul(rw["kr"][:, :, :, 0], by_tile(rw["kk"]), by_tile(rw["eLm"]), "kq", *K)
                ve.wait_ge(*Sa.at("eN", *K))
                ve.wait_ge(*Sv.at("b", *K))
                mul(rw["bt"].rearrange("p j t -> p (j t)"), rw["a"], rw["eN"], "bt", *K)
                mul(rw["kt"].rearrange("p j t -> p (j t)"), rw["kmod"], rw["eN"], "kt0", *K)
                ve.wait_ge(*Sa.at("eL", *K))
                mul(rw["kr"][:, :, :, 1], by_tile(r), by_tile(rw["eL"]), "kt", *K)
                ve.wait_ge(*Sp.at("rk_sum", *K))
                mul(rw["bonus"], bank(3), v, "bonus", *K)
                ve.wait_ge(*So.at("hats", *K, 1))
                ve.wait_ge(*Sv.at("kt", *K))
                mask = T2("upper", second_at).unsqueeze(1).to_broadcast([P, 4, 2 * P])
                for n, g, b in (("gram_b", "gb", 0), ("gram_k", "gk", 4)):
                    ve.wait_ge(*Sp.at(n, *K))
                    for hh in range(2):
                        src = ps_t[:, (b + 2 * hh) * HALF:(b + 2 * hh + 2) * HALF].rearrange("p (q n) -> p q n", q=4)
                        V.tensor_tensor(rw[g][:, 4 * hh:4 * hh + 4], src, mask, ALU.mult).then_inc(*Sv.up(g, *K, hh))
                ident = T1("ident").unsqueeze(1).to_broadcast([P, 4, P])
                neg = T2("neg_pair", second_at).unsqueeze(1).to_broadcast([P, 4, P])
                neg_t = T2("neg_pair_t", second_at).unsqueeze(1).to_broadcast([P, 4, P])
                inv, inv_t = rw["inv"], rw["inv_t"]
                ve.wait_ge(*Sp.at("gram_a", *K))
                hs = lambda hh: slice(4 * hh, 4 * hh + 4)
                for hh in range(2):
                    V.tensor_tensor(inv[:, hs(hh)], bank(hh).rearrange("p (q n) -> p q n", q=4), neg, ALU.mult
                                    ).then_inc(*Sv.up("inv0", *K, hh))
                for hh in range(2):
                    V.tensor_tensor(inv_t[:, hs(hh)], rw["gb"][:, hs(hh), 0:P], neg_t, ALU.mult).then_inc(*Sv.up("inv_t0", *K, hh))
                for hh in range(2):
                    ve.wait_ge(*Sv.at("inv0", *K, hh))
                    V.tensor_tensor(inv[:, hs(hh)], inv[:, hs(hh)], ident, ALU.add).then_inc(*Sv.up("inv", *K, 0, hh))
                for hh in range(2):
                    ve.wait_ge(*Sv.at("inv_t0", *K, hh))
                    V.tensor_tensor(inv_t[:, hs(hh)], inv_t[:, hs(hh)], ident, ALU.add).then_inc(*Sv.up("inv_t", *K, 0, hh))
                for n in range(1, LEVELS):
                    for hh in range(2):
                        for x, m, b in (("inv", inv, 4), ("inv_t", inv_t, 6)):
                            if x == "inv" and n == LEVELS - 1:
                                continue
                            ve.wait_ge(*Sp.at(x, *K, n, hh))
                            if x == "inv":
                                ve.wait_ge(*Sp.at("step", *K, n, hh))
                            ve.wait_ge(*Sp.at("inv_t", *K, n, hh))
                            ve.wait_ge(*Sv.at(x, *K, n - 1, hh))
                            V.tensor_tensor(m[:, hs(hh)], m[:, hs(hh)], bank(b + hh).rearrange("p (q n) -> p q n", q=4),
                                            ALU.subtract).then_inc(*Sv.up(x, *K, n, hh))
                gh = rw["prod"]
                for hh in range(2):
                    ve.wait_ge(*Sp.at("gh", *K, hh))
                    V.tensor_scalar(gh[:, hs(hh)], bank(2 + hh).rearrange("p (q n) -> p q n", q=4), -1.0, None, ALU.mult
                                    ).then_inc(*Sv.up("gh", *K, hh))
                ve.wait_ge(*Sp.at("y0", *K))
                V.tensor_tensor(rw["z"].rearrange("p j (a t) -> p j a t", a=2), bank(5).rearrange("p (j a t) -> p j a t", j=2, a=2),
                                rw["kr"][:, :, :, 1], ALU.add).then_inc(*Sv.up("z", *K))
                ve.wait_ge(*Sa.at("carried", *K, 1))
                stt, carried = rw["state"], rw["carried"]
                V.tensor_copy(stt[:, 1], carried[:, 0]).then_inc(*Sv.up("state", *K, 1))
                for c in (1, 2):
                    ve.wait_ge(*Sv.at("state", *K, c))
                    for jj in range(2):
                        x = jj * T + c * CH + CH - 1
                        V.scalar_tensor_tensor(out=stt[:, c + 1, jj], in0=stt[:, c, jj], scalar=rw["eL"][:, x:x + 1],
                                               in1=carried[:, c, jj], op0=ALU.mult, op1=ALU.add).then_inc(*Sv.up("decayed", *K, c, jj))
                    ve.wait_ge(*Sv.at("decayed", *K, c, 1))
                    ve.wait_ge(*Sp.at("move", *K, c))
                    for hh in range(2):
                        o = 64 * hh
                        V.tensor_tensor(stt[o:o + 64, c + 1], stt[o:o + 64, c + 1], bank(6 + hh, P)[o:o + 64].rearrange("p (j n) -> p j n", j=2),
                                        ALU.add).then_inc(*Sv.up(*(("state", *K, c + 1) if hh else ("state0", *K, c + 1))))
                ve.wait_ge(*Sp.at("read", *K))
                ve.wait_ge(*Sa.at("y0", *K))
                y = rw["y"]
                for hh in range(2):
                    o = 64 * hh
                    src = bank(2 + hh)[o:o + 64].rearrange("p (j t) -> p j t", j=2)[:, :, CH:T]
                    V.tensor_tensor(y[o:o + 64, :, CH:T], src, y[o:o + 64, :, CH:T], ALU.add
                                    ).then_inc(*Sv.up(*(("y", *K) if hh else ("y_low", *K))))
                yf = y.rearrange("p j t -> p (j t)")
                ve.wait_ge(*Sv.at("y", *K))
                ve.wait_ge(*Sp.at("gn_mean", *K))
                V.scalar_tensor_tensor(out=yf, in0=bank(4), scalar=-1.0 / 64, in1=yf, op0=ALU.mult, op1=ALU.add
                                       ).then_inc(*Sv.up("centred", *K))
                ve.wait_ge(*Sa.at("gn_root", *K))
                V.reciprocal(rw["tmp2"], rw["tmp2"]).then_inc(*Sv.up("gn_rs", *K))
                ve.wait_ge(*Sv.at("gn_rs", *K))
                mul(yf, yf, rw["tmp2"], "scaled", *K)
                ve.wait_ge(*Sv.at("scaled", *K))
                for jj in range(2):
                    V.tensor_scalar(half(yf, jj), half(yf, jj), PC(f"lnx_g{l}", 2 * p + jj), PC(f"lnx_b{l}", 2 * p + jj),
                                    ALU.mult, ALU.add).then_inc(*Sv.up("affine", *K, jj))
                ve.wait_ge(*Sv.at("affine", *K, 1))
                V.tensor_tensor(yf, yf, rw["bonus"], ALU.add).then_inc(*Sv.up("with_bonus", *K))
                ve.wait_ge(*Sv.at("with_bonus", *K))
                oc = s2["oc"][:, 2 * p:2 * p + 2].rearrange("p j t -> p (j t)")
                mul(oc, oc, yf, "o", *K)
                ve.wait_ge(*Sv.at("o", *K))

            def attention_parts(l):
                Sa, Sp, Sv = S("second_act"), S("second_pe"), S("second_dve")
                Nd = S("norm_dve")

                def norm2(i):
                    u = ("sec", l, i)
                    r0, r1, n, _, b, _ = unit(l, i)
                    ve.wait_ge(*S("norm_act").at("sd", u))
                    if before(u):
                        ve.wait_ge(*Nd.at("out", before(u)))
                    m = T if i == 0 else n
                    rs = at2["t1"][r0:r1, 0:m]
                    V.reciprocal(rs, at2["sd"][r0:r1, 0:m]).then_inc(*Nd.up("rs", u))
                    ve.wait_ge(*Nd.at("rs", u))
                    x = unit_source(l, i)

                    def scaled(dst, src, gain, by, last):
                        V.scalar_tensor_tensor(out=dst, in0=src, scalar=gain, in1=by, op0=ALU.mult, op1=ALU.mult
                                               ).then_inc(*Nd.up(last, u))

                    if i == 0:
                        for j in range(2):
                            scaled(at2["cq"][:, j], x[:, j * T:j * T + T], PC(f"qa_g{l}", j), rs, "out" if j else "plain")
                    elif i == 1:
                        scaled(at2["ckv"], x, PC(f"kva_g{l}"), rs, "out")
                    elif i < 7:
                        gain = par[r0:r1, par_at[(f"mk_g{l}" if i == 2 else f"mq_g{l}")][0]:][:, 0:1]
                        xn, t1, t2 = (at2[x_][r0:r1, 0:n] for x_ in ("xn", "t1", "t2"))
                        scaled(xn, x, gain, rs, "xn")
                        ve.wait_ge(*Nd.at("xn", u))
                        tiles = n // T
                        both = lambda ap: ap.rearrange("p (j t) -> p j t", j=tiles)
                        wide = lambda name: T2(name, second_at)[r0:r1].unsqueeze(1).to_broadcast([r1 - r0, tiles, T])
                        V.tensor_tensor(both(t1), both(xn), wide("cos"), ALU.mult).then_inc(*Nd.up("t1", u))
                        ve.wait_ge(*S("norm_pe").at("swap", u))
                        V.tensor_tensor(both(t2), both(bank(7, n)[r0:r1]), wide("sin"), ALU.mult).then_inc(*Nd.up("t2", u))
                        ve.wait_ge(*Nd.at("t2", u))
                        if i == 2:
                            for hd in range(H2):
                                V.tensor_tensor(at2["k"][r0:r1, hd], t1, t2, ALU.add).then_inc(*Nd.up("out" if hd == 7 else "copy", u))
                        else:
                            j = 2 * (i - 3)
                            V.tensor_tensor(at2["q"][r0:r1, j:j + 2], both(t1), both(t2), ALU.add).then_inc(*Nd.up("out", u))
                    elif i < 11:
                        j = 2 * (i - 7)
                        scaled(at2["k"][0:64, j:j + 2].rearrange("p j t -> p (j t)"), x, PC(f"mk_g{l}", 0, 64), rs, "out")
                    else:
                        j, t = (i - 11) % 2 * 2, ("q", "k")[(i - 11) // 2]
                        scaled(at2[t][:, j:j + 2].rearrange("p j t -> p (j t)"), x, PC(f"f{t}_g{l}"), rs, "out")

                for i in range(11):
                    norm2(i)
                for a in range(TT):
                    V.tensor_copy(at2["v"][:, a], bank((6, 0)[a])).then_inc(*Sv.up("values", l, 0, a))
                attention2(l, 0, 96.0 ** -0.5)
                for i in range(11, 15):
                    norm2(i)
                ve.wait_ge(*consumed(("in", l, "fv")))
                for a in range(TT):
                    V.tensor_copy(at2["v"][:, a], bank(5 + a)).then_inc(*Sv.up("values", l, 1, a))
                V.memset(at2["cum"], 0.0).then_inc(*Sv.up("zero", l, 0))
                V.memset(at2["ncum"], 0.0).then_inc(*Sv.up("zero", l, 1))
                f = at2["ff"][0:8]
                ve.wait_ge(*Sa.at("log", l))
                V.tensor_scalar(f[:, 1], bank(7, T)[0:8], PC(f"fb{l}", 0, 8), 0.0, ALU.add, ALU.min).then_inc(*Sv.up("low", l))
                ve.wait_ge(*Sv.at("low", l))
                V.tensor_tensor(f[:, 2], f[:, 1], f[:, 0], ALU.subtract).then_inc(*Sv.up("log_f", l))
                ve.wait_ge(*Sv.at("log_f", l))
                V.tensor_tensor_scan(f[:, 3], T1("ones")[0:8, 0:1].to_broadcast([8, T]), f[:, 2], 0.0, ALU.mult, ALU.add
                                     ).then_inc(*Sv.up("scan", l))
                ve.wait_ge(*Sv.at("scan", l))
                ve.wait_ge(*Sv.at("zero", l, 1))
                V.tensor_scalar(at2["cum"][0:8], f[:, 3], 8.0, None, ALU.mult).then_inc(*Sv.up("cum", l))
                V.tensor_scalar(at2["ncum"][0:8], f[:, 3], -8.0, None, ALU.mult).then_inc(*Sv.up("ncum", l))
                attention2(l, 1, 0.125)
                Sg = S("gate_act")
                for b in range(3):
                    ve.wait_ge(*consumed(("proj", l, b)))
                    for i in range(4):
                        ve.wait_ge(*(Sg.at(("in", l, "merge", 0, i // 2), i % 2) if b == 0 else Sg.at("merge", l, b, i)))
                        m2 = merged[:, 2 * i:2 * i + 2].rearrange("p j t -> p (j t)")
                        dst = m2 if b == 0 else at2["mt"]
                        if b and 4 * b + i >= 5:
                            x = 4 * b + i - 1
                            ve.wait_ge(*Sv.at("merged", l, x // 4, x % 4))
                        V.tensor_tensor(dst, bank(4 * (b % 2) + i), merge_gate[b][:, 2 * i:2 * i + 2].rearrange("p j t -> p (j t)"),
                                        ALU.mult).then_inc(*Sv.up("weighed", l, b, i))
                        ve.wait_ge(*Sv.at("weighed", l, b, i))
                        if b:
                            V.tensor_tensor(m2, m2, at2["mt"], ALU.add).then_inc(*Sv.up("merged", l, b, i))
                for a in range(TT):
                    ve.wait_ge(*consumed(("out", l, 1)))
                    V.tensor_tensor(h[:, a], ps_t[:, 2 * a * HALF:(2 * a + 2) * HALF], h[:, a], ALU.add
                                    ).then_inc(*Sv.up("residual", l, a))

            def attention2(l, br, scale):
                Sa, Sp, Sv = S("att_act"), S("att_pe"), S("att_dve")
                st, o2 = at2["stat"], at2["oa" if br == 0 else "ob"]
                K = (1, l, br)
                for u in range(10):
                    if u < 8:
                        c = 4 * (u % 2)
                        sc_ = at2["score"][:, u % 2]
                        ve.wait_ge(*Sp.at("score", *K, u))
                        if u >= 2:
                            ve.wait_ge(*Sa.at("exp", *K, u - 2, 1))
                        V.scalar_tensor_tensor(out=sc_, in0=bank(u % 2, 384), scalar=scale, in1=T2("causal", second_at),
                                               op0=ALU.mult, op1=ALU.add).then_inc(*Sv.up("score", *K, u))
                        ve.wait_ge(*Sv.at("score", *K, u))
                        V.tensor_reduce(st[:, 16:17], sc_[:, 0:P], AX_X, ALU.max).then_inc(*Sv.up("row_max", *K, u, 0))
                        V.tensor_reduce(st[:, 17:18], sc_[:, P:384], AX_X, ALU.max).then_inc(*Sv.up("row_max", *K, u, 1))
                        ve.wait_ge(*Sv.at("row_max", *K, u, 1))
                        V.tensor_scalar(st[:, c:c + 2], st[:, 16:18], -1.0, None, ALU.mult).then_inc(*Sv.up("max", *K, u))
                        ve.wait_ge(*Sv.at("max", *K, u))
                    if 1 <= u <= 8:
                        v = u - 1
                        c = 8 + 4 * (v % 2)
                        ve.wait_ge(*Sa.at("exp", *K, v, 1))
                        V.reciprocal(st[:, 18:20], st[:, c:c + 2]).then_inc(*Sv.up("inverse", *K, v))
                        ve.wait_ge(*Sv.at("inverse", *K, v))
                        pr = at2["prob"][:, v % 2]
                        V.tensor_scalar(pr[:, 0:P], pr[:, 0:P], st[:, 18:19], None, ALU.mult).then_inc(*Sv.up("prob", *K, v, 0))
                        V.tensor_scalar(pr[:, P:384], pr[:, P:384], st[:, 19:20], None, ALU.mult).then_inc(*Sv.up("prob", *K, v, 1))
                        ve.wait_ge(*Sv.at("prob", *K, v, 1))
                    if u >= 2:
                        v = u - 2
                        o = 64 * (v % 2)
                        ve.wait_ge(*Sp.at("value", *K, v))
                        if v == 0:
                            ve.wait_ge(*S("gate_act").at(("in", l, "ff_gate_b" if br else "gate_a"), 1))
                        V.tensor_tensor(o2[o:o + 64, v // 2], bank(3 + v % 2, T)[o:o + 64], o2[o:o + 64, v // 2], ALU.mult
                                        ).then_inc(*Sv.up("value", *K, v))

            condition()
            for j in (4, 5, 10, 11):
                mod_gate(0, j)
            mod_columns(0)
            turned("ctx", m0["uc"], lambda k: modcol[:, 0, 1, k, 1:2], lambda k: modcol[:, 0, 0, k, 1:2])
            turned("mix0", m0["ut"], lambda k: modcol[:, 0, 1, k, 0:1], lambda k: modcol[:, 0, 0, k, 0:1])
            mixer0()
            attention0()
            pool0()
            post_norm(0, 0, lambda half: consumed(("mix_out", 0, half)))
            turned("ffn0", ff["ut"], lambda k: modcol[:, 0, 3, k, 0:1], lambda k: modcol[:, 0, 2, k, 0:1])
            ffn(0)
            post_norm(0, 1, lambda half: S("expert0_dve").turn(NG - 1, "acc", half))
            turned("mix1", m1["ut"], lambda k: modcol[:, 1, 1, k, 0:1], lambda k: modcol[:, 1, 0, k, 0:1])
            conv1()
            post_norm(1, 0, lambda half: consumed(("mix_out", 1, half)))
            turned("ffn1", ff["ut"], lambda k: modcol[:, 1, 3, k, 0:1], lambda k: modcol[:, 1, 2, k, 0:1])
            ffn(1)
            post_norm(1, 1, lambda half: S("expert1_dve").turn(NG - 1, "acc", half))
            second(0)
            second(1)

        @block.gpsimd
        def _(po):
            G = nc.gpsimd

            def gate_bias(l):
                for i, m in enumerate((2, 5)):
                    po.dma_start(gates[l][:, i], w["b_mod"][l:l + 1, m * D:(m + 1) * D].to_broadcast([P, D])
                                 ).then_inc(loaded(f"gate_bias{l}")[0], 16)

            def ln_params(l, part, last):
                if last is not None:
                    po.wait_ge(*last)
                for i, n in enumerate(("ln_mix_g", "ln_mix_b") if part == 0 else ("ln_ffn_g", "ln_ffn_b")):
                    po.dma_start(ln[:, i], w[n][l:l + 1, :].to_broadcast([P, D])).then_inc(loaded("ln")[0], 16)

            def router(l):
                if l:
                    po.wait_ge(*S("ffn_pe").at("logits", 0))
                po.dma_start(small_t[:, 512:640].rearrange("p (k e) -> p k e", k=KD),
                             w["w_router"][l].rearrange("(k p) e -> p k e", p=P)).then_inc(loaded("router")[0], 16)

            def ffn(l):
                Sx = S(f"expert{l}_pool")
                base = number[("expert", l, 0)]
                po.wait_ge(*S("ffn_dve").at("pick", l, 1))
                po.wait_ge(*S("ffn_dve").at("put", l, 3))
                Sx.open_loop()
                with po.Fori(0, NG) as g:
                    po.wait_ge(used, g * (3 * KD) + (base - KD))
                    G.tensor_copy(ff["pick_g"], ff["pick"][:, :, bass.ds(g * P, P)]).then_inc(*Sx.up("pick"))
                    po.wait_ge(used, g * (3 * KD) + (base + 1))
                    G.tensor_copy(ff["put_g"], ff["put"][:, bass.ds(g, 1)].rearrange("p a n -> p (a n)")).then_inc(*Sx.up("put"))
                Sx.close_loop(NG)

            def second(l):
                Sv, So = S("second_dve"), S("second_pool")
                if l == 0:
                    po.wait_ge(*S("ffn_dve").at("put", 1, 3))
                    po.dma_start(tab2[:, 0:n_second], w["tables_second"]).then_inc(loaded("tables_second")[0], 16)
                    po.wait_ge(*S("ffn_pe").at("logits", 1))
                else:
                    po.wait_ge(*S("rwkv_pe").at("lora", 0, 1))
                for dst, src in ((small_t[:, 0:512], w["rwkv_lora"][l]),
                                 (small_t[:, 512:640].rearrange("p (k n) -> p k n", k=4),
                                  w["rwkv_v_down_2"][0].rearrange("(k p) n -> p k n", p=P)),
                                 (small_t[0:32, 640:1152], w["rwkv_v_up_2"][0])):
                    po.dma_start(dst, src).then_inc(loaded("small2")[0], 16)
                for p in range(2):
                    K = (l, p)
                    Ra, Rp, Rv, Ro = S("rwkv_act"), S("rwkv_pe"), S("rwkv_dve"), S("rwkv_pool")
                    flat = lambda ap: ap.rearrange("p j t -> p (j t)")
                    po.wait_ge(*Ra.at("eH", *K))
                    po.wait_ge(*Rv.at("b", *K))
                    G.tensor_tensor(flat(rw["bh"]), rw["a"], rw["eH"], ALU.mult).then_inc(*Ro.up("hats", *K, 0))
                    G.tensor_tensor(flat(rw["kh"]), rw["kmod"], rw["eH"], ALU.mult).then_inc(*Ro.up("hats", *K, 1))
                    for n in range(1, LEVELS):
                        if n == 1:
                            po.wait_ge(*Rv.at("gb", *K, 1))
                            po.wait_ge(*Rp.at("gram_a", *K))
                            po.wait_ge(*Rp.at("gram_k", *K))
                        if n >= 3:
                            po.wait_ge(*Rp.at("step", *K, n - 2, 1))
                        G.tensor_tensor(rw[f"lev{n % 2}"], rw["gb"][:, :, 0:P],
                                        T2(f"level{n}", second_at).unsqueeze(1).to_broadcast([P, 8, P]), ALU.mult
                                        ).then_inc(*Ro.up("level", *K, n))

            gate_bias(0)
            po.wait_ge(*consumed(("mod", 0, LATE)))
            gate_bias(1)
            ln_params(0, 0, None)
            router(0)
            ffn(0)
            ln_params(0, 1, S("post_dve").at("h", 0, 0, 1))
            ln_params(1, 0, S("post_dve").at("h", 0, 1, 1))
            router(1)
            ffn(1)
            ln_params(1, 1, S("post_dve").at("h", 1, 0, 1))
            second(0)
            second(1)


def host_arrays(inp):
    a = {n: np.ascontiguousarray(inp[n]) for n in INPUTS if n in inp}
    a["tables"], a["tables_first"], a["tables_second"] = common_tables()[0], first_tables()[0], second_tables()[0]
    a["params"] = param_columns(inp)[0]
    a["rwkv_lora"] = np.concatenate([inp["rwkv_w_up_2"], inp["rwkv_a_up_2"]], 1)
    return a


def declare(nc, arrays):
    w = {n: nc.dram_tensor("in_" + n, arrays[n].shape, F32, kind="ExternalInput").ap() for n in INPUTS}
    return w, nc.dram_tensor("out_0", (1, T, D), F32, kind="ExternalOutput").ap()


def kernel(**inputs):
    import concourse.bacc as bacc
    from concourse.bass_utils import run_bass_kernel_spmd

    arrays = host_arrays({n: np.asarray(a) for n, a in inputs.items()})
    marks = {}
    for _ in range(2):
        nc = bacc.Bacc("TRN2", target_bir_lowering=False, num_devices=1)
        w, out = declare(nc, arrays)
        two_block_program(nc, w, out, marks)
    r = run_bass_kernel_spmd(nc, [{"in_" + n: a for n, a in arrays.items()}], core_ids=[0])
    return r.results[0]["out_0"]
```
